# Optimizing a Trainium2 kernel written in Bass

```python
import jax
import jax.numpy as jnp
from jax import lax
import numpy as np

D_MODEL = 1024
BATCH = 1
SEQ = 256
DEPTH = 2

CHUNK = 64
Q_BLOCK = 128
N_BRANCH = 4
BRANCH_W = D_MODEL // N_BRANCH
HEAD_DIM = 64
N_HEADS = BRANCH_W // HEAD_DIM
POOL_WINDOWS = (2, 4, 8, 16)
POOL_GROUP = BRANCH_W // len(POOL_WINDOWS)
RET_DECAY_BASE = 5.0
ROPE_BASE = 10000.0
FOX_BIAS_INIT = 2.0
D_FF = 7 * D_MODEL // 2
N_EXPERTS = 8
TOP_K = 2
N_DENSE = (DEPTH + 1) // 2
N_MOE = DEPTH // 2
RMS_EPS = 1e-6
LN_EPS = 1e-5
IN_SPLITS = (BRANCH_W, BRANCH_W, BRANCH_W, BRANCH_W,
             BRANCH_W, BRANCH_W, BRANCH_W, N_HEADS,
             BRANCH_W,
             BRANCH_W, BRANCH_W, BRANCH_W, BRANCH_W,
             N_BRANCH * D_MODEL)
IN_COLS = 12 * BRANCH_W + N_HEADS + N_BRANCH * D_MODEL

kernel_name = "hybrid_gated_mixers_moe_encoder"

def rmsnorm(x, gain):
    xf = x.astype(jnp.float32)
    y = xf * lax.rsqrt(jnp.mean(xf * xf, axis=-1, keepdims=True) + RMS_EPS)
    return (y * gain.astype(jnp.float32)).astype(x.dtype)

def split_heads(t):
    b, s, _ = t.shape
    return t.reshape(b, s, -1, HEAD_DIM).transpose(0, 2, 1, 3)

def merge_heads(t):
    b, h, s, d = t.shape
    return t.transpose(0, 2, 1, 3).reshape(b, s, h * d)

def split_columns(proj):
    parts, start = [], 0
    for width in IN_SPLITS:
        parts.append(proj[..., start:start + width])
        start += width
    return parts

def hgrn_lower_bounds(lb_logits):
    p = jax.nn.softmax(lb_logits.astype(jnp.float32), axis=0)
    return jnp.cumsum(p, axis=0) - p[0]

def hgrn2_mixer(q, f_logit, i, g, lb, norm_g):
    b, s, _ = q.shape
    n = s // CHUNK
    lbf = lb.astype(jnp.float32)
    log_f = jnp.log(lbf + (1.0 - lbf) * jax.nn.sigmoid(f_logit.astype(jnp.float32)))
    k = -jnp.expm1(log_f)

    def chunked(t):
        return t.astype(jnp.float32).reshape(b, n, CHUNK, N_HEADS, HEAD_DIM).transpose(1, 0, 3, 2, 4)

    qc, kc, vc = chunked(q), chunked(k), chunked(i)
    bc = jnp.cumsum(chunked(log_f), axis=3)
    causal = jnp.tril(jnp.ones((CHUNK, CHUNK), dtype=bool))[:, :, None]

    def step(state, inp):
        qq, kk, vv, bb = inp
        rel = bb[:, :, :, None, :] - bb[:, :, None, :, :]
        decay = jnp.exp(jnp.where(causal, rel, -jnp.inf))
        scores = jnp.einsum("bhtk,bhsk,bhtsk->bhts", qq, kk, decay)
        out = (jnp.einsum("bhts,bhsv->bhtv", scores, vv)
               + jnp.einsum("bhtk,bhkv->bhtv", qq * jnp.exp(bb), state))
        b_last = bb[:, :, -1:, :]
        state = (jnp.exp(b_last[:, :, 0, :])[..., None] * state
                 + jnp.einsum("bhsk,bhsv->bhkv", kk * jnp.exp(b_last - bb), vv))
        return state, out

    s0 = jnp.zeros((b, N_HEADS, HEAD_DIM, HEAD_DIM), jnp.float32)
    _, o = lax.scan(step, s0, (qc, kc, vc, bc))
    o = o.transpose(1, 0, 3, 2, 4)
    o = o * lax.rsqrt(jnp.mean(o * o, axis=-1, keepdims=True) + RMS_EPS)
    o = o.reshape(b, s, BRANCH_W) * norm_g.astype(jnp.float32)
    return (o * jax.nn.silu(g.astype(jnp.float32))).astype(q.dtype)

def fox_mixer(q, k, v, f_logit, f_bias):
    b, s, _ = q.shape
    qh = split_heads(q) * HEAD_DIM ** -0.5
    kh = split_heads(k)
    vh = split_heads(v)
    log_f = jax.nn.log_sigmoid(f_logit.astype(jnp.float32) + f_bias.astype(jnp.float32))
    cum = jnp.cumsum(log_f, axis=1).transpose(0, 2, 1)
    key_pos = jnp.arange(s)

    def block(start):
        qb = lax.dynamic_slice_in_dim(qh, start, Q_BLOCK, axis=2)
        cb = lax.dynamic_slice_in_dim(cum, start, Q_BLOCK, axis=2)
        logits = (jnp.einsum("bhtd,bhsd->bhts", qb, kh).astype(jnp.float32)
                  + (cb[..., None] - cum[:, :, None, :]))
        q_pos = start + jnp.arange(Q_BLOCK)
        logits = jnp.where(key_pos[None, :] <= q_pos[:, None], logits, -jnp.inf)
        p = jax.nn.softmax(logits, axis=-1)
        return jnp.einsum("bhts,bhsd->bhtd", p.astype(vh.dtype), vh)

    o = lax.map(block, jnp.arange(0, s, Q_BLOCK))
    o = o.transpose(1, 2, 0, 3, 4).reshape(b, N_HEADS, s, HEAD_DIM)
    return merge_heads(o).astype(q.dtype)

def pool_mixer(u, w_pool, scale):
    b, s, _ = u.shape
    uf = u.astype(jnp.float32)
    cs = jnp.concatenate([jnp.zeros((b, 1, BRANCH_W), jnp.float32), jnp.cumsum(uf, axis=1)], axis=1)
    count_pos = jnp.arange(1, s + 1, dtype=jnp.float32)[None, :, None]
    diffs = []
    for gi, w in enumerate(POOL_WINDOWS):
        lo, hi = gi * POOL_GROUP, (gi + 1) * POOL_GROUP
        c = cs[..., lo:hi]
        lower = jnp.pad(c[:, : s + 1 - w], ((0, 0), (w - 1, 0), (0, 0)))
        mean = (c[:, 1:] - lower) / jnp.minimum(count_pos, float(w))
        diffs.append(mean - uf[..., lo:hi])
    d = jnp.stack(diffs, axis=2)
    y = jnp.einsum("bsgc,gcd->bsgd", d, w_pool.astype(jnp.float32)).reshape(b, s, BRANCH_W)
    return (y * scale.astype(jnp.float32)).astype(u.dtype)

def retention_mixer(q, k, v, g, gn_g, gn_b):
    b, s, _ = q.shape
    n = s // CHUNK
    half = HEAD_DIM // 2
    pos = jnp.arange(s, dtype=jnp.float32)
    inv_freq = ROPE_BASE ** (-jnp.arange(half, dtype=jnp.float32) / half)
    ang = pos[:, None] * inv_freq[None, :]
    cos, sin = jnp.cos(ang), jnp.sin(ang)

    def rope(t):
        t1, t2 = t[..., :half], t[..., half:]
        return jnp.concatenate([t1 * cos - t2 * sin, t1 * sin + t2 * cos], axis=-1)

    def chunked(t):
        return t.reshape(b, N_HEADS, n, CHUNK, HEAD_DIM)

    qc = chunked(rope(split_heads(q.astype(jnp.float32))))
    kc = chunked(rope(split_heads(k.astype(jnp.float32))) * HEAD_DIM ** -0.5)
    vc = chunked(split_heads(v.astype(jnp.float32)))
    log_gamma = jnp.log1p(-jnp.exp2(-RET_DECAY_BASE - jnp.arange(N_HEADS, dtype=jnp.float32)))
    ci = jnp.arange(CHUNK, dtype=jnp.float32)
    diff = ci[:, None] - ci[None, :]
    intra_decay = jnp.where(diff >= 0, jnp.exp(diff * log_gamma[:, None, None]), 0.0)
    scores = jnp.einsum("bhntd,bhnsd->bhnts", qc, kc) * intra_decay[None, :, None]
    intra = jnp.einsum("bhnts,bhnsv->bhntv", scores, vc)
    zeta = jnp.exp((CHUNK - 1 - ci) * log_gamma[:, None])
    xi = jnp.exp((ci + 1) * log_gamma[:, None])
    u_chunk = jnp.einsum("bhnsd,bhnsv->nbhdv", kc * zeta[None, :, None, :, None], vc)
    g_chunk = jnp.exp(CHUNK * log_gamma)[None, :, None, None]

    def step(state, upd):
        return g_chunk * state + upd, state

    s0 = jnp.zeros((b, N_HEADS, HEAD_DIM, HEAD_DIM), jnp.float32)
    _, r_prev = lax.scan(step, s0, u_chunk)
    inter = jnp.einsum("bhntd,nbhdv->bhntv", qc * xi[None, :, None, :, None], r_prev)
    o = (intra + inter).reshape(b, N_HEADS, s, HEAD_DIM)
    mu = jnp.mean(o, axis=-1, keepdims=True)
    var = jnp.mean((o - mu) ** 2, axis=-1, keepdims=True)
    o = (o - mu) * lax.rsqrt(var + LN_EPS)
    o = merge_heads(o) * gn_g.astype(jnp.float32) + gn_b.astype(jnp.float32)
    return (o * jax.nn.silu(g.astype(jnp.float32))).astype(q.dtype)

def swiglu(h, w_gate, w_up, w_down):
    return (jax.nn.silu(h @ w_gate) * (h @ w_up)) @ w_down

def moe_ffn(h, router, w_gate, w_up, w_down):
    logits = (h @ router).astype(jnp.float32)
    top_val, top_idx = lax.top_k(logits, TOP_K)
    top_w = jax.nn.softmax(top_val, axis=-1)
    gate = jnp.einsum("bske,bsk->bse", jax.nn.one_hot(top_idx, N_EXPERTS, dtype=jnp.float32), top_w)
    out = jnp.zeros(h.shape, jnp.float32)
    for e in range(N_EXPERTS):
        out = out + gate[..., e:e + 1] * swiglu(h, w_gate[e], w_up[e], w_down[e]).astype(jnp.float32)
    return out.astype(h.dtype)

def setup_inputs(seed: int = 0) -> dict:
    key = jax.random.key(seed)
    ks = jax.random.split(key, 21)

    def normal(k, shape, scale):
        return scale * jax.random.normal(k, shape, jnp.float32)

    return {
        "x": normal(ks[0], (BATCH, SEQ, D_MODEL), 1.0),
        "w_in": normal(ks[1], (DEPTH, D_MODEL, IN_COLS), D_MODEL ** -0.5),
        "w_branch": normal(ks[2], (DEPTH, N_BRANCH, BRANCH_W, D_MODEL), BRANCH_W ** -0.5),
        "w_out": normal(ks[3], (DEPTH, D_MODEL, D_MODEL), D_MODEL ** -0.5),
        "norm_mix_g": 1.0 + normal(ks[4], (DEPTH, D_MODEL), 0.02),
        "hgrn_lb_logits": normal(ks[5], (DEPTH, BRANCH_W), 0.5),
        "hgrn_norm_g": 1.0 + normal(ks[6], (DEPTH, BRANCH_W), 0.02),
        "fox_f_bias": FOX_BIAS_INIT + normal(ks[7], (DEPTH, N_HEADS), 0.5),
        "pool_w": normal(ks[8], (DEPTH, len(POOL_WINDOWS), POOL_GROUP, POOL_GROUP), POOL_GROUP ** -0.5),
        "pool_scale": 1.0 + normal(ks[9], (DEPTH, BRANCH_W), 0.02),
        "ret_gn_g": 1.0 + normal(ks[10], (DEPTH, BRANCH_W), 0.02),
        "ret_gn_b": normal(ks[11], (DEPTH, BRANCH_W), 0.02),
        "norm_ffn_g": 1.0 + normal(ks[12], (DEPTH, D_MODEL), 0.02),
        "ffn_w_gate": normal(ks[13], (N_DENSE, D_MODEL, D_FF), D_MODEL ** -0.5),
        "ffn_w_up": normal(ks[14], (N_DENSE, D_MODEL, D_FF), D_MODEL ** -0.5),
        "ffn_w_down": normal(ks[15], (N_DENSE, D_FF, D_MODEL), D_FF ** -0.5),
        "moe_router": normal(ks[16], (N_MOE, D_MODEL, N_EXPERTS), D_MODEL ** -0.5),
        "moe_w_gate": normal(ks[17], (N_MOE, N_EXPERTS, D_MODEL, D_FF), D_MODEL ** -0.5),
        "moe_w_up": normal(ks[18], (N_MOE, N_EXPERTS, D_MODEL, D_FF), D_MODEL ** -0.5),
        "moe_w_down": normal(ks[19], (N_MOE, N_EXPERTS, D_FF, D_MODEL), D_FF ** -0.5),
        "final_norm_g": 1.0 + normal(ks[20], (D_MODEL,), 0.02),
    }

def reference(x, w_in, w_branch, w_out, norm_mix_g, hgrn_lb_logits, hgrn_norm_g, fox_f_bias,
              pool_w, pool_scale, ret_gn_g, ret_gn_b, norm_ffn_g, ffn_w_gate, ffn_w_up, ffn_w_down,
              moe_router, moe_w_gate, moe_w_up, moe_w_down, final_norm_g):
    b, s, _ = x.shape
    lower_bounds = hgrn_lower_bounds(hgrn_lb_logits)
    for layer in range(DEPTH):
        h = rmsnorm(x, norm_mix_g[layer])
        (hg_q, hg_f, hg_i, hg_g, fx_q, fx_k, fx_v, fx_f, pl_u,
         rt_q, rt_k, rt_v, rt_g, gate_logits) = split_columns(h @ w_in[layer])
        branches = (
            hgrn2_mixer(hg_q, hg_f, hg_i, hg_g, lower_bounds[layer], hgrn_norm_g[layer]),
            fox_mixer(fx_q, fx_k, fx_v, fx_f, fox_f_bias[layer]),
            pool_mixer(pl_u, pool_w[layer], pool_scale[layer]),
            retention_mixer(rt_q, rt_k, rt_v, rt_g, ret_gn_g[layer], ret_gn_b[layer]),
        )
        merged = jnp.zeros((b, s, D_MODEL), x.dtype)
        for bi, o_b in enumerate(branches):
            gate_b = jax.nn.sigmoid(gate_logits[..., bi * D_MODEL:(bi + 1) * D_MODEL])
            merged = merged + gate_b * (o_b @ w_branch[layer, bi])
        x = x + merged @ w_out[layer]
        h = rmsnorm(x, norm_ffn_g[layer])
        if layer % 2 == 0:
            ffn = swiglu(h, ffn_w_gate[layer // 2], ffn_w_up[layer // 2], ffn_w_down[layer // 2])
        else:
            ffn = moe_ffn(h, moe_router[layer // 2], moe_w_gate[layer // 2],
                          moe_w_up[layer // 2], moe_w_down[layer // 2])
        x = x + ffn
    return rmsnorm(x, final_norm_g)


_drawn_inputs = setup_inputs


def setup_inputs(seed=0):
    import zlib

    import numpy as np

    out = dict(_drawn_inputs(seed))
    spreads = {}
    factors = {'hgrn_norm_g': 4.124,
     'ret_gn_g': 4.24,
     'ret_gn_b': 5.072,
     'final_norm_g': 8.716,
     'pool_scale': 5.152,
     'norm_ffn_g': 2.751}
    for name, (base, spread) in spreads.items():
        noise = np.random.default_rng([zlib.crc32(name.encode()), seed]).standard_normal(out[name].shape)
        drawn = base * np.exp(spread * noise) if base else spread * noise
        out[name] = jnp.asarray(drawn.astype(out[name].dtype))
    for name, factor in factors.items():
        out[name] = (out[name] * factor).astype(out[name].dtype)
    return out
```

```python
from contextlib import ExitStack

import numpy as np

import concourse.bass as bass
from concourse import mybir
from concourse.alu_op_type import AluOpType as ALU

F32 = mybir.dt.float32
F32R = mybir.dt.float32r
I32 = mybir.dt.int32
U32 = mybir.dt.uint32
ACT = mybir.ActivationFunctionType
AX = mybir.AxisListType

P = 128
SEQ, DM, DEPTH = 256, 1024, 2
NT = SEQ // P
KC = DM // P
BW, HD, NH, NB = 256, 64, 4, 4
CH = 64
NCH = SEQ // CH
FF, NE = 7 * DM // 2, 8
FCH = 512
NF = FF // FCH
FB = FCH // P
RMS_EPS, LN_EPS = 1e-6, 1e-5
NEG = -1e30
TINY = 2.0 ** -63

RAW, RING = 6, 3
UNIT = 2048

C_HQ, C_HI, C_FQ, C_FV, C_PU, C_RK, C_RG, C_GATE = 0, 512, 1024, 1536, 1796, 2308, 2820, 3076
MIX_CHUNKS = [(C_PU, 512, "T"), (C_RK, 512, "M"), (C_RG, 256, "N"), (C_FQ, 512, "T"),
              (C_FV, 260, "N"), (C_HQ, 512, "T"), (C_HI, 512, "N")]
Q_PU, Q_RK, Q_RG, Q_FQ, Q_FV, Q_HQ, Q_HI = range(7)
BRANCHES = [2, 3, 1, 0]
LEVELS = [128, 64, 32, 16, 8, 4, 2]

N_MIX = 2 * len(MIX_CHUNKS)
N_LAYER = N_MIX + NB * 5 + 4
N_FFN = NF * 6
FFN0 = N_LAYER
LAYER1 = N_LAYER + N_FFN
MOE0 = LAYER1 + N_LAYER


def constants():
    i = np.arange(P)
    s, t = i[:, None], i[None, :]
    parts = {}
    masks = []
    for b in LEVELS:
        h = b // 2
        masks.append(((s // b == t // b) & (s % b < h) & (t % b >= h)).astype(np.float32))
    parts["masks"] = np.concatenate(masks, 1)
    parts["ident"] = np.eye(P, dtype=np.float32)
    parts["tri"] = (s <= t).astype(np.float32)
    parts["ones"] = np.ones((P, P), np.float32)
    causal = np.where(t <= s, 0.0, NEG).astype(np.float32)
    parts["causal"] = np.concatenate([causal, np.zeros((P, P), np.float32), causal], 1)
    rot = np.zeros((P, P), np.float32)
    half = HD // 2
    for m in range(P):
        if m % HD < half:
            rot[m + half, m] = -1.0
        else:
            rot[m - half, m] = 1.0
    parts["rot"] = rot
    parts["iota"] = np.broadcast_to(i.astype(np.float32), (P, P))
    tt = np.arange(SEQ)[None, :]
    gamma = np.log1p(-np.exp2(-5.0 - np.arange(NH)))
    parts["decay"] = np.concatenate(
        [np.where(tt >= s, np.exp((tt - s) * gamma[h]), 0.0) for h in range(NH)], 1).astype(np.float32)
    inv_freq = (10000.0 ** (-np.arange(half, dtype=np.float32) / half)).astype(np.float32)
    ang = (np.arange(SEQ, dtype=np.float32)[None, :] * inv_freq[(i % half)][:, None]).astype(np.float32)
    parts["cos"] = np.cos(ang).astype(np.float32)
    parts["sin"] = np.sin(ang).astype(np.float32)
    win = np.array([[2, 8], [4, 16]])[(i >= 64).astype(int)]
    head = np.minimum(np.arange(16)[None, None, :] + 1, win[:, :, None])
    parts["inv_win"] = (1.0 / win).astype(np.float32)
    parts["win_head"] = (win[:, :, None] / head).reshape(P, 32).astype(np.float32)
    where, at = {}, 0
    for name, a in parts.items():
        where[name] = (at, a.shape[1])
        at += a.shape[1]
    return np.ascontiguousarray(np.concatenate(list(parts.values()), 1), dtype=np.float32), where


STAGE_SHAPES = {
    "bounds": (0, 1, 9),
    "norm": (0, 1, 6), "turn": (1, 4, 4),
    "pool_means": (0, 0, 13), "pool_out": (1, 1, 1),
    "rope": (1, 0, 6),
    "ret_head": (1, 0, 2), "ret_last": (1, 1, 0), "ret_norm": (0, 1, 11),
    "fox_log": (0, 3, 4), "fox_head": (1, 2, 4), "fox_probs": (1, 1, 0), "fox_mix": (1, 0, 2),
    "hgrn_log": (0, 1, 13), "hgrn_span": (0, 1, 30),
    "hgrn_a": (1, 0, 3), "hgrn_b": (1, 0, 3), "hgrn_last": (1, 1, 0), "hgrn_norm": (0, 1, 7),
    "branch_turn": (1, 1, 1),
    "split_router": (0, 0, 2), "router": (1, 0, 1), "gates": (0, 2, 16), "places": (1, 0, 6),
}


def mixer_plan():
    plan = {}
    put = lambda at, *st: plan.setdefault(at, []).append(st)
    put(2, "pool_means", 0)
    put(3, "pool_out", 0)
    put(5, "rope", 0)
    for h in range(NH):
        put(6 + h, "ret_head", h)
    put(10, "ret_last", 0)
    put(10, "ret_norm", 0)
    put(11, "fox_log", 0)
    put(12, "branch_turn", 3)
    for h in range(NH):
        put(13 + h, "fox_head", h)
    for h in range(NH):
        put(17 + h, "fox_probs", h)
        put(17 + h, "fox_mix", h)
    put(21, "branch_turn", 1)
    put(21, "hgrn_log", 0)
    put(22, "hgrn_span", 0)
    put(23, "hgrn_a", 0)
    put(24, "hgrn_b", 0)
    put(25, "hgrn_a", 1)
    put(25, "hgrn_b", 1)
    put(26, "hgrn_span", 1)
    put(27, "hgrn_a", 2)
    put(28, "hgrn_b", 2)
    put(29, "hgrn_a", 3)
    put(30, "hgrn_b", 3)
    put(31, "hgrn_last", 0)
    put(31, "hgrn_norm", 0)
    put(33, "branch_turn", 0)
    return plan


PLAN = mixer_plan()


def stage_order():
    order = [("bounds", 0, 0)]
    for layer in range(DEPTH):
        order += [("norm", layer, 0), ("turn", layer, 0)]
        for u in range(N_LAYER):
            order += [(name, layer, arg) for name, arg in PLAN.get(u, [])]
            if u == N_LAYER - 4:
                order.append(("turn", layer, 1))
        order += [("norm", layer, 1), ("turn", layer, 2)]
        if layer == 1:
            order += [("split_router", layer, 0), ("router", layer, 0), ("gates", layer, 0), ("places", layer, 0)]
    order.append(("norm", DEPTH, 0))
    return order


def build(nc, where, A, consts_ap, out_ap):
    ctx = ExitStack()
    with ctx:
        sem = lambda name: ctx.enter_context(nc.semaphore(name))
        keep = ExitStack()

        def sb(name, shape, dt=F32, stack=ctx):
            return stack.enter_context(nc.sbuf_tensor(name, shape, dt))

        raw = [sb(f"raw{i}", [P, UNIT]) for i in range(RAW)]
        w_hi = [sb(f"w_hi{i}", [P, UNIT], F32R) for i in range(RING)]
        w_lo = [sb(f"w_lo{i}", [P, UNIT], F32R) for i in range(RING)]
        table = sb("table", [P, sum(w for _, w in where.values())])
        T = {k: table[:, a:a + w] for k, (a, w) in where.items()}
        ident = T["ident"]
        x = sb("x_sb", [P, NT, DM])
        hT_hi = sb("hT_hi", [P, KC, SEQ], F32R)
        hT_lo = sb("hT_lo", [P, KC, SEQ], F32R)
        nat = sb("nat", [P, NT, DM])
        sig = sb("sig", [P, NT, DM])
        gain_row = sig[:, 0, :]
        zeros_r = sb("zeros_r", [P, P], F32R)
        stat = sb("stat", [P, 64])
        lb_in = sb("lb_in", [P, 2, DEPTH])
        lower = sb("lower", [P, DEPTH, 2])
        upper = sb("upper", [P, DEPTH, 2])
        pool_w = sb("pool_w_sb", [P, DEPTH, 2, HD])
        pool_s = sb("pool_s_sb", [P, DEPTH, 2])
        fox_b = sb("fox_b_sb", [P, DEPTH, NH])
        rows = sb("rows", [P, 3, BW])
        lower1 = sb("lower1", [P, 8])

        mx = ExitStack()
        sbm = lambda name, shape, dt=F32: sb(name, shape, dt, mx)
        hq = sbm("hq", [P, 2, SEQ])
        hf = sbm("hf", [P, 2, SEQ])
        hk = sbm("hk", [P, 2, SEQ])
        fq = sbm("fq", [P, 2, SEQ])
        fk = sbm("fk", [P, 2, SEQ])
        rq = sbm("rq", [P, 2, SEQ])
        rk = sbm("rk", [P, 2, SEQ])
        upad = sbm("upad", [P, 2, 16 + SEQ])
        hv = sbm("hv", [P, NT, BW])
        hg = sbm("hg", [P, NT, BW])
        rv = sbm("rv", [P, NT, BW])
        rg = sbm("rg", [P, NT, BW])
        fv = sbm("fv", [P, NT, BW + NH])
        big = sbm("big", [P, 3072])
        pool_sum = [big[:, 272 * 2 * i:272 * 2 * (i + 1)].rearrange("p (c n) -> p c n", c=2) for i in range(2)]
        pool_d = big[:, 1088 + 512:1088 + 1024].rearrange("p (c n) -> p c n", c=2)
        fox_p = big[:, 0:4 * 384].rearrange("p (h n) -> p h n", h=NH)
        fox_pT = big[:, 4 * 384:8 * 384].rearrange("p (h n) -> p h n", h=NH)
        span = big[:, 0:2048].rearrange("p (l n) -> p l n", l=8)
        masked = big[:, 2048:3072].rearrange("p (l n) -> p l n", l=8)
        score = sbm("score", [P, 2, 384])
        square = score[:, :, :].rearrange("p a b -> p (a b)")[:, 0:512]
        o_nat = sbm("o_nat", [P, NT, BW])
        oT_hi = [sbm(f"oT_hi{i}", [P, 2, SEQ], F32R) for i in range(2)]
        oT_lo = [sbm(f"oT_lo{i}", [P, 2, SEQ], F32R) for i in range(2)]
        mx.close()

        silu_g = sb("silu_g", [P, NT, FCH], stack=keep)
        act = sb("act", [P, NT, FCH], stack=keep)
        aT_hi = sb("aT_hi", [P, FB, SEQ], F32R, keep)
        aT_lo = sb("aT_lo", [P, FB, SEQ], F32R, keep)
        h_hi = sb("h_hi", [P, NT, DM], F32R, keep)
        h_lo = sb("h_lo", [P, NT, DM], F32R, keep)
        pick = sb("pick", [P, NT, P], F32R, keep)
        pickT = sb("pickT", [P, SEQ], F32R, keep)
        e_hi = sb("e_hi", [P, KC, P], F32R, keep)
        e_lo = sb("e_lo", [P, KC, P], F32R, keep)
        y_hi = sb("y_hi", [P, DM], F32R, keep)
        y_lo = sb("y_lo", [P, DM], F32R, keep)
        router = sb("router_sb", [P, KC, NE], stack=keep)
        router_hi = sb("router_hi", [P, KC, NE], F32R, keep)
        router_lo = sb("router_lo", [P, KC, NE], F32R, keep)
        logit = sb("logit", [P, NT, NE], stack=keep)
        top = sb("top", [P, NT, 8], stack=keep)
        top_at = sb("top_at", [P, NT, 8], U32, keep)
        top_f = sb("top_f", [P, NT, 8], stack=keep)
        hot = sb("hot", [P, 2, NT, NE], stack=keep)
        weight = sb("weight", [P, 2, NT], stack=keep)
        gate = sb("gate", [P, NT, NE], stack=keep)
        chosen = sb("chosen", [P, NT, NE], stack=keep)
        slot = sb("slot", [P, NT, 2 * NE], stack=keep)
        passes = sb("passes", [P, 1], I32, keep)
        keep.close()

        PB = [ctx.enter_context(nc.psum_tensor(f"PB{i}", [P, 512], F32)) for i in range(4)]
        MB = [ctx.enter_context(nc.psum_tensor(f"MB{i}", [P, 512], F32)) for i in range(4)]

        raw_full = [sem(f"raw_full{i}") for i in range(RAW)]
        hi_made, lo_made, unit_used = sem("hi_made"), sem("lo_made"), sem("unit_used")
        chunk_out = sem("chunk_out")
        branch_out = sem("branch_out")
        branch_done = sem("branch_done")
        out_added = sem("out_added")
        stage_psum, act_step, dve_step = sem("stage_psum"), sem("act_step"), sem("dve_step")
        x_in, table_in, params_in, rows_in, gains_in, router_in = (
            sem(n) for n in ("x_in", "table_in", "params_in", "rows_in", "gains_in", "router_in"))
        zeroed = sem("zeroed")
        silu_made, act_made, act_turned, aT_hi_made, aT_lo_made = (
            sem(n) for n in ("silu_made", "act_made", "act_turned", "aT_hi_made", "aT_lo_made"))
        ffn_added, down_done = sem("ffn_added"), sem("down_done")
        h_split = sem("h_split")
        sig_used = sem("sig_used")
        picked, gathered, gather_hi, gather_lo = (
            sem(n) for n in ("picked", "gathered", "gather_hi", "gather_lo"))
        y_hi_made, y_lo_made, scattered, moe_added = (
            sem(n) for n in ("y_hi_made", "y_lo_made", "scattered", "moe_added"))
        stored = sem("stored")

        ORDER = stage_order()
        base, pe_n, a_n, d_n = {}, 0, 0, 0
        for key in ORDER:
            base[key] = (pe_n, a_n, d_n)
            shape = STAGE_SHAPES[key[0]]
            pe_n, a_n, d_n = pe_n + shape[0], a_n + shape[1], d_n + shape[2]

        def slot_of(u):
            return u % RING

        def size_of(u):
            local = u if u < FFN0 else u - LAYER1
            return 4 * MIX_CHUNKS[local // 2][1] if 0 <= local < N_MIX else UNIT

        def col_view(buf, width):
            return buf[:, 0:4 * width].rearrange("p (k n) -> p k n", k=4)

        def row_view(buf):
            return buf[:, :].rearrange("p (k n) -> p k n", k=2)

        def broadcast(a, n):
            return a.unsqueeze(2).broadcast_to([P, a.shape[1], n])

        N_PARAMS = 9
        block = ctx.enter_context(nc.Block())

        @block.sync
        def _(sp):
            sp.dma_start(x[:, :, :], A["x"][0].rearrange("(t p) d -> p t d", p=P)).then_inc(x_in, 16)

            def load(u, turns, src, dst):
                if u >= RAW:
                    sp.wait_ge(hi_made, turns * RAW + (u - RAW + 1))
                    sp.wait_ge(lo_made, turns * RAW + (u - RAW + 1))
                sp.dma_start(dst(raw[u % RAW]), src).then_inc(raw_full[u % RAW], 16)

            def load_cols(u, turns, w, half, c0, width):
                src = w[half * 512:(half + 1) * 512, c0:c0 + width].rearrange("(k p) n -> p k n", p=P)
                load(u, turns, src, lambda b: col_view(b, width))

            def load_rows(u, turns, w):
                load(u, turns, w.rearrange("(k p) n -> p k n", p=P), row_view)

            def load_layer(layer, u0):
                u = u0
                for c0, width, _ in MIX_CHUNKS:
                    for half in range(2):
                        load_cols(u, 0, A["w_in"][layer], half, c0, width)
                        u += 1
                for b in BRANCHES:
                    for c in range(2):
                        for half in range(2):
                            load_cols(u, 0, A["w_in"][layer], half, C_GATE + b * DM + c * 512, 512)
                            u += 1
                    load_rows(u, 0, A["w_branch"][layer, b])
                    u += 1
                for c in range(2):
                    for half in range(2):
                        load_cols(u, 0, A["w_out"][layer], half, c * 512, 512)
                        u += 1

            def load_ffn(u0, turns, w_gate, w_up, w_down):
                for half in range(2):
                    load_cols(u0 + half, turns, w_gate, half, 0, FCH)
                for half in range(2):
                    load_cols(u0 + 2 + half, turns, w_up, half, 0, FCH)
                with sp.Fori(1, NF) as j:
                    o = turns + (j - 1)
                    for w, at in ((w_gate, 4), (w_up, 6)):
                        for half in range(2):
                            src = w[half * 512:(half + 1) * 512, bass.ds(j * FCH, FCH)].rearrange(
                                "(k p) n -> p k n", p=P)
                            load(u0 + at + half, o, src, lambda b: col_view(b, FCH))
                    for i in range(2):
                        load_rows(u0 + 8 + i, o, w_down[bass.ds((j - 1) * FCH + i * 256, 256), :])
                for i in range(2):
                    load_rows(u0 + 40 + i, turns, w_down[FF - FCH + i * 256:FF - FCH + (i + 1) * 256, :])

            load_layer(0, 0)
            load_ffn(FFN0, 0, A["ffn_w_gate"][0], A["ffn_w_up"][0], A["ffn_w_down"][0])
            load_layer(1, LAYER1)

            def load_experts(job0):
                with sp.Fori(0, NE) as e:
                    w = [A[n][0, bass.ds(e, 1)].rearrange("a k n -> (a k) n")
                         for n in ("moe_w_gate", "moe_w_up", "moe_w_down")]
                    load_ffn(MOE0, (e + job0) * NF, *w)

            load_experts(0)
            sp.wait_ge(dve_step, base[("places", 1, 0)][2] + STAGE_SHAPES["places"][2])
            n_pass = sp.value_load(passes[0:1, 0:1], min_val=1, max_val=2)
            with sp.If(n_pass > 1):
                load_experts(NE)
            for i in range(RING):
                u = MOE0 + i
                sp.wait_ge(hi_made, (n_pass * (NE * N_FFN)) + (u - RAW + 1))
                sp.sem_inc(raw_full[u % RAW], 16)
            key = ("norm", DEPTH, 0)
            sp.wait_ge(dve_step, base[key][2] + STAGE_SHAPES["norm"][2])
            sp.dma_start(out_ap[0].rearrange("(t p) d -> p t d", p=P), nat[:, :, :]).then_inc(stored, 16)
            sp.wait_ge(stored, 16)

        @block.gpsimd
        def _(pool):
            pool.dma_start(table[:, :], consts_ap).then_inc(table_in, 16)
            row = lambda a: a.partition_broadcast(P)
            pool.dma_start(gain_row, row(A["norm_mix_g"][0])).then_inc(gains_in, 16)
            pool.dma_start(rows[:, 0, :], row(A["hgrn_norm_g"][0])).then_inc(rows_in, 16)
            pool.dma_start(rows[:, 1, :], row(A["ret_gn_g"][0])).then_inc(rows_in, 16)
            pool.dma_start(rows[:, 2, :], row(A["ret_gn_b"][0])).then_inc(rows_in, 16)
            for layer in range(DEPTH):
                pool.dma_start(lb_in[:, :, layer], A["hgrn_lb_logits"][layer].rearrange("(c p) -> p c", p=P),
                               allow_slow_non_contiguous=True).then_inc(params_in, 16)
                pool.dma_start(pool_s[:, layer, :], A["pool_scale"][layer].rearrange("(c p) -> p c", p=P),
                               allow_slow_non_contiguous=True).then_inc(params_in, 16)
            for b in range(2):
                for layer in range(DEPTH):
                    pool.dma_start(pool_w[b * HD:(b + 1) * HD, layer],
                                   A["pool_w"][layer].rearrange("(a b) i o -> b i a o", b=2)[b],
                                   ).then_inc(params_in, 16)
            pool.dma_start(fox_b[:, :, :], A["fox_f_bias"].partition_broadcast(P)).then_inc(params_in, 16)

            def gains(src, n):
                pool.dma_start(gain_row, row(src)).then_inc(gains_in, 16)

            for layer in range(DEPTH):
                pool.wait_ge(branch_out, 16 * (layer + 1))
                gains(A["norm_ffn_g"][layer], 2 * layer + 1)
                pool.wait_ge(dve_step, base[("norm", layer, 1)][2] + STAGE_SHAPES["norm"][2])
                if layer == 0:
                    gains(A["norm_mix_g"][1], 2)
                    pool.dma_start(rows[:, 0, :], row(A["hgrn_norm_g"][1])).then_inc(rows_in, 16)
                    pool.dma_start(rows[:, 1, :], row(A["ret_gn_g"][1])).then_inc(rows_in, 16)
                    pool.dma_start(rows[:, 2, :], row(A["ret_gn_b"][1])).then_inc(rows_in, 16)
                else:
                    gains(A["final_norm_g"], 4)
                    pool.dma_start(router[:, :, :], A["moe_router"][0].rearrange("(k p) e -> p k e", p=P),
                                   ).then_inc(router_in, 16)

        @block.tensor
        def _(pe):
            def lo_ready(u, turns):
                pe.wait_ge(lo_made, turns * RAW + (u + 1))

            def product(out, lhs, rhs, first, last):
                pe.matmul(out, lhs[0], rhs[0], start=first, stop=False)
                pe.matmul(out, lhs[0], rhs[1], start=False, stop=False)
                return pe.matmul(out, lhs[1], rhs[0], start=False, stop=last)

            def begin(key):
                p, a, d = base[key]
                if a:
                    pe.wait_ge(act_step, a)
                if d:
                    pe.wait_ge(dve_step, d)

            def turn(key):
                begin(key)
                for b in range(4):
                    for k in range(2):
                        for t in range(NT):
                            last = pe.transpose(PB[b][:, k * SEQ + t * P:k * SEQ + (t + 1) * P],
                                                nat[:, t, (2 * b + k) * P:(2 * b + k + 1) * P], ident)
                last.then_inc(stage_psum, 1)

            def cols(u, q, layer, kind, width):
                pair = PB[2 * (q % 2):2 * (q % 2) + 2]
                for half in range(2):
                    lo_ready(u + half, 0)
                    hi, lo = (col_view(w[slot_of(u + half)], width) for w in (w_hi, w_lo))
                    for k in range(4):
                        kk = 4 * half + k
                        first, end = kk == 0, kk == KC - 1
                        h = (hT_hi[:, kk, :], hT_lo[:, kk, :])
                        n_t = {"T": 4, "M": 2, "N": 0}[kind]
                        for m in range(n_t):
                            w = tuple(x[:, k, m * P:(m + 1) * P] for x in (hi, lo))
                            last = product(pair[m // 2][:, (m % 2) * SEQ:(m % 2 + 1) * SEQ], w, h,
                                           first and m % 2 == 0, end and m % 2 == 1)
                        if kind == "T":
                            continue
                        for t in range(NT):
                            ht = tuple(x[:, t * P:(t + 1) * P] for x in h)
                            if kind == "N":
                                last = product(pair[t][:, 0:width], ht, (hi[:, k, :], lo[:, k, :]), first, end)
                            else:
                                last = product(pair[1][:, t * BW:(t + 1) * BW], ht,
                                               (hi[:, k, BW:2 * BW], lo[:, k, BW:2 * BW]),
                                               first and t == 0, end and t == 1)
                    last.then_inc(unit_used, 1)

            def heads(h):
                return h // 2, (h % 2) * HD

            def values(m, v, h):
                vs = [v[:, t, h * HD:(h + 1) * HD] for t in range(NT)]
                pe.matmul(MB[2][:, h * HD:(h + 1) * HD], m[:, 0:P], vs[0], start=True, stop=True)
                pe.matmul(MB[3][:, h * HD:(h + 1) * HD], m[:, P:2 * P], vs[0], start=True, stop=False)
                return pe.matmul(MB[3][:, h * HD:(h + 1) * HD], m[:, 2 * P:3 * P], vs[1], start=False, stop=True)

            def stage(name, layer, arg):
                key = (name, layer, arg)
                if not STAGE_SHAPES[name][0]:
                    return
                begin(key)
                if name == "pool_out":
                    for c in range(2):
                        for b in range(2):
                            s = slice(b * HD, (b + 1) * HD)
                            last = pe.matmul(MB[0][s, c * SEQ:(c + 1) * SEQ], pool_w[s, layer, c, :],
                                             pool_d[s, c, :], start=True, stop=True)
                elif name == "rope":
                    pe.wait_ge(chunk_out, 15 * layer + Q_RK + 1)
                    for i, t in enumerate((rq, rk)):
                        last = pe.matmul(MB[i][:, :], T["rot"], t[:, :, :].rearrange("p c n -> p (c n)"),
                                         start=True, stop=True)
                elif name == "ret_head":
                    if arg:
                        values(score[:, (arg - 1) % 2, :], rv, arg - 1)
                    c, b = heads(arg)
                    s = slice(b, b + HD)
                    bank = MB[arg % 2]
                    pe.matmul(bank[:, 0:SEQ], rk[s, c, 0:P], rq[s, c, :], start=True, stop=True)
                    last = pe.matmul(bank[:, SEQ:SEQ + P], rk[s, c, P:SEQ], rq[s, c, P:SEQ], start=True, stop=True)
                elif name in ("ret_last", "hgrn_last"):
                    last = values(score[:, (NH - 1) % 2, :], rv if name == "ret_last" else hv, NH - 1)
                elif name == "fox_head":
                    c, b = heads(arg)
                    s = slice(b, b + HD)
                    for t in range(NT):
                        n = P * (t + 1)
                        o = MB[arg][:, t * P:t * P + n]
                        pe.matmul(o, fq[s, c, t * P:(t + 1) * P], fk[s, c, 0:n], start=True, stop=False)
                        for tt in range(t + 1):
                            nl = stat[:, 16 + tt * NH + arg:17 + tt * NH + arg].broadcast_to([P, P])
                            if tt == 0:
                                rhs, oo = table[:, where["tri"][0]:where["tri"][0] + n], o
                            else:
                                rhs, oo = T["tri"], o[:, P:2 * P]
                            last = pe.matmul(oo, nl, rhs, start=False, stop=tt == t)
                elif name == "fox_probs":
                    for i in range(3):
                        last = pe.transpose(MB[arg % 2][:, i * P:(i + 1) * P], fox_p[:, arg, i * P:(i + 1) * P], ident)
                elif name == "fox_mix":
                    last = values(fox_pT[:, arg, :], fv, arg)
                elif name in ("hgrn_a", "hgrn_b"):
                    t = 0 if name == "hgrn_a" else 1
                    c, b = heads(arg)
                    s = slice(b, b + HD)
                    pe.wait_ge(chunk_out, 15 * layer + Q_HI + 1)
                    if t == 0 and arg:
                        values(score[:, (arg - 1) % 2, :], hv, arg - 1)
                    ts = slice(t * P, (t + 1) * P)
                    for i in range(8):
                        o = MB[i // 4][:, (i % 4) * P:(i % 4 + 1) * P]
                        if i < 7:
                            last = pe.matmul(o, span[s, 1 + i, ts], span[s, 1 + i, ts], start=True, stop=True)
                        else:
                            last = pe.matmul(o, hk[s, c, ts], hq[s, c, ts], start=True, stop=True)
                    if t == 1:
                        last = pe.matmul(MB[2][:, SEQ:SEQ + P], span[s, 0, 0:P], span[s, 0, P:SEQ], start=True, stop=True)
                elif name == "branch_turn":
                    for c in range(2):
                        for t in range(NT):
                            last = pe.transpose(MB[0][:, c * SEQ + t * P:c * SEQ + (t + 1) * P],
                                                o_nat[:, t, c * P:(c + 1) * P], ident)
                elif name == "router":
                    for t in range(NT):
                        for k in range(KC):
                            ts = slice(t * P, (t + 1) * P)
                            last = product(MB[0][:, t * NE:(t + 1) * NE], (hT_hi[:, k, ts], hT_lo[:, k, ts]),
                                           (router_hi[:, k, :], router_lo[:, k, :]), k == 0, k == KC - 1)
                elif name == "places":
                    m = [chosen[:, t, :] for t in range(NT)]
                    pe.matmul(MB[0][:, 0:NE], T["tri"], m[0], start=True, stop=True)
                    pe.matmul(MB[0][:, NE:2 * NE], T["ones"], m[0], start=True, stop=False)
                    pe.matmul(MB[0][:, NE:2 * NE], T["tri"], m[1], start=False, stop=True)
                    pe.matmul(MB[0][:, 2 * NE:3 * NE], T["ones"], m[0], start=True, stop=False)
                    last = pe.matmul(MB[0][:, 2 * NE:3 * NE], T["ones"], m[1], start=False, stop=True)
                last.then_inc(stage_psum, 1)

            def layer_body(layer, u0):
                turn(("turn", layer, 0))
                q = 0
                p, a, d = base[("turn", layer, 0)]
                pe.wait_ge(act_step, a + 4)
                pe.wait_ge(dve_step, d + 4)
                for u in range(N_LAYER):
                    for name, arg in PLAN.get(u, []):
                        stage(name, layer, arg)
                    if u < N_MIX:
                        if u % 2 == 0:
                            if u >= 4:
                                pe.wait_ge(chunk_out, 15 * layer + q - 1)
                            cols(u0 + u, q, layer, MIX_CHUNKS[q][2], MIX_CHUNKS[q][1])
                            q += 1
                    elif u < N_LAYER - 4:
                        i, r = divmod(u - N_MIX, 5)
                        if r < 4:
                            if r % 2 == 0:
                                pe.wait_ge(chunk_out, 15 * layer + q - 1)
                                if i:
                                    pe.wait_ge(branch_out, 16 * layer + 4 * i)
                                cols(u0 + u, q, layer, "N", 512)
                                q += 1
                        else:
                            pe.wait_ge(chunk_out, 15 * layer + q)
                            turned = ("pool_out", layer, 0) if BRANCHES[i] == 2 else ("branch_turn", layer, BRANCHES[i])
                            pe.wait_ge(act_step, base[turned][1] + 1)
                            pe.wait_ge(dve_step, base[turned][2] + 1)
                            lo_ready(u0 + u, 0)
                            hi, lo = (row_view(w[slot_of(u0 + u)]) for w in (w_hi, w_lo))
                            for t in range(NT):
                                for c in range(2):
                                    for k in range(2):
                                        ts, cs = slice(t * P, (t + 1) * P), slice(c * 512, (c + 1) * 512)
                                        last = product(PB[2 * t + c][:, :], (oT_hi[i % 2][:, k, ts], oT_lo[i % 2][:, k, ts]),
                                                       (hi[:, k, cs], lo[:, k, cs]), k == 0, k == 1)
                                    if (t, c) != (1, 1):
                                        last.then_inc(branch_done, 1)
                            last.then_inc(unit_used, 1)
                    else:
                        c, half = divmod(u - (N_LAYER - 4), 2)
                        if (c, half) == (0, 0):
                            pe.wait_ge(branch_out, 16 * (layer + 1))
                            turn(("turn", layer, 1))
                            p, a, d = base[("turn", layer, 1)]
                            pe.wait_ge(act_step, a + 4)
                            pe.wait_ge(dve_step, d + 4)
                        lo_ready(u0 + u, 0)
                        hi, lo = (col_view(w[slot_of(u0 + u)], 512) for w in (w_hi, w_lo))
                        for k in range(4):
                            kk = 4 * half + k
                            for t in range(NT):
                                ts = slice(t * P, (t + 1) * P)
                                last = product(PB[2 * c + t][:, :], (hT_hi[:, kk, ts], hT_lo[:, kk, ts]),
                                               (hi[:, k, :], lo[:, k, :]), kk == 0, kk == KC - 1)
                        last.then_inc(unit_used, 1)
                turn(("turn", layer, 2))
                p, a, d = base[("turn", layer, 2)]
                pe.wait_ge(act_step, a + 4)
                pe.wait_ge(dve_step, d + 4)

            def wide(u, turns, bank0, src, tiles):
                for half in range(2):
                    lo_ready(u + half, turns)
                    hi, lo = (col_view(w[slot_of(u + half)], FCH) for w in (w_hi, w_lo))
                    for k in range(4):
                        kk = 4 * half + k
                        for t in range(tiles):
                            ts = slice(t * P, (t + 1) * P)
                            last = product(PB[bank0 + t][:, :], (src[0][:, kk, ts], src[1][:, kk, ts]),
                                           (hi[:, k, :], lo[:, k, :]), kk == 0, kk == KC - 1)
                    last.then_inc(unit_used, 1)

            def down(u, turns, c, tiles, final):
                pe.wait_ge(aT_lo_made, c + 1)
                for i in range(2):
                    lo_ready(u + i, turns)
                    hi, lo = (row_view(w[slot_of(u + i)]) for w in (w_hi, w_lo))
                    for k in range(2):
                        for t in range(tiles):
                            ts = slice(t * P, (t + 1) * P)
                            for cc in range(2):
                                cs = slice(cc * 512, (cc + 1) * 512)
                                last = product(MB[2 * t + cc][:, :], (aT_hi[:, 2 * i + k, ts], aT_lo[:, 2 * i + k, ts]),
                                               (hi[:, k, cs], lo[:, k, cs]), False,
                                               final and i == 1 and k == 1)
                    last.then_inc(unit_used, 1)
                return last

            def turn_act(c, tiles):
                pe.wait_ge(act_made, c + 1)
                for t in range(tiles):
                    for b in range(FB):
                        last = pe.transpose(PB[2 + t][:, b * P:(b + 1) * P], act[:, t, b * P:(b + 1) * P], ident)
                last.then_inc(act_turned, 1)

            def ffn(u0, turns, c0, src, tiles):
                for t in range(tiles):
                    for cc in range(2):
                        pe.matmul(MB[2 * t + cc][:, :], zeros_r[:, :],
                                  hT_hi[:, 0:2, :].rearrange("p a b -> p (a b)"), start=True, stop=False)
                wide(u0, turns, 0, src, tiles)
                wide(u0 + 2, turns, 2, src, tiles)
                turn_act(c0, tiles)
                with pe.Fori(1, NF) as j:
                    o = turns + (j - 1)
                    c = c0 + j
                    pe.wait_ge(silu_made, c)
                    wide(u0 + 4, o, 0, src, tiles)
                    pe.wait_ge(aT_lo_made, c)
                    wide(u0 + 6, o, 2, src, tiles)
                    down(u0 + 8, o, c - 1, tiles, False)
                    turn_act(c, tiles)
                return down(u0 + 40, turns, c0 + (NF - 1), tiles, True)

            pe.wait_ge(table_in, 16)
            pe.wait_ge(params_in, 16 * N_PARAMS)
            layer_body(0, 0)
            pe.wait_ge(zeroed, 1)
            ffn(FFN0, 0, 0, (hT_hi, hT_lo), NT)
            layer_body(1, LAYER1)
            stage("router", 1, 0)
            stage("places", 1, 0)
            pe.wait_ge(dve_step, base[("places", 1, 0)][2] + STAGE_SHAPES["places"][2])
            n_pass = pe.value_load(passes[0:1, 0:1], min_val=1, max_val=2)
            with pe.Fori(0, n_pass) as ps:
                with pe.Fori(0, NE) as e:
                    job = ps * NE + e
                    pe.wait_ge(picked, job + 1)
                    pe.wait_ge(h_split, 1)
                    for t in range(NT):
                        pe.transpose(PB[3][:, t * P:(t + 1) * P], pick[:, t, :].bitcast(F32), ident)
                    for k in range(KC):
                        o = MB[2 + k // 4][:, (k % 4) * P:(k % 4 + 1) * P]
                        ks = slice(k * P, (k + 1) * P)
                        for t in range(NT):
                            pe.matmul(o, h_hi[:, t, ks], pick[:, t, :], start=t == 0, stop=False)
                            last = pe.matmul(o, h_lo[:, t, ks], pick[:, t, :], start=False, stop=t == NT - 1)
                    last.then_inc(gathered, 1)
                    pe.wait_ge(gather_hi, job + 1)
                    pe.wait_ge(gather_lo, job + 1)
                    ffn(MOE0, job * NF, NF + job * NF, (e_hi, e_lo), 1)
                    pe.wait_ge(y_hi_made, job + 1)
                    pe.wait_ge(y_lo_made, job + 1)
                    pe.wait_ge(silu_made, NF + job * NF + NF)
                    pe.wait_ge(aT_lo_made, NF + job * NF + NF)
                    for t in range(NT):
                        for c in range(2):
                            bank = (MB[2 + c], PB[1 + 2 * c])[t]
                            cs = slice(c * 512, (c + 1) * 512)
                            pe.matmul(bank[:, :], pickT[:, t * P:(t + 1) * P], y_hi[:, cs], start=True, stop=False)
                            last = pe.matmul(bank[:, :], pickT[:, t * P:(t + 1) * P], y_lo[:, cs], start=False, stop=True)
                    last.then_inc(scattered, 1)
                    pe.wait_ge(moe_added, job + 1)

        @block.scalar
        def _(act_e):
            def convert(u, turns):
                act_e.wait_ge(raw_full[u % RAW], turns * 16 + (u // RAW + 1) * 16)
                if u >= RING:
                    act_e.wait_ge(unit_used, turns * RAW + (u - RING + 1))
                n = size_of(u)
                act_e.activation(w_hi[slot_of(u)][:, 0:n], raw[u % RAW][:, 0:n], ACT.Copy).then_inc(hi_made, 1)

            def turn(key):
                p, a, d = base[key]
                act_e.wait_ge(stage_psum, p + 1)
                for b in range(4):
                    act_e.activation(hT_hi[:, 2 * b:2 * b + 2, :].rearrange("p k n -> p (k n)"), PB[b][:, :],
                                     ACT.Copy).then_inc(act_step, 1)

            def take_chunk(q, u, layer):
                pair = PB[2 * (q % 2):2 * (q % 2) + 2]
                flat = lambda t: t[:, :, :].rearrange("p c n -> p (c n)")
                act_e.wait_ge(unit_used, u + 1)
                copy = lambda o, i, f=ACT.Copy, **kw: act_e.activation(o, i, f, **kw)
                if layer and q == 0:
                    act_e.wait_ge(ffn_added, 4)
                if q == Q_PU:
                    copy(upad[:, :, 16:16 + SEQ], pair[0][:, :].rearrange("p (c n) -> p c n", c=2))
                    last = copy(flat(rq), pair[1][:, :])
                elif q == Q_RK:
                    copy(flat(rk), pair[0][:, :], scale=HD ** -0.5)
                    last = copy(flat(rv), pair[1][:, :])
                elif q == Q_RG:
                    for t in range(NT):
                        last = copy(rg[:, t, :], pair[t][:, 0:BW], ACT.Silu)
                elif q == Q_FQ:
                    copy(flat(fq), pair[0][:, :], scale=HD ** -0.5)
                    last = copy(flat(fk), pair[1][:, :])
                elif q == Q_FV:
                    for t in range(NT):
                        last = copy(fv[:, t, :], pair[t][:, 0:BW + NH])
                elif q == Q_HQ:
                    copy(flat(hq), pair[0][:, :])
                    copy(flat(hf), pair[1][:, :], ACT.Sigmoid)
                    last = copy(flat(hk), pair[1][:, :], ACT.Sigmoid, scale=-1.0)
                elif q == Q_HI:
                    for t in range(NT):
                        copy(hv[:, t, :], pair[t][:, 0:BW])
                    for t in range(NT):
                        last = copy(hg[:, t, :], pair[t][:, BW:2 * BW], ACT.Silu)
                else:
                    i, c = divmod(q - 7, 2)
                    if c == 0 and i:
                        act_e.wait_ge(branch_out, 16 * layer + 4 * i)
                    for t in range(NT):
                        last = copy(sig[:, t, c * 512:(c + 1) * 512], pair[t][:, :], ACT.Sigmoid)
                last.then_inc(chunk_out, 1)

            def stage(name, layer, arg):
                p, a, d = base[(name, layer, arg)]
                if STAGE_SHAPES[name][1] == 0:
                    return
                dve = lambda n: act_e.wait_ge(dve_step, d + n)
                psum = lambda: act_e.wait_ge(stage_psum, p + 1)
                done = lambda ins: ins.then_inc(act_step, 1)
                if name == "bounds":
                    dve(2)
                    done(act_e.activation(lower1[:, 0:4], lower1[:, 4:8], ACT.Exp))
                elif name == "norm":
                    dve(3)
                    done(act_e.activation(stat[:, 2:4], stat[:, 2:4], ACT.Sqrt))
                elif name == "pool_out":
                    psum()
                    for c in range(2):
                        last = act_e.activation(oT_hi[0][:, c, :], MB[0][:, c * SEQ:(c + 1) * SEQ], ACT.Copy,
                                                scale=pool_s[:, layer, c:c + 1])
                    done(last)
                elif name in ("ret_last", "hgrn_last"):
                    psum()
                    if name == "hgrn_last":
                        act_e.wait_ge(stage_psum, base[("branch_turn", layer, 1)][0] + 1)
                    for t in range(NT):
                        last = act_e.activation(o_nat[:, t, :], MB[2 + t][:, 0:BW], ACT.Copy)
                    done(last)
                elif name == "ret_norm":
                    dve(6)
                    done(act_e.activation(stat[:, 32:40], stat[:, 32:40], ACT.Sqrt))
                elif name == "hgrn_norm":
                    dve(3)
                    done(act_e.activation(stat[:, 32:40], stat[:, 32:40], ACT.Sqrt))
                elif name == "fox_log":
                    dve(1)
                    done(act_e.activation(stat[:, 48:56], stat[:, 40:48], ACT.Abs))
                    act_e.wait_ge(act_step, a + 1)
                    done(act_e.activation(stat[:, 48:56], stat[:, 48:56], ACT.Exp, scale=-1.0))
                    dve(2)
                    done(act_e.activation(stat[:, 48:56], stat[:, 48:56], ACT.Ln))
                elif name == "fox_head":
                    dve(3)
                    for t in range(NT):
                        cs = slice(0, P) if t == 0 else slice(P, 3 * P)
                        done(act_e.activation(fox_p[:, arg, cs], fox_p[:, arg, cs], ACT.Exp,
                                              bias=stat[:, 24 + t:25 + t], accum_out=stat[:, 26 + t:27 + t]))
                elif name == "fox_probs":
                    psum()
                    done(act_e.activation(fox_pT[:, arg, :], MB[arg % 2][:, 0:384], ACT.Copy))
                elif name == "hgrn_log":
                    dve(5)
                    done(act_e.activation(hf[:, :, :].rearrange("p c n -> p (c n)"),
                                          hf[:, :, :].rearrange("p c n -> p (c n)"), ACT.Ln))
                elif name == "hgrn_span":
                    dve(14)
                    done(act_e.activation(span[:, :, :].rearrange("p l n -> p (l n)"),
                                          span[:, :, :].rearrange("p l n -> p (l n)"), ACT.Exp))
                elif name == "branch_turn":
                    psum()
                    i = BRANCHES.index(arg)
                    if i >= 2:
                        act_e.wait_ge(unit_used, (0, LAYER1)[layer] + N_MIX + 5 * (i - 2) + 5)
                    done(act_e.activation(oT_hi[i % 2][:, :, :].rearrange("p c n -> p (c n)"), MB[0][:, :], ACT.Copy))
                elif name == "gates":
                    dve(8)
                    done(act_e.activation(stat[:, 8:10], stat[:, 8:10], ACT.Exp))
                    for t in range(NT):
                        last = act_e.activation(h_hi[:, t, :], nat[:, t, :], ACT.Copy)
                    done(last)

            def layer_points(layer, u0):
                q = 0
                for u in range(N_LAYER):
                    if 0 < u <= N_MIX and u % 2 == 0:
                        take_chunk(q, u0 + u - 1, layer)
                        q += 1
                    elif u > N_MIX and (u - N_MIX) % 5 in (2, 4) and u < N_LAYER - 4:
                        take_chunk(q, u0 + u - 1, layer)
                        q += 1
                    for name, arg in PLAN.get(u, []):
                        stage(name, layer, arg)
                    if u == N_LAYER - 4:
                        turn(("turn", layer, 1))
                    convert(u0 + u + RING, 0)

            def take_silu(u, turns, c, tiles):
                act_e.wait_ge(unit_used, turns * RAW + (u + 1))
                if not (isinstance(c, int) and c == 0):
                    act_e.wait_ge(act_made, c)
                for t in range(tiles):
                    last = act_e.activation(silu_g[:, t, :], PB[t][:, :], ACT.Silu)
                last.then_inc(silu_made, 1)

            def take_turned(c, tiles):
                act_e.wait_ge(act_turned, c + 1)
                for t in range(tiles):
                    last = act_e.activation(aT_hi[:, :, t * P:(t + 1) * P],
                                            PB[2 + t][:, :].rearrange("p (b n) -> p b n", b=FB), ACT.Copy)
                last.then_inc(aT_hi_made, 1)

            def ffn_points(u0, turns, c0, tiles):
                ahead = lambda u, o: convert(u + RING, o)
                ahead(u0, turns)
                ahead(u0 + 1, turns)
                take_silu(u0 + 1, turns, c0, tiles)
                ahead(u0 + 2, turns)
                ahead(u0 + 3, turns)
                take_turned(c0, tiles)
                with act_e.Fori(1, NF) as j:
                    o = turns + (j - 1)
                    c = c0 + j
                    ahead(u0 + 4, o)
                    ahead(u0 + 5, o)
                    take_silu(u0 + 5, o, c, tiles)
                    for i in range(6, 10):
                        ahead(u0 + i, o)
                    take_turned(c, tiles)
                ahead(u0 + 40, turns)
                ahead(u0 + 41, turns)

            stage("bounds", 0, 0)
            stage("norm", 0, 0)
            for u in range(RING):
                convert(u, 0)
            turn(("turn", 0, 0))
            layer_points(0, 0)
            stage("norm", 0, 1)
            turn(("turn", 0, 2))
            ffn_points(FFN0, 0, 0, NT)
            stage("norm", 1, 0)
            turn(("turn", 1, 0))
            layer_points(1, LAYER1)
            stage("norm", 1, 1)
            turn(("turn", 1, 2))
            stage("gates", 1, 0)
            act_e.wait_ge(dve_step, base[("places", 1, 0)][2] + STAGE_SHAPES["places"][2])
            n_pass = act_e.value_load(passes[0:1, 0:1], min_val=1, max_val=2)
            with act_e.Fori(0, n_pass) as ps:
                with act_e.Fori(0, NE) as e:
                    job = ps * NE + e
                    act_e.wait_ge(gathered, job + 1)
                    act_e.activation(pickT[:, :], PB[3][:, 0:SEQ], ACT.Copy)
                    for b in range(2):
                        last = act_e.activation(e_hi[:, 4 * b:4 * b + 4, :].rearrange("p k n -> p (k n)"),
                                                MB[2 + b][:, :], ACT.Copy)
                    last.then_inc(gather_hi, 1)
                    ffn_points(MOE0, job * NF, NF + job * NF, 1)
                    act_e.wait_ge(unit_used, job * N_FFN + (MOE0 + N_FFN))
                    for c in range(2):
                        last = act_e.activation(y_hi[:, c * 512:(c + 1) * 512], MB[c][:, :], ACT.Copy)
                    last.then_inc(y_hi_made, 1)
            stage("norm", DEPTH, 0)

        @block.vector
        def _(dve):
            v = nc.vector
            count = [0]

            def inc(instruction):
                count[0] += 1
                return instruction.then_inc(dve_step, 1)

            def link(instruction):
                inc(instruction)
                dve.wait_ge(dve_step, count[0])

            def end(key):
                want = base[key][2] + STAGE_SHAPES[key[0]][2]
                assert count[0] == want, (key, count[0] - base[key][2])

            def convert(u, turns):
                dve.wait_ge(hi_made, turns * RAW + (u + 1))
                if u >= RING:
                    dve.wait_ge(unit_used, turns * RAW + (u - RING + 1))
                n = size_of(u)
                v.tensor_tensor(w_lo[slot_of(u)][:, 0:n], raw[u % RAW][:, 0:n], w_hi[slot_of(u)][:, 0:n].bitcast(F32),
                                ALU.subtract).then_inc(lo_made, 1)

            def rest(lo, src, hi):
                return v.tensor_tensor(lo, src, hi.bitcast(F32), ALU.subtract)

            def turn(key):
                p, a, d = base[key]
                for b in range(4):
                    dve.wait_ge(act_step, a + b + 1)
                    f = lambda t: t[:, 2 * b:2 * b + 2, :].rearrange("p k n -> p (k n)")
                    inc(rest(f(hT_lo), PB[b][:, :], f(hT_hi)))
                end(key)

            def norm(layer, i):
                key = ("norm", layer, i)
                p, a, d = base[key]
                n = 2 * layer + i
                if n == 0:
                    dve.wait_ge(x_in, 16)
                if d:
                    dve.wait_ge(dve_step, d)
                for t in range(NT):
                    inc(v.scalar_tensor_tensor(out=nat[:, t, :], in0=x[:, t, :], scalar=1.0, in1=x[:, t, :],
                                               op0=ALU.mult, op1=ALU.mult, accum_out=stat[:, t:t + 1]))
                dve.wait_ge(dve_step, count[0])
                link(v.tensor_scalar(stat[:, 2:4], stat[:, 0:2], 1.0 / DM, RMS_EPS, ALU.mult, ALU.add))
                dve.wait_ge(act_step, a + 1)
                link(v.reciprocal(stat[:, 4:6], stat[:, 2:4]))
                dve.wait_ge(gains_in, 16 * (n + 1))
                for t in range(NT):
                    link(v.scalar_tensor_tensor(out=nat[:, t, :], in0=x[:, t, :], scalar=stat[:, 4 + t:5 + t],
                                                in1=gain_row, op0=ALU.mult, op1=ALU.mult))
                end(key)

            def head_norm(key, center):
                p, a, d = base[key]
                before = base[("ret_last" if center else "hgrn_last", key[1], 0)]
                dve.wait_ge(act_step, before[1] + 1)
                o3 = o_nat[:, :, :].rearrange("p t (h d) -> p (t h) d", d=HD)
                sq3 = square.rearrange("p (g d) -> p g d", d=HD)
                eps = RMS_EPS
                if center:
                    eps = LN_EPS
                    link(v.tensor_reduce(stat[:, 32:40], o3, axis=AX.X, op=ALU.add))
                    link(v.tensor_scalar(stat[:, 32:40], stat[:, 32:40], 1.0 / HD, None, ALU.mult))
                    link(v.tensor_tensor(o3, o3, broadcast(stat[:, 32:40], HD), ALU.subtract))
                link(v.tensor_tensor(sq3, o3, o3, ALU.mult))
                link(v.tensor_reduce(stat[:, 32:40], sq3, axis=AX.X, op=ALU.add))
                link(v.tensor_scalar(stat[:, 32:40], stat[:, 32:40], 1.0 / HD, eps, ALU.mult, ALU.add))
                dve.wait_ge(act_step, a + 1)
                link(v.reciprocal(stat[:, 32:40], stat[:, 32:40]))
                link(v.tensor_tensor(o3, o3, broadcast(stat[:, 32:40], HD), ALU.mult))
                row = lambda i: rows[:, i:i + 1, :].broadcast_to([P, NT, BW])
                dve.wait_ge(rows_in, 48 * (key[1] + 1))
                link(v.tensor_tensor(o_nat[:, :, :], o_nat[:, :, :], row(1 if center else 0), ALU.mult))
                if center:
                    link(v.tensor_tensor(o_nat[:, :, :], o_nat[:, :, :], row(2), ALU.add))
                g = rg if center else hg
                dve.wait_ge(chunk_out, 15 * key[1] + (Q_RG if center else Q_HI) + 1)
                link(v.tensor_tensor(o_nat[:, :, :], o_nat[:, :, :], g[:, :, :], ALU.mult))

            def stage(name, layer, arg):
                key = (name, layer, arg)
                p, a, d = base[key]
                assert count[0] == d, key
                if STAGE_SHAPES[name][2] == 0:
                    return
                if d:
                    dve.wait_ge(dve_step, d)
                chunk = lambda q: dve.wait_ge(chunk_out, 15 * layer + q + 1)
                psum = lambda: dve.wait_ge(stage_psum, p + 1)
                if name == "bounds":
                    dve.wait_ge(params_in, 16 * N_PARAMS)
                    l0, l1 = lb_in[:, :, 0], lb_in[:, :, 1]
                    link(v.tensor_tensor(lower1[:, 0:2], l0, l1, ALU.max))
                    top2 = lower1[:, 0:2]
                    both = lower1[:, 4:8].rearrange("p (l c) -> p l c", l=2)
                    v.tensor_tensor(both[:, 0, :], l0, top2, ALU.subtract)
                    inc(v.tensor_tensor(both[:, 1, :], l1, top2, ALU.subtract))
                    dve.wait_ge(act_step, a + 1)
                    link(v.tensor_tensor(lower1[:, 4:6], lower1[:, 0:2], lower1[:, 2:4], ALU.add))
                    link(v.reciprocal(lower1[:, 4:6], lower1[:, 4:6]))
                    link(v.tensor_tensor(lower1[:, 0:2], lower1[:, 0:2], lower1[:, 4:6], ALU.mult))
                    link(v.tensor_tensor(lower1[:, 2:4], lower1[:, 2:4], lower1[:, 4:6], ALU.mult))
                    link(v.tensor_tensor(lower1[:, 4:6], lower1[:, 0:2], lower1[:, 2:4], ALU.add))
                    v.tensor_tensor(lower[:, 0, :], lower1[:, 0:2], lower1[:, 0:2], ALU.subtract)
                    link(v.tensor_tensor(lower[:, 1, :], lower1[:, 4:6], lower1[:, 0:2], ALU.subtract))
                    link(v.tensor_scalar(upper[:, :, :], lower[:, :, :], -1.0, 1.0, ALU.mult, ALU.add))
                elif name == "pool_means":
                    chunk(Q_PU)
                    s2, s4 = pool_sum
                    inc(v.memset(upad[:, :, 0:16], 0.0))
                    dve.wait_ge(dve_step, count[0])
                    link(v.tensor_tensor(s2[:, :, 1:272], upad[:, :, 1:272], upad[:, :, 0:271], ALU.add))
                    link(v.tensor_tensor(s4[:, :, 3:272], s2[:, :, 3:272], s2[:, :, 1:270], ALU.add))
                    link(v.tensor_tensor(s2[:, 1, 7:272], s4[:, 1, 7:272], s4[:, 1, 3:268], ALU.add))
                    link(v.tensor_tensor(s4[64:128, 1, 15:272], s2[64:128, 1, 15:272], s2[64:128, 1, 7:264], ALU.add))
                    heads_tab = T["win_head"].rearrange("p (c n) -> p c n", c=2)
                    for c in range(2):
                        for b, s in ((0, s2), (1, s4)):
                            ps = slice(64 * b, 64 * b + 64)
                            link(v.tensor_tensor(s[ps, c, 16:32], s[ps, c, 16:32], heads_tab[ps, c, :], ALU.mult))
                            inc(v.scalar_tensor_tensor(out=pool_d[ps, c, :], in0=s[ps, c, 16:272],
                                                       scalar=T["inv_win"][ps, c:c + 1], in1=upad[ps, c, 16:272],
                                                       op0=ALU.mult, op1=ALU.subtract))
                elif name == "pool_out":
                    dve.wait_ge(act_step, a + 1)
                    for c in range(2):
                        last = v.scalar_tensor_tensor(out=oT_lo[0][:, c, :], in0=MB[0][:, c * SEQ:(c + 1) * SEQ],
                                                      scalar=pool_s[:, layer, c:c + 1],
                                                      in1=oT_hi[0][:, c, :].bitcast(F32), op0=ALU.mult, op1=ALU.subtract)
                    inc(last)
                elif name == "rope":
                    psum()
                    tmp = o_nat[:, :, :]
                    tab = lambda n: T[n].unsqueeze(1).broadcast_to([P, 2, SEQ])
                    for i, t in enumerate((rq, rk)):
                        link(v.tensor_tensor(tmp, MB[i][:, :].rearrange("p (c n) -> p c n", c=2), tab("sin"), ALU.mult))
                        link(v.tensor_tensor(t[:, :, :], t[:, :, :], tab("cos"), ALU.mult))
                        link(v.tensor_tensor(t[:, :, :], t[:, :, :], tmp, ALU.add))
                elif name == "ret_head":
                    psum()
                    dec = T["decay"][:, arg * SEQ:(arg + 1) * SEQ]
                    bank = MB[arg % 2]
                    inc(v.tensor_tensor(score[:, arg % 2, 0:SEQ], bank[:, 0:SEQ], dec, ALU.mult))
                    inc(v.tensor_tensor(score[:, arg % 2, SEQ:384], bank[:, SEQ:384], dec[:, 0:P], ALU.mult))
                elif name == "ret_norm":
                    head_norm(key, True)
                elif name == "hgrn_norm":
                    head_norm(key, False)
                elif name == "fox_log":
                    chunk(Q_FV)
                    z3 = stat[:, 40:48].rearrange("p (t h) -> p t h", t=NT)
                    link(v.tensor_tensor(z3, fv[:, :, BW:BW + NH],
                                         fox_b[:, layer:layer + 1, :].broadcast_to([P, NT, NH]), ALU.add))
                    dve.wait_ge(act_step, a + 2)
                    link(v.tensor_scalar(stat[:, 48:56], stat[:, 48:56], 1.0, None, ALU.add))
                    link(v.tensor_scalar(stat[:, 40:48], stat[:, 40:48], 0.0, None, ALU.min))
                    dve.wait_ge(act_step, a + 3)
                    inc(v.tensor_tensor(stat[:, 16:24], stat[:, 48:56], stat[:, 40:48], ALU.subtract))
                elif name == "fox_head":
                    psum()
                    link(v.tensor_tensor(fox_p[:, arg, :], MB[arg][:, 0:384], T["causal"], ALU.add))
                    inc(v.tensor_reduce(stat[:, 24:25], fox_p[:, arg, 0:P], axis=AX.X, op=ALU.max, negate=True))
                    inc(v.tensor_reduce(stat[:, 25:26], fox_p[:, arg, P:384], axis=AX.X, op=ALU.max, negate=True))
                    dve.wait_ge(act_step, a + 2)
                    inc(v.reciprocal(stat[:, 6 + 2 * arg:8 + 2 * arg], stat[:, 26:28]))
                    dve.wait_ge(dve_step, count[0])
                elif name == "fox_mix":
                    psum()
                    hs = slice(arg * HD, (arg + 1) * HD)
                    for t in range(NT):
                        inc(v.tensor_scalar(o_nat[:, t, hs], MB[2 + t][:, hs], stat[:, 6 + 2 * arg + t:7 + 2 * arg + t],
                                            None, ALU.mult))
                elif name == "hgrn_log":
                    chunk(Q_HQ)
                    for c in range(2):
                        inc(v.tensor_scalar(hf[:, c, :], hf[:, c, :], upper[:, layer, c:c + 1],
                                            lower[:, layer, c:c + 1], ALU.mult, ALU.add))
                        inc(v.tensor_scalar(hk[:, c, :], hk[:, c, :], upper[:, layer, c:c + 1], None, ALU.mult))
                    dve.wait_ge(dve_step, count[0])
                    inc(v.tensor_scalar(hf[:, :, :], hf[:, :, :], TINY, None, ALU.max))
                    dve.wait_ge(act_step, a + 1)
                    for c in range(2):
                        for n in range(NCH):
                            s = slice(n * CH, (n + 1) * CH)
                            inc(v.tensor_tensor_scan(hf[:, c, s], T["ones"][:, 0:CH], hf[:, c, s], 0.0,
                                                     ALU.mult, ALU.add))
                elif name == "hgrn_span":
                    c = arg
                    if c == 0:
                        dve.wait_ge(stage_psum, base[("branch_turn", layer, 1)][0] + 1)
                    else:
                        dve.wait_ge(stage_psum, base[("hgrn_b", layer, 1)][0] + 1)
                    lg = hf[:, c, :]
                    for i, b in enumerate(LEVELS[1:]):
                        h = b // 2
                        src = lg.rearrange("p (n b) -> p n b", b=b)
                        dst = span[:, 2 + i, :].rearrange("p (n b) -> p n b", b=b)
                        mid = src[:, :, h - 1:h].broadcast_to([P, SEQ // b, h])
                        inc(v.tensor_tensor(dst[:, :, h:b], src[:, :, h:b], mid, ALU.subtract))
                        inc(v.tensor_tensor(dst[:, :, 0:h], mid, src[:, :, 0:h], ALU.subtract))
                    src = lg.rearrange("p (g n b) -> p g n b", n=2, b=CH)
                    dst = span[:, 1, :].rearrange("p (g n b) -> p g n b", n=2, b=CH)
                    v.tensor_copy(dst[:, :, 1, :], src[:, :, 1, :])
                    link(v.tensor_tensor(dst[:, :, 0, :], src[:, :, 0, CH - 1:CH].broadcast_to([P, 2, CH]),
                                         src[:, :, 0, :], ALU.subtract))
                    last_of = lambda n: lg[:, n * CH + CH - 1:n * CH + CH]
                    sl = lambda n: slice(n * CH, (n + 1) * CH)
                    v.tensor_scalar(span[:, 0, sl(0)], span[:, 1, sl(0)], last_of(1), None, ALU.add)
                    v.tensor_tensor(span[:, 0, sl(1)], last_of(1).broadcast_to([P, CH]), lg[:, sl(1)], ALU.subtract)
                    v.tensor_copy(span[:, 0, sl(2)], lg[:, sl(2)])
                    inc(v.tensor_scalar(span[:, 0, sl(3)], lg[:, sl(3)], last_of(2), None, ALU.add))
                    dve.wait_ge(act_step, a + 1)
                    for lev, b in enumerate([256] + LEVELS):
                        h = b // 2
                        e = span[:, lev, :].rearrange("p (n b) -> p n b", b=b)
                        q = hq[:, c, :].rearrange("p (n b) -> p n b", b=b)
                        k = hk[:, c, :].rearrange("p (n b) -> p n b", b=b)
                        inc(v.tensor_tensor(e[:, :, h:b], e[:, :, h:b], q[:, :, h:b], ALU.mult))
                        inc(v.tensor_tensor(e[:, :, 0:h], e[:, :, 0:h], k[:, :, 0:h], ALU.mult))
                elif name in ("hgrn_a", "hgrn_b"):
                    psum()
                    t = 0 if name == "hgrn_a" else 1
                    mk = T["masks"]
                    inc(v.tensor_tensor(masked[:, 0:4, :].rearrange("p l n -> p (l n)"), MB[0][:, :],
                                        table[:, where["masks"][0]:where["masks"][0] + 512], ALU.mult))
                    link(v.tensor_tensor(masked[:, 4:8, :].rearrange("p l n -> p (l n)"), MB[1][:, :],
                                         table[:, where["masks"][0] + 512:where["masks"][0] + 1024], ALU.mult))
                    if t == 1:
                        v.tensor_copy(score[:, arg % 2, P:2 * P], MB[2][:, SEQ:SEQ + P])
                    inc(v.tensor_reduce(score[:, arg % 2, t * SEQ:t * SEQ + P],
                                        masked[:, :, :].rearrange("p l n -> p n l"), axis=AX.X, op=ALU.add))
                    dve.wait_ge(dve_step, count[0])
                elif name == "branch_turn":
                    dve.wait_ge(act_step, a + 1)
                    i = BRANCHES.index(arg)
                    flat = lambda t: t[:, :, :].rearrange("p c n -> p (c n)")
                    inc(rest(flat(oT_lo[i % 2]), MB[0][:, :], flat(oT_hi[i % 2])))
                elif name == "split_router":
                    dve.wait_ge(router_in, 16)
                    link(v.tensor_copy(router_hi[:, :, :], router[:, :, :]))
                    inc(rest(router_lo[:, :, :], router[:, :, :], router_hi[:, :, :]))
                elif name == "router":
                    psum()
                    inc(v.tensor_copy(logit[:, :, :].rearrange("p t e -> p (t e)"), MB[0][:, 0:NT * NE]))
                    dve.wait_ge(dve_step, count[0])
                elif name == "gates":
                    for t in range(NT):
                        inc(v.max(top[:, t, :], logit[:, t, :]))
                    dve.wait_ge(dve_step, count[0])
                    for t in range(NT):
                        inc(v.max_index(top_at[:, t, :], top[:, t, :], logit[:, t, :]))
                    dve.wait_ge(dve_step, count[0])
                    link(v.tensor_copy(top_f[:, :, :], top_at[:, :, :]))
                    iota8 = T["iota"][:, 0:NE]
                    for r in range(2):
                        for t in range(NT):
                            v_ = v.tensor_scalar(hot[:, r, t, :], iota8, top_f[:, t, r:r + 1], None, ALU.is_equal)
                        inc(v_)
                    link(v.tensor_tensor(stat[:, 8:10], top[:, :, 1], top[:, :, 0], ALU.subtract))
                    dve.wait_ge(act_step, a + 1)
                    link(v.tensor_scalar(stat[:, 10:12], stat[:, 8:10], 1.0, None, ALU.add))
                    link(v.reciprocal(weight[:, 0, :], stat[:, 10:12]))
                    link(v.tensor_tensor(weight[:, 1, :], weight[:, 0, :], stat[:, 8:10], ALU.mult))
                    for t in range(NT):
                        link(v.tensor_scalar(gate[:, t, :], hot[:, 1, t, :], weight[:, 1, t:t + 1], None, ALU.mult))
                        link(v.scalar_tensor_tensor(out=gate[:, t, :], in0=hot[:, 0, t, :], scalar=weight[:, 0, t:t + 1],
                                                    in1=gate[:, t, :], op0=ALU.mult, op1=ALU.add))
                    inc(v.tensor_tensor(chosen[:, :, :], hot[:, 0], hot[:, 1], ALU.add))
                    dve.wait_ge(act_step, a + 2)
                    rest(h_lo[:, :, :], nat[:, :, :], h_hi[:, :, :]).then_inc(h_split, 1)
                elif name == "places":
                    psum()
                    cum = MB[0][:, 0:2 * NE].rearrange("p (t e) -> p t e", t=NT)
                    link(v.tensor_tensor(slot[:, :, 0:NE], cum, chosen[:, :, :], ALU.mult))
                    link(v.tensor_scalar(slot[:, :, 0:NE], slot[:, :, 0:NE], -1.0, None, ALU.add))
                    link(v.tensor_scalar(slot[:, :, NE:2 * NE], slot[:, :, 0:NE], -float(P), None, ALU.add))
                    link(v.tensor_reduce(stat[:, 12:13], MB[0][:, 2 * NE:3 * NE], axis=AX.X, op=ALU.max))
                    link(v.tensor_scalar(stat[:, 12:13], stat[:, 12:13], float(P), 1.0, ALU.is_gt, ALU.add))
                    link(v.tensor_copy(passes[:, :], stat[:, 12:13]))
                end(key)

            def layer_points(layer, u0):
                for u in range(N_LAYER):
                    r = (u - N_MIX) % 5
                    if u > N_MIX and r == 0 and u <= N_LAYER - 4:
                        i = (u - N_MIX) // 5 - 1
                        for t in range(NT):
                            for c in range(2):
                                if (t, c) == (1, 1):
                                    dve.wait_ge(unit_used, u0 + u)
                                else:
                                    dve.wait_ge(branch_done, 12 * layer + 3 * i + 2 * t + c + 1)
                                cs = slice(c * 512, (c + 1) * 512)
                                if i == 0:
                                    v.tensor_tensor(nat[:, t, cs], PB[2 * t + c][:, :], sig[:, t, cs],
                                                    ALU.mult).then_inc(branch_out, 1)
                                else:
                                    v.tensor_tensor(sig[:, t, cs], PB[2 * t + c][:, :], sig[:, t, cs],
                                                    ALU.mult).then_inc(sig_used, 1)
                                    dve.wait_ge(sig_used, 12 * layer + 4 * (i - 1) + 2 * t + c + 1)
                                    v.tensor_tensor(nat[:, t, cs], nat[:, t, cs], sig[:, t, cs],
                                                    ALU.add).then_inc(branch_out, 1)
                    for name, arg in PLAN.get(u, []):
                        stage(name, layer, arg)
                    if u == N_LAYER - 4:
                        turn(("turn", layer, 1))
                    if u == N_LAYER - 2:
                        add_out(layer, 0, u0 + u)
                    convert(u0 + u + RING, 0)
                add_out(layer, 1, u0 + N_LAYER)

            def add_out(layer, c, u):
                dve.wait_ge(unit_used, u)
                for t in range(NT):
                    cs = slice(c * 512, (c + 1) * 512)
                    v.tensor_tensor(x[:, t, cs], x[:, t, cs], PB[2 * c + t][:, :], ALU.add).then_inc(out_added, 1)
                if c:
                    dve.wait_ge(out_added, 4 * (layer + 1))

            def take_act(u, turns, c, tiles):
                dve.wait_ge(unit_used, turns * RAW + (u + 1))
                dve.wait_ge(silu_made, c + 1)
                if not (isinstance(c, int) and c == 0):
                    dve.wait_ge(act_turned, c)
                for t in range(tiles):
                    last = v.tensor_tensor(act[:, t, :], silu_g[:, t, :], PB[2 + t][:, :], ALU.mult)
                last.then_inc(act_made, 1)

            def take_turned(c, tiles):
                dve.wait_ge(aT_hi_made, c + 1)
                for t in range(tiles):
                    ts = slice(t * P, (t + 1) * P)
                    last = rest(aT_lo[:, :, ts], PB[2 + t][:, :].rearrange("p (b n) -> p b n", b=FB), aT_hi[:, :, ts])
                last.then_inc(aT_lo_made, 1)

            def ffn_points(u0, turns, c0, tiles):
                ahead = lambda u, o: convert(u + RING, o)
                for i in range(4):
                    ahead(u0 + i, turns)
                take_act(u0 + 3, turns, c0, tiles)
                take_turned(c0, tiles)
                with dve.Fori(1, NF) as j:
                    o = turns + (j - 1)
                    c = c0 + j
                    for i in range(4, 8):
                        ahead(u0 + i, o)
                    take_act(u0 + 7, o, c, tiles)
                    ahead(u0 + 8, o)
                    ahead(u0 + 9, o)
                    take_turned(c, tiles)
                ahead(u0 + 40, turns)
                ahead(u0 + 41, turns)

            v.memset(zeros_r[:, :].bitcast(F32), 0.0).then_inc(zeroed, 1)
            stage("bounds", 0, 0)
            norm(0, 0)
            for u in range(RING):
                convert(u, 0)
            turn(("turn", 0, 0))
            dve.wait_ge(table_in, 16)
            layer_points(0, 0)
            norm(0, 1)
            turn(("turn", 0, 2))
            ffn_points(FFN0, 0, 0, NT)
            dve.wait_ge(unit_used, FFN0 + N_FFN)
            for t in range(NT):
                for c in range(2):
                    cs = slice(c * 512, (c + 1) * 512)
                    v.tensor_tensor(x[:, t, cs], x[:, t, cs], MB[2 * t + c][:, :], ALU.add).then_inc(ffn_added, 1)
            dve.wait_ge(ffn_added, 4)
            norm(1, 0)
            turn(("turn", 1, 0))
            layer_points(1, LAYER1)
            norm(1, 1)
            turn(("turn", 1, 2))
            stage("split_router", 1, 0)
            stage("router", 1, 0)
            stage("gates", 1, 0)
            stage("places", 1, 0)
            dve.wait_ge(dve_step, count[0])
            n_pass = dve.value_load(passes[0:1, 0:1], min_val=1, max_val=2)
            with dve.Fori(0, n_pass) as ps:
                with dve.Fori(0, NE) as e:
                    job = ps * NE + e
                    for t in range(NT):
                        last = v.tensor_scalar(pick[:, t, :], T["iota"], slot[:, t, bass.ds(job, 1)], None, ALU.is_equal)
                    last.then_inc(picked, 1)
                    dve.wait_ge(gather_hi, job + 1)
                    for b in range(2):
                        f = lambda t_: t_[:, 4 * b:4 * b + 4, :].rearrange("p k n -> p (k n)")
                        last = rest(f(e_lo), MB[2 + b][:, :], f(e_hi))
                    last.then_inc(gather_lo, 1)
                    ffn_points(MOE0, job * NF, NF + job * NF, 1)
                    dve.wait_ge(y_hi_made, job + 1)
                    for c in range(2):
                        cs = slice(c * 512, (c + 1) * 512)
                        last = rest(y_lo[:, cs], MB[c][:, :], y_hi[:, cs])
                    last.then_inc(y_lo_made, 1)
                    dve.wait_ge(scattered, job + 1)
                    for t in range(NT):
                        for c in range(2):
                            cs = slice(c * 512, (c + 1) * 512)
                            bank = (MB[2 + c], PB[1 + 2 * c])[t]
                            last = v.scalar_tensor_tensor(out=x[:, t, cs], in0=bank[:, :],
                                                          scalar=gate[:, t, bass.ds(e, 1)], in1=x[:, t, cs],
                                                          op0=ALU.mult, op1=ALU.add)
                    last.then_inc(moe_added, 1)
                    dve.wait_ge(moe_added, job + 1)
            norm(DEPTH, 0)


_INS = ["x", "w_in", "w_branch", "w_out", "norm_mix_g", "hgrn_lb_logits", "hgrn_norm_g", "fox_f_bias",
        "pool_w", "pool_scale", "ret_gn_g", "ret_gn_b", "norm_ffn_g", "ffn_w_gate", "ffn_w_up",
        "ffn_w_down", "moe_router", "moe_w_gate", "moe_w_up", "moe_w_down", "final_norm_g"]


def kernel(**inputs):
    import concourse.bacc as bacc
    from concourse.bass_utils import run_bass_kernel_spmd

    nc = bacc.Bacc("TRN2", target_bir_lowering=False, num_devices=1)
    consts, where = constants()
    arrays = {"in_consts": consts}
    A = {}
    for name in _INS:
        a = np.ascontiguousarray(inputs[name])
        arrays[f"in_{name}"] = a
        A[name] = nc.dram_tensor(f"in_{name}", a.shape, mybir.dt.from_np(a.dtype), kind="ExternalInput").ap()
    c = nc.dram_tensor("in_consts", consts.shape, F32, kind="ExternalInput").ap()
    o = nc.dram_tensor("out_0", (1, SEQ, DM), F32, kind="ExternalOutput").ap()
    build(nc, where, A, c, o)
    r = run_bass_kernel_spmd(nc, [arrays], core_ids=[0])
    return r.results[0]["out_0"]
```

```python
from contextlib import ExitStack

import numpy as np

import concourse.bass as bass
from concourse import mybir
from concourse.alu_op_type import AluOpType as ALU

F32 = mybir.dt.float32
F32R = mybir.dt.float32r
I32 = mybir.dt.int32
U32 = mybir.dt.uint32
ACT = mybir.ActivationFunctionType
AX = mybir.AxisListType

P = 128
SEQ, DM, DEPTH = 256, 1024, 2
NT = SEQ // P
KC = DM // P
BW, HD, NH, NB = 256, 64, 4, 4
CH = 64
NCH = SEQ // CH
FF, NE = 7 * DM // 2, 8
FCH = 512
NF = FF // FCH
FB = FCH // P
RMS_EPS, LN_EPS = 1e-6, 1e-5
NEG = -1e30
TINY = 2.0 ** -63

RAW, RING, AHEAD = 6, 3, 2
UNIT = 2048

C_HQ, C_HI, C_FQ, C_FV, C_PU, C_RK, C_RG, C_GATE = 0, 512, 1024, 1536, 1796, 2308, 2820, 3076
MIX_CHUNKS = [(C_PU, 512, "T"), (C_RK, 512, "M"), (C_RG, 256, "N"), (C_FQ, 512, "T"),
              (C_FV, 260, "N"), (C_HQ, 512, "T"), (C_HI, 512, "N")]
Q_PU, Q_RK, Q_RG, Q_FQ, Q_FV, Q_HQ, Q_HI = range(7)
BRANCHES = [2, 3, 1, 0]
LEVELS = [128, 64, 32, 16, 8, 4, 2]

N_MIX = 2 * len(MIX_CHUNKS)
N_LAYER = N_MIX + NB * 5 + 4
N_FFN = NF * 6
FFN0 = N_LAYER
LAYER1 = N_LAYER + N_FFN
MOE0 = LAYER1 + N_LAYER


def constants():
    i = np.arange(P)
    s, t = i[:, None], i[None, :]
    parts = {}
    masks = []
    for b in LEVELS:
        h = b // 2
        masks.append(((s // b == t // b) & (s % b < h) & (t % b >= h)).astype(np.float32))
    parts["masks"] = np.concatenate(masks, 1)
    parts["ident"] = np.eye(P, dtype=np.float32)
    parts["tri"] = (s <= t).astype(np.float32)
    parts["ones"] = np.ones((P, P), np.float32)
    causal = np.where(t <= s, 0.0, NEG).astype(np.float32)
    parts["causal"] = np.concatenate([causal, np.zeros((P, P), np.float32), causal], 1)
    rot = np.zeros((P, P), np.float32)
    half = HD // 2
    for m in range(P):
        if m % HD < half:
            rot[m + half, m] = -1.0
        else:
            rot[m - half, m] = 1.0
    parts["rot"] = rot
    parts["iota"] = np.broadcast_to(i.astype(np.float32), (P, P))
    tt = np.arange(SEQ)[None, :]
    gamma = np.log1p(-np.exp2(-5.0 - np.arange(NH)))
    parts["decay"] = np.concatenate(
        [np.where(tt >= s, np.exp((tt - s) * gamma[h]), 0.0) for h in range(NH)], 1).astype(np.float32)
    inv_freq = (10000.0 ** (-np.arange(half, dtype=np.float32) / half)).astype(np.float32)
    ang = (np.arange(SEQ, dtype=np.float32)[None, :] * inv_freq[(i % half)][:, None]).astype(np.float32)
    parts["cos"] = np.cos(ang).astype(np.float32)
    parts["sin"] = np.sin(ang).astype(np.float32)
    win = np.array([[2, 8], [4, 16]])[(i >= 64).astype(int)]
    head = np.minimum(np.arange(16)[None, None, :] + 1, win[:, :, None])
    parts["inv_win"] = (1.0 / win).astype(np.float32)
    parts["win_head"] = (win[:, :, None] / head).reshape(P, 32).astype(np.float32)
    where, at = {}, 0
    for name, a in parts.items():
        where[name] = (at, a.shape[1])
        at += a.shape[1]
    return np.ascontiguousarray(np.concatenate(list(parts.values()), 1), dtype=np.float32), where


STAGE_SHAPES = {
    "bounds": (0, 1, 9),
    "norm": (0, 1, 6), "turn": (1, 4, 4),
    "pool_means": (0, 0, 13), "pool_out": (1, 1, 1),
    "rope": (1, 0, 6),
    "ret_pair": (1, 0, 4), "ret_last": (1, 1, 0), "ret_norm": (0, 1, 11),
    "fox_log": (0, 3, 4), "fox_pair": (1, 4, 7), "fox_probs": (1, 2, 0), "fox_last": (1, 0, 2),
    "hgrn_log": (0, 0, 5), "hgrn_ln": (0, 1, 0), "hgrn_scan": (0, 0, 8),
    "hgrn_exponents": (0, 0, 14), "hgrn_exp": (0, 1, 0), "hgrn_span": (0, 0, 16),
    "hgrn_a": (1, 0, 3), "hgrn_b": (1, 0, 3), "hgrn_last": (1, 1, 0), "hgrn_norm": (0, 1, 7),
    "branch_turn": (1, 1, 1),
    "split_router": (0, 0, 2), "router": (1, 0, 1), "gates": (0, 2, 18), "places": (1, 0, 7),
}


def mixer_plan(layer):
    plan = {}
    put = lambda at, *st: plan.setdefault(at, []).append(st)
    put(2, "pool_means", 0)
    put(4, "pool_out", 0)
    put(5, "rope", 0)
    put(7, "ret_pair", 0)
    put(8, "ret_pair", 1)
    put(9, "ret_last", 0)
    put(9, "ret_norm", 0)
    put(10, "fox_log", 0)
    put(11, "branch_turn", 3)
    put(12, "fox_pair", 0)
    put(13, "fox_pair", 1)
    if layer == 0:
        put(14, "bounds", 0)
    put(14, "hgrn_log", 0)
    put(15, "fox_probs", 0)
    put(15, "hgrn_ln", 0)
    put(16, "fox_probs", 1)
    put(16, "hgrn_scan", 0)
    put(17, "fox_last", 0)
    put(18, "hgrn_exponents", 0)
    put(19, "branch_turn", 1)
    put(19, "hgrn_exp", 0)
    put(20, "hgrn_span", 0)
    for h in range(2):
        put(21 + 2 * h, "hgrn_a", h)
        put(22 + 2 * h, "hgrn_b", h)
    put(24, "hgrn_exponents", 1)
    put(25, "hgrn_exp", 1)
    put(26, "hgrn_span", 1)
    for h in range(2):
        put(27 + 2 * h, "hgrn_a", 2 + h)
        put(28 + 2 * h, "hgrn_b", 2 + h)
    put(31, "hgrn_last", 0)
    put(31, "hgrn_norm", 0)
    put(33, "branch_turn", 0)
    return plan


HGRN_PREPARES = ("bounds", "hgrn_log", "hgrn_ln", "hgrn_scan", "hgrn_exponents", "hgrn_exp")
APART = {"fox_probs": HGRN_PREPARES, "fox_last": HGRN_PREPARES, "branch_turn": HGRN_PREPARES + ("fox_log",)}

PLANS = [mixer_plan(layer) for layer in range(DEPTH)]


def stage_order():
    order = []
    for layer in range(DEPTH):
        if layer == 1:
            order.append(("split_router", layer, 0))
        order += [("norm", layer, 0), ("turn", layer, 0)]
        for u in range(N_LAYER):
            order += [(name, layer, arg) for name, arg in PLANS[layer].get(u, [])]
            if u == N_LAYER - 4:
                order.append(("turn", layer, 1))
        order += [("norm", layer, 1), ("turn", layer, 2)]
        if layer == 1:
            order += [("router", layer, 0), ("gates", layer, 0), ("places", layer, 0)]
    order.append(("norm", DEPTH, 0))
    return order


def build(nc, where, A, consts_ap, out_ap):
    ctx = ExitStack()
    with ctx:
        sem = lambda name: ctx.enter_context(nc.semaphore(name))
        keep = ExitStack()

        def sb(name, shape, dt=F32, stack=ctx):
            return stack.enter_context(nc.sbuf_tensor(name, shape, dt))

        raw = [sb(f"raw{i}", [P, UNIT]) for i in range(RAW)]
        w_hi = [sb(f"w_hi{i}", [P, UNIT], F32R) for i in range(RING)]
        w_lo = [sb(f"w_lo{i}", [P, UNIT], F32R) for i in range(RING)]
        table = sb("table", [P, sum(w for _, w in where.values())])
        T = {k: table[:, a:a + w] for k, (a, w) in where.items()}
        ident = T["ident"]
        x = sb("x_sb", [P, NT, DM])
        hT_hi = sb("hT_hi", [P, KC, SEQ], F32R)
        hT_lo = sb("hT_lo", [P, KC, SEQ], F32R)
        nat = sb("nat", [P, NT, DM])
        sig = sb("sig", [P, NT, DM])
        gain_row = sig[:, 0, :]
        zeros_r = sb("zeros_r", [P, P], F32R)
        stat = sb("stat", [P, 88])
        lb_in = sb("lb_in", [P, 2, DEPTH])
        lower = sb("lower", [P, DEPTH, 2])
        upper = sb("upper", [P, DEPTH, 2])
        pool_w = sb("pool_w_sb", [P, DEPTH, 2, HD])
        pool_s = sb("pool_s_sb", [P, DEPTH, 2])
        fox_b = sb("fox_b_sb", [P, DEPTH, NH])
        rows = sb("rows", [P, 3, BW])
        lower1 = sb("lower1", [P, 8])
        router = sb("router_sb", [P, KC, NE])
        router_hi = sb("router_hi", [P, KC, NE], F32R)
        router_lo = sb("router_lo", [P, KC, NE], F32R)

        mx = ExitStack()
        sbm = lambda name, shape, dt=F32: sb(name, shape, dt, mx)
        hq = sbm("hq", [P, 2, SEQ])
        hf = sbm("hf", [P, 2, SEQ])
        hk = sbm("hk", [P, 2, SEQ])
        fq = sbm("fq", [P, 2, SEQ])
        fk = sbm("fk", [P, 2, SEQ])
        rq = sbm("rq", [P, 2, SEQ])
        rk = sbm("rk", [P, 2, SEQ])
        upad = sbm("upad", [P, 2, 16 + SEQ])
        hv = sbm("hv", [P, NT, BW])
        hg = sbm("hg", [P, NT, BW])
        rv = sbm("rv", [P, NT, BW])
        rg = sbm("rg", [P, NT, BW])
        fv = sbm("fv", [P, NT, BW + NH])
        big = sbm("big", [P, 3072])
        pool_sum = [big[:, 272 * 2 * i:272 * 2 * (i + 1)].rearrange("p (c n) -> p c n", c=2) for i in range(2)]
        pool_d = big[:, 1088 + 512:1088 + 1024].rearrange("p (c n) -> p c n", c=2)
        fox_p = big[:, 0:4 * 384].rearrange("p (h n) -> p h n", h=NH)
        fox_pT = big[:, 4 * 384:8 * 384].rearrange("p (h n) -> p h n", h=NH)
        span = big[:, 0:2048].rearrange("p (l n) -> p l n", l=8)
        masked = big[:, 2048:3072].rearrange("p (l n) -> p l n", l=8)
        score = sbm("score", [P, 2, 384])
        square = score[:, :, :].rearrange("p a b -> p (a b)")[:, 0:512]
        o_nat = sbm("o_nat", [P, NT, BW])
        oT_hi = [sbm(f"oT_hi{i}", [P, 2, SEQ], F32R) for i in range(2)]
        oT_lo = [sbm(f"oT_lo{i}", [P, 2, SEQ], F32R) for i in range(2)]
        mx.close()

        silu_g = sb("silu_g", [P, NT, FCH], stack=keep)
        act = sb("act", [P, NT, FCH], stack=keep)
        aT_hi = sb("aT_hi", [P, FB, SEQ], F32R, keep)
        aT_lo = sb("aT_lo", [P, FB, SEQ], F32R, keep)
        h_hi = sb("h_hi", [P, NT, DM], F32R, keep)
        h_lo = sb("h_lo", [P, NT, DM], F32R, keep)
        pick = sb("pick", [P, NT, P], F32R, keep)
        pickT = sb("pickT", [P, SEQ], F32R, keep)
        e_hi = sb("e_hi", [P, KC, P], F32R, keep)
        e_lo = sb("e_lo", [P, KC, P], F32R, keep)
        y_hi = sb("y_hi", [P, DM], F32R, keep)
        y_lo = sb("y_lo", [P, DM], F32R, keep)
        logit = sb("logit", [P, NT, NE], stack=keep)
        top = sb("top", [P, NT, 8], stack=keep)
        top_at = sb("top_at", [P, NT, 8], U32, keep)
        top_f = sb("top_f", [P, NT, 8], stack=keep)
        hot = sb("hot", [P, 2, NT, NE], stack=keep)
        weight = sb("weight", [P, 2, NT], stack=keep)
        gate = sb("gate", [P, NT, NE], stack=keep)
        chosen = sb("chosen", [P, NT, NE], stack=keep)
        slot = sb("slot", [P, NT, 2 * NE + 2], stack=keep)
        job_gate = sb("job_gate", [P, NT, 2 * NE + 1], stack=keep)
        pick_back = sb("pick_back", [P, NT, P], stack=keep)
        passes = sb("passes", [P, 1], I32, keep)
        keep.close()

        PB = [ctx.enter_context(nc.psum_tensor(f"PB{i}", [P, 512], F32)) for i in range(4)]
        MB = [ctx.enter_context(nc.psum_tensor(f"MB{i}", [P, 512], F32)) for i in range(4)]

        raw_full = [sem(f"raw_full{i}") for i in range(RAW)]
        hi_made, lo_made, unit_used = sem("hi_made"), sem("lo_made"), sem("unit_used")
        chunk_out = sem("chunk_out")
        branch_out = sem("branch_out")
        merged = sem("merged")
        branch_done = sem("branch_done")
        out_added = sem("out_added")
        stage_psum, act_step, dve_step = sem("stage_psum"), sem("act_step"), sem("dve_step")
        x_in, first_gains_in, ident_in, table_in, params_in, rows_in, gains_in, router_in = (
            sem(n) for n in ("x_in", "first_gains_in", "ident_in", "table_in", "params_in", "rows_in", "gains_in", "router_in"))
        zeroed = sem("zeroed")
        silu_made, act_made, act_turned, aT_hi_made, aT_lo_made = (
            sem(n) for n in ("silu_made", "act_made", "act_turned", "aT_hi_made", "aT_lo_made"))
        ffn_added, down_done = sem("ffn_added"), sem("down_done")
        h_split = sem("h_split")
        picked, gathered, gather_hi, gather_lo = (
            sem(n) for n in ("picked", "gathered", "gather_hi", "gather_lo"))
        back_picked, back_turned, pickT_made = (sem(n) for n in ("back_picked", "back_turned", "pickT_made"))
        y_hi_made, y_lo_made, scattered, moe_added = (
            sem(n) for n in ("y_hi_made", "y_lo_made", "scattered", "moe_added"))
        stored = sem("stored")

        ORDER = stage_order()
        base, pe_n, a_n, d_n = {}, 0, 0, 0
        for key in ORDER:
            base[key] = (pe_n, a_n, d_n)
            shape = STAGE_SHAPES[key[0]]
            pe_n, a_n, d_n = pe_n + shape[0], a_n + shape[1], d_n + shape[2]

        def slot_of(u):
            return u % RING

        def size_of(u):
            local = u if u < FFN0 else u - LAYER1
            return 4 * MIX_CHUNKS[local // 2][1] if 0 <= local < N_MIX else UNIT

        def col_view(buf, width):
            return buf[:, 0:4 * width].rearrange("p (k n) -> p k n", k=4)

        def row_view(buf):
            return buf[:, :].rearrange("p (k n) -> p k n", k=2)

        def gate_bank(c, t):
            return PB[2 * ((len(MIX_CHUNKS) + c) % 2) + t]

        def broadcast(a, n):
            return a.unsqueeze(2).broadcast_to([P, a.shape[1], n])

        N_PARAMS = 9
        block = ctx.enter_context(nc.Block())

        @block.sync
        def _(sp):
            sp.dma_start(x[:, :, :], A["x"][0].rearrange("(t p) d -> p t d", p=P)).then_inc(x_in, 16)
            sp.dma_start(gain_row, A["norm_mix_g"][0].partition_broadcast(P)).then_inc(first_gains_in, 16)
            a, w = where["ident"]
            sp.dma_start(ident, consts_ap[:, a:a + w]).then_inc(ident_in, 16)

            def load(u, turns, src, dst):
                if u >= RAW:
                    sp.wait_ge(hi_made, turns * RAW + (u - RAW + 1))
                    sp.wait_ge(lo_made, turns * RAW + (u - RAW + 1))
                sp.dma_start(dst(raw[u % RAW]), src).then_inc(raw_full[u % RAW], 16)

            def load_cols(u, turns, w, half, c0, width):
                src = w[half * 512:(half + 1) * 512, c0:c0 + width].rearrange("(k p) n -> p k n", p=P)
                load(u, turns, src, lambda b: col_view(b, width))

            def load_rows(u, turns, w):
                load(u, turns, w.rearrange("(k p) n -> p k n", p=P), row_view)

            def load_layer(layer, u0):
                u = u0
                for c0, width, _ in MIX_CHUNKS:
                    for half in range(2):
                        load_cols(u, 0, A["w_in"][layer], half, c0, width)
                        u += 1
                for b in BRANCHES:
                    for c in range(2):
                        for half in range(2):
                            load_cols(u, 0, A["w_in"][layer], half, C_GATE + b * DM + c * 512, 512)
                            u += 1
                    load_rows(u, 0, A["w_branch"][layer, b])
                    u += 1
                for c in range(2):
                    for half in range(2):
                        load_cols(u, 0, A["w_out"][layer], half, c * 512, 512)
                        u += 1

            def load_ffn(u0, turns, w_gate, w_up, w_down):
                for half in range(2):
                    load_cols(u0 + half, turns, w_gate, half, 0, FCH)
                for half in range(2):
                    load_cols(u0 + 2 + half, turns, w_up, half, 0, FCH)
                with sp.Fori(1, NF) as j:
                    o = turns + (j - 1)
                    for w, at in ((w_gate, 4), (w_up, 6)):
                        for half in range(2):
                            src = w[half * 512:(half + 1) * 512, bass.ds(j * FCH, FCH)].rearrange(
                                "(k p) n -> p k n", p=P)
                            load(u0 + at + half, o, src, lambda b: col_view(b, FCH))
                    for i in range(2):
                        load_rows(u0 + 8 + i, o, w_down[bass.ds((j - 1) * FCH + i * 256, 256), :])
                for i in range(2):
                    load_rows(u0 + 40 + i, turns, w_down[FF - FCH + i * 256:FF - FCH + (i + 1) * 256, :])

            load_layer(0, 0)
            load_ffn(FFN0, 0, A["ffn_w_gate"][0], A["ffn_w_up"][0], A["ffn_w_down"][0])
            load_layer(1, LAYER1)

            def load_experts(job0):
                with sp.Fori(0, NE) as e:
                    w = [A[n][0, bass.ds(e, 1)].rearrange("a k n -> (a k) n")
                         for n in ("moe_w_gate", "moe_w_up", "moe_w_down")]
                    load_ffn(MOE0, (e + job0) * NF, *w)

            load_experts(0)
            sp.wait_ge(dve_step, base[("places", 1, 0)][2] + STAGE_SHAPES["places"][2])
            n_pass = sp.value_load(passes[0:1, 0:1], min_val=1, max_val=2)
            with sp.If(n_pass > 1):
                load_experts(NE)
            for i in range(AHEAD):
                u = MOE0 + i
                sp.wait_ge(hi_made, (n_pass * (NE * N_FFN)) + (u - RAW + 1))
                sp.sem_inc(raw_full[u % RAW], 16)
            key = ("norm", DEPTH, 0)
            sp.wait_ge(dve_step, base[key][2] + STAGE_SHAPES["norm"][2])
            sp.dma_start(out_ap[0].rearrange("(t p) d -> p t d", p=P), nat[:, :, :]).then_inc(stored, 16)
            sp.wait_ge(stored, 16)

        @block.gpsimd
        def _(pool):
            row = lambda a: a.partition_broadcast(P)
            a, w = where["ident"]
            pool.wait_ge(raw_full[1], 16)
            pool.dma_start(table[:, 0:a], consts_ap[:, 0:a]).then_inc(table_in, 16)
            pool.dma_start(table[:, a + w:], consts_ap[:, a + w:]).then_inc(table_in, 16)
            pool.dma_start(rows[:, 0, :], row(A["hgrn_norm_g"][0])).then_inc(rows_in, 16)
            pool.dma_start(rows[:, 1, :], row(A["ret_gn_g"][0])).then_inc(rows_in, 16)
            pool.dma_start(rows[:, 2, :], row(A["ret_gn_b"][0])).then_inc(rows_in, 16)
            for layer in range(DEPTH):
                pool.dma_start(lb_in[:, :, layer], A["hgrn_lb_logits"][layer].rearrange("(c p) -> p c", p=P),
                               allow_slow_non_contiguous=True).then_inc(params_in, 16)
                pool.dma_start(pool_s[:, layer, :], A["pool_scale"][layer].rearrange("(c p) -> p c", p=P),
                               allow_slow_non_contiguous=True).then_inc(params_in, 16)
            for b in range(2):
                for layer in range(DEPTH):
                    pool.dma_start(pool_w[b * HD:(b + 1) * HD, layer],
                                   A["pool_w"][layer].rearrange("(a b) i o -> b i a o", b=2)[b],
                                   ).then_inc(params_in, 16)
            pool.dma_start(fox_b[:, :, :], A["fox_f_bias"].partition_broadcast(P)).then_inc(params_in, 16)

            pool.dma_start(router[:, :, :], A["moe_router"][0].rearrange("(k p) e -> p k e", p=P)).then_inc(router_in, 16)

            def gains(src, n):
                pool.dma_start(gain_row, row(src)).then_inc(gains_in, 16)

            for layer in range(DEPTH):
                for i in range(1, NB):
                    for c in range(2):
                        for t in range(NT):
                            n = 4 * (i - 1) + 2 * c + t
                            pool.wait_ge(branch_out, 16 * layer + 4 + n + 1)
                            if i > 1:
                                pool.wait_ge(merged, 12 * layer + n - 3)
                            cs = slice(c * 512, (c + 1) * 512)
                            pool.tensor_tensor(nat[:, t, cs], nat[:, t, cs], sig[:, t, cs], ALU.add).then_inc(merged, 1)
                pool.wait_ge(merged, 12 * (layer + 1))
                gains(A["norm_ffn_g"][layer], 2 * layer + 1)
                pool.wait_ge(dve_step, base[("norm", layer, 1)][2] + STAGE_SHAPES["norm"][2])
                if layer == 0:
                    gains(A["norm_mix_g"][1], 2)
                    pool.dma_start(rows[:, 0, :], row(A["hgrn_norm_g"][1])).then_inc(rows_in, 16)
                    pool.dma_start(rows[:, 1, :], row(A["ret_gn_g"][1])).then_inc(rows_in, 16)
                    pool.dma_start(rows[:, 2, :], row(A["ret_gn_b"][1])).then_inc(rows_in, 16)
                else:
                    gains(A["final_norm_g"], 4)

        @block.tensor
        def _(pe):
            def lo_ready(u, turns):
                pe.wait_ge(lo_made, turns * RAW + (u + 1))

            def product(out, lhs, rhs, first, last):
                pe.matmul(out, lhs[0], rhs[0], start=first, stop=False)
                pe.matmul(out, lhs[0], rhs[1], start=False, stop=False)
                return pe.matmul(out, lhs[1], rhs[0], start=False, stop=last)

            def begin(key):
                i = ORDER.index(key)
                while i and ORDER[i - 1][0] in APART.get(key[0], ()):
                    i -= 1
                p, a, d = base[ORDER[i]]
                if key == ("pool_out", 0, 0):
                    pe.wait_ge(table_in, 32)
                    pe.wait_ge(params_in, 16 * N_PARAMS)
                if a:
                    pe.wait_ge(act_step, a)
                if d:
                    pe.wait_ge(dve_step, d)

            def turn(key):
                begin(key)
                for b in range(4):
                    for k in range(2):
                        for t in range(NT):
                            last = pe.transpose(PB[b][:, k * SEQ + t * P:k * SEQ + (t + 1) * P],
                                                nat[:, t, (2 * b + k) * P:(2 * b + k + 1) * P], ident)
                last.then_inc(stage_psum, 1)

            def cols(u, half, q, kind, width):
                pair = PB[2 * (q % 2):2 * (q % 2) + 2]
                lo_ready(u, 0)
                hi, lo = (col_view(w[slot_of(u)], width) for w in (w_hi, w_lo))
                for k in range(4):
                    kk = 4 * half + k
                    first, end = kk == 0, kk == KC - 1
                    h = (hT_hi[:, kk, :], hT_lo[:, kk, :])
                    n_t = {"T": 4, "M": 2, "N": 0}[kind]
                    for m in range(n_t):
                        w = tuple(x[:, k, m * P:(m + 1) * P] for x in (hi, lo))
                        last = product(pair[m // 2][:, (m % 2) * SEQ:(m % 2 + 1) * SEQ], w, h,
                                       first and m % 2 == 0, end and m % 2 == 1)
                    if kind == "T":
                        continue
                    for t in range(NT):
                        ht = tuple(x[:, t * P:(t + 1) * P] for x in h)
                        if kind == "N":
                            last = product(pair[t][:, 0:width], ht, (hi[:, k, :], lo[:, k, :]), first, end)
                        else:
                            last = product(pair[1][:, t * BW:(t + 1) * BW], ht,
                                           (hi[:, k, BW:2 * BW], lo[:, k, BW:2 * BW]),
                                           first and t == 0, end and t == 1)
                last.then_inc(unit_used, 1)

            def heads(h):
                return h // 2, (h % 2) * HD

            def values(m, v, h):
                vs = [v[:, t, h * HD:(h + 1) * HD] for t in range(NT)]
                pe.matmul(MB[2][:, h * HD:(h + 1) * HD], m[:, 0:P], vs[0], start=True, stop=True)
                pe.matmul(MB[3][:, h * HD:(h + 1) * HD], m[:, P:2 * P], vs[0], start=True, stop=False)
                return pe.matmul(MB[3][:, h * HD:(h + 1) * HD], m[:, 2 * P:3 * P], vs[1], start=False, stop=True)

            def stage(name, layer, arg):
                key = (name, layer, arg)
                if not STAGE_SHAPES[name][0]:
                    return
                begin(key)
                if name == "pool_out":
                    for c in range(2):
                        for b in range(2):
                            s = slice(b * HD, (b + 1) * HD)
                            last = pe.matmul(MB[0][s, c * SEQ:(c + 1) * SEQ], pool_w[s, layer, c, :],
                                             pool_d[s, c, :], start=True, stop=True)
                elif name == "rope":
                    pe.wait_ge(chunk_out, 15 * layer + Q_RK + 1)
                    for i, t in enumerate((rq, rk)):
                        last = pe.matmul(MB[i][:, :], T["rot"], t[:, :, :].rearrange("p c n -> p (c n)"),
                                         start=True, stop=True)
                elif name == "ret_pair":
                    for h in (2 * arg, 2 * arg + 1):
                        if arg:
                            values(score[:, h % 2, :], rv, h - 2)
                    for h in (2 * arg, 2 * arg + 1):
                        c, b = heads(h)
                        s = slice(b, b + HD)
                        bank = MB[h % 2]
                        pe.matmul(bank[:, 0:SEQ], rk[s, c, 0:P], rq[s, c, :], start=True, stop=True)
                        last = pe.matmul(bank[:, SEQ:SEQ + P], rk[s, c, P:SEQ], rq[s, c, P:SEQ], start=True, stop=True)
                elif name == "ret_last":
                    for h in (NH - 2, NH - 1):
                        last = values(score[:, h % 2, :], rv, h)
                elif name == "hgrn_last":
                    last = values(score[:, (NH - 1) % 2, :], hv, NH - 1)
                elif name == "fox_pair":
                    for h in (2 * arg, 2 * arg + 1):
                        c, b = heads(h)
                        s = slice(b, b + HD)
                        for t in range(NT):
                            n = P * (t + 1)
                            o = MB[h][:, t * P:t * P + n]
                            pe.matmul(o, fq[s, c, t * P:(t + 1) * P], fk[s, c, 0:n], start=True, stop=False)
                            for tt in range(t + 1):
                                nl = stat[:, 16 + tt * NH + h:17 + tt * NH + h].broadcast_to([P, P])
                                if tt == 0:
                                    rhs, oo = table[:, where["tri"][0]:where["tri"][0] + n], o
                                else:
                                    rhs, oo = T["tri"], o[:, P:2 * P]
                                last = pe.matmul(oo, nl, rhs, start=False, stop=tt == t)
                elif name == "fox_probs":
                    if arg:
                        for h in range(2):
                            values(fox_pT[:, h, :], fv, h)
                    for h in (2 * arg, 2 * arg + 1):
                        for i in range(3):
                            last = pe.transpose(MB[h % 2][:, i * P:(i + 1) * P], fox_p[:, h, i * P:(i + 1) * P], ident)
                elif name == "fox_last":
                    for h in (2, 3):
                        last = values(fox_pT[:, h, :], fv, h)
                elif name in ("hgrn_a", "hgrn_b"):
                    t = 0 if name == "hgrn_a" else 1
                    c, b = heads(arg)
                    s = slice(b, b + HD)
                    pe.wait_ge(chunk_out, 15 * layer + Q_HI + 1)
                    if t == 0 and arg:
                        values(score[:, (arg - 1) % 2, :], hv, arg - 1)
                    ts = slice(t * P, (t + 1) * P)
                    for i in range(8):
                        o = MB[i // 4][:, (i % 4) * P:(i % 4 + 1) * P]
                        if i < 7:
                            last = pe.matmul(o, span[s, 1 + i, ts], span[s, 1 + i, ts], start=True, stop=True)
                        else:
                            last = pe.matmul(o, hk[s, c, ts], hq[s, c, ts], start=True, stop=True)
                    if t == 1:
                        last = pe.matmul(MB[2][:, SEQ:SEQ + P], span[s, 0, 0:P], span[s, 0, P:SEQ], start=True, stop=True)
                elif name == "branch_turn":
                    for c in range(2):
                        for t in range(NT):
                            last = pe.transpose(MB[0][:, c * SEQ + t * P:c * SEQ + (t + 1) * P],
                                                o_nat[:, t, c * P:(c + 1) * P], ident)
                elif name == "router":
                    for t in range(NT):
                        for k in range(KC):
                            ts = slice(t * P, (t + 1) * P)
                            last = product(MB[0][:, t * NE:(t + 1) * NE], (hT_hi[:, k, ts], hT_lo[:, k, ts]),
                                           (router_hi[:, k, :], router_lo[:, k, :]), k == 0, k == KC - 1)
                elif name == "places":
                    m = [chosen[:, t, :] for t in range(NT)]
                    pe.matmul(MB[0][:, 0:NE], T["tri"], m[0], start=True, stop=True)
                    pe.matmul(MB[0][:, NE:2 * NE], T["ones"], m[0], start=True, stop=False)
                    pe.matmul(MB[0][:, NE:2 * NE], T["tri"], m[1], start=False, stop=True)
                    pe.matmul(MB[0][:, 2 * NE:3 * NE], T["ones"], m[0], start=True, stop=False)
                    last = pe.matmul(MB[0][:, 2 * NE:3 * NE], T["ones"], m[1], start=False, stop=True)
                last.then_inc(stage_psum, 1)

            def layer_body(layer, u0):
                turn(("turn", layer, 0))
                q = 0
                p, a, d = base[("turn", layer, 0)]
                pe.wait_ge(act_step, a + 4)
                pe.wait_ge(dve_step, d + 4)
                for u in range(N_LAYER):
                    for name, arg in PLANS[layer].get(u, []):
                        stage(name, layer, arg)
                    if u < N_MIX:
                        if u % 2 == 0:
                            if u >= 4:
                                pe.wait_ge(chunk_out, 15 * layer + q - 1)
                        cols(u0 + u, u % 2, q, MIX_CHUNKS[q][2], MIX_CHUNKS[q][1])
                        q += u % 2
                    elif u < N_LAYER - 4:
                        i, r = divmod(u - N_MIX, 5)
                        if r < 4:
                            if r % 2 == 0:
                                pe.wait_ge(chunk_out, 15 * layer + q - 1)
                                if i:
                                    pe.wait_ge(branch_out, 16 * layer + 4 * (i - 1) + (2 if r == 0 else 4))
                            cols(u0 + u, r % 2, q, "N", 512)
                            q += r % 2
                        else:
                            turned = ("pool_out", layer, 0) if BRANCHES[i] == 2 else ("branch_turn", layer, BRANCHES[i])
                            pe.wait_ge(act_step, base[turned][1] + 1)
                            pe.wait_ge(dve_step, base[turned][2] + 1)
                            lo_ready(u0 + u, 0)
                            hi, lo = (row_view(w[slot_of(u0 + u)]) for w in (w_hi, w_lo))
                            for c in range(2):
                                pe.wait_ge(chunk_out, 15 * layer + q - 1 + c)
                                for t in range(NT):
                                    for k in range(2):
                                        ts, cs = slice(t * P, (t + 1) * P), slice(c * 512, (c + 1) * 512)
                                        last = product(gate_bank(c, t)[:, :],
                                                       (oT_hi[i % 2][:, k, ts], oT_lo[i % 2][:, k, ts]),
                                                       (hi[:, k, cs], lo[:, k, cs]), k == 0, k == 1)
                                    if (c, t) != (1, 1):
                                        last.then_inc(branch_done, 1)
                            last.then_inc(unit_used, 1)
                    else:
                        c, half = divmod(u - (N_LAYER - 4), 2)
                        if (c, half) == (0, 0):
                            pe.wait_ge(merged, 12 * (layer + 1))
                            turn(("turn", layer, 1))
                            p, a, d = base[("turn", layer, 1)]
                            pe.wait_ge(act_step, a + 4)
                            pe.wait_ge(dve_step, d + 4)
                        lo_ready(u0 + u, 0)
                        hi, lo = (col_view(w[slot_of(u0 + u)], 512) for w in (w_hi, w_lo))
                        for k in range(4):
                            kk = 4 * half + k
                            for t in range(NT):
                                ts = slice(t * P, (t + 1) * P)
                                last = product(PB[2 * c + t][:, :], (hT_hi[:, kk, ts], hT_lo[:, kk, ts]),
                                               (hi[:, k, :], lo[:, k, :]), kk == 0, kk == KC - 1)
                        last.then_inc(unit_used, 1)
                turn(("turn", layer, 2))
                p, a, d = base[("turn", layer, 2)]
                pe.wait_ge(act_step, a + 4)
                pe.wait_ge(dve_step, d + 4)

            def wide(u, turns, bank0, src, tiles):
                for half in range(2):
                    lo_ready(u + half, turns)
                    hi, lo = (col_view(w[slot_of(u + half)], FCH) for w in (w_hi, w_lo))
                    for k in range(4):
                        kk = 4 * half + k
                        for t in range(tiles):
                            ts = slice(t * P, (t + 1) * P)
                            last = product(PB[bank0 + t][:, :], (src[0][:, kk, ts], src[1][:, kk, ts]),
                                           (hi[:, k, :], lo[:, k, :]), kk == 0, kk == KC - 1)
                    last.then_inc(unit_used, 1)

            def down(u, turns, c, tiles, final):
                pe.wait_ge(aT_lo_made, c + 1)
                for i in range(2):
                    lo_ready(u + i, turns)
                    hi, lo = (row_view(w[slot_of(u + i)]) for w in (w_hi, w_lo))
                    for k in range(2):
                        for t in range(tiles):
                            ts = slice(t * P, (t + 1) * P)
                            for cc in range(2):
                                cs = slice(cc * 512, (cc + 1) * 512)
                                last = product(MB[2 * t + cc][:, :], (aT_hi[:, 2 * i + k, ts], aT_lo[:, 2 * i + k, ts]),
                                               (hi[:, k, cs], lo[:, k, cs]), False,
                                               final and i == 1 and k == 1)
                    last.then_inc(unit_used, 1)
                return last

            def turn_act(c, tiles):
                pe.wait_ge(act_made, c + 1)
                for t in range(tiles):
                    for b in range(FB):
                        last = pe.transpose(PB[2 + t][:, b * P:(b + 1) * P], act[:, t, b * P:(b + 1) * P], ident)
                last.then_inc(act_turned, 1)

            def clear(tiles):
                for t in range(tiles):
                    for cc in range(2):
                        pe.matmul(MB[2 * t + cc][:, :], zeros_r[:, :],
                                  hT_hi[:, 0:2, :].rearrange("p a b -> p (a b)"), start=True, stop=False)

            def ffn_loop(u0, turns, c0, src, tiles):
                with pe.Fori(1, NF) as j:
                    o = turns + (j - 1)
                    c = c0 + j
                    pe.wait_ge(silu_made, c)
                    wide(u0 + 4, o, 0, src, tiles)
                    pe.wait_ge(aT_lo_made, c)
                    wide(u0 + 6, o, 2, src, tiles)
                    down(u0 + 8, o, c - 1, tiles, False)
                    turn_act(c, tiles)

            def dense():
                clear(NT)
                wide(FFN0, 0, 0, (hT_hi, hT_lo), NT)
                wide(FFN0 + 2, 0, 2, (hT_hi, hT_lo), NT)
                turn_act(0, NT)
                ffn_loop(FFN0, 0, 0, (hT_hi, hT_lo), NT)
                down(FFN0 + 40, 0, NF - 1, NT, True)

            def gather(job):
                pe.wait_ge(picked, job + 1)
                for k in range(KC):
                    o = MB[2 + k // 4][:, (k % 4) * P:(k % 4 + 1) * P]
                    ks = slice(k * P, (k + 1) * P)
                    for t in range(NT):
                        pe.matmul(o, h_hi[:, t, ks], pick[:, t, :], start=t == 0, stop=False)
                        last = pe.matmul(o, h_lo[:, t, ks], pick[:, t, :], start=False, stop=t == NT - 1)
                last.then_inc(gathered, 1)

            def turn_back(n):
                pe.wait_ge(back_picked, n + 1)
                for t in range(NT):
                    last = pe.transpose(PB[3][:, t * P:(t + 1) * P], pick_back[:, t, :], ident)
                last.then_inc(back_turned, 1)

            def scatter(n):
                pe.wait_ge(pickT_made, n + 1)
                pe.wait_ge(y_lo_made, n + 1)
                for t in range(NT):
                    for c in range(2):
                        bank = (MB[2 + c], PB[1 + 2 * c])[t]
                        cs = slice(c * 512, (c + 1) * 512)
                        pe.matmul(bank[:, :], pickT[:, t * P:(t + 1) * P], y_hi[:, cs], start=True, stop=False)
                        last = pe.matmul(bank[:, :], pickT[:, t * P:(t + 1) * P], y_lo[:, cs], start=False, stop=True)
                last.then_inc(scattered, 1)

            pe.wait_ge(ident_in, 16)
            layer_body(0, 0)
            pe.wait_ge(zeroed, 1)
            dense()
            layer_body(1, LAYER1)
            stage("router", 1, 0)
            stage("places", 1, 0)
            pe.wait_ge(dve_step, base[("places", 1, 0)][2] + STAGE_SHAPES["places"][2])
            n_pass = pe.value_load(passes[0:1, 0:1], min_val=1, max_val=2)
            pe.wait_ge(h_split, 1)
            gather(0)
            with pe.Fori(0, n_pass) as ps:
                with pe.Fori(0, NE) as e:
                    job = ps * NE + e
                    src = (e_hi, e_lo)
                    pe.wait_ge(gather_hi, job + 1)
                    pe.wait_ge(gather_lo, job + 1)
                    wide(MOE0, job * NF, 0, src, 1)
                    turn_back(job)
                    wide(MOE0 + 2, job * NF, 2, src, 1)
                    scatter(job)
                    clear(1)
                    turn_act(NF + job * NF, 1)
                    ffn_loop(MOE0, job * NF, NF + job * NF, src, 1)
                    pe.wait_ge(moe_added, job + 1)
                    gather(job + 1)
                    down(MOE0 + 40, job * NF, NF + job * NF + (NF - 1), 1, True)
            turn_back(n_pass * NE)
            scatter(n_pass * NE)

        @block.scalar
        def _(act_e):
            def convert(u, turns):
                act_e.wait_ge(raw_full[u % RAW], turns * 16 + (u // RAW + 1) * 16)
                if u >= RING:
                    act_e.wait_ge(unit_used, turns * RAW + (u - RING + 1))
                n = size_of(u)
                act_e.activation(w_hi[slot_of(u)][:, 0:n], raw[u % RAW][:, 0:n], ACT.Copy).then_inc(hi_made, 1)

            def turn(key):
                p, a, d = base[key]
                act_e.wait_ge(stage_psum, p + 1)
                for b in range(4):
                    act_e.activation(hT_hi[:, 2 * b:2 * b + 2, :].rearrange("p k n -> p (k n)"), PB[b][:, :],
                                     ACT.Copy).then_inc(act_step, 1)

            def take_chunk(q, u, layer):
                pair = PB[2 * (q % 2):2 * (q % 2) + 2]
                flat = lambda t: t[:, :, :].rearrange("p c n -> p (c n)")
                act_e.wait_ge(unit_used, u + 1)
                copy = lambda o, i, f=ACT.Copy, **kw: act_e.activation(o, i, f, **kw)
                if layer and q == 0:
                    act_e.wait_ge(ffn_added, 4)
                if q == Q_PU:
                    copy(upad[:, :, 16:16 + SEQ], pair[0][:, :].rearrange("p (c n) -> p c n", c=2))
                    last = copy(flat(rq), pair[1][:, :])
                elif q == Q_RK:
                    copy(flat(rk), pair[0][:, :], scale=HD ** -0.5)
                    last = copy(flat(rv), pair[1][:, :])
                elif q == Q_RG:
                    for t in range(NT):
                        last = copy(rg[:, t, :], pair[t][:, 0:BW], ACT.Silu)
                elif q == Q_FQ:
                    copy(flat(fq), pair[0][:, :], scale=HD ** -0.5)
                    last = copy(flat(fk), pair[1][:, :])
                elif q == Q_FV:
                    for t in range(NT):
                        last = copy(fv[:, t, :], pair[t][:, 0:BW + NH])
                elif q == Q_HQ:
                    copy(flat(hq), pair[0][:, :])
                    copy(flat(hf), pair[1][:, :], ACT.Sigmoid)
                    last = copy(flat(hk), pair[1][:, :], ACT.Sigmoid, scale=-1.0)
                elif q == Q_HI:
                    for t in range(NT):
                        copy(hv[:, t, :], pair[t][:, 0:BW])
                    for t in range(NT):
                        last = copy(hg[:, t, :], pair[t][:, BW:2 * BW], ACT.Silu)
                else:
                    i, c = divmod(q - 7, 2)
                    if c == 0 and i:
                        if i == 1:
                            act_e.wait_ge(branch_out, 16 * layer + 4)
                        else:
                            act_e.wait_ge(merged, 12 * layer + 4 * (i - 1))
                    for t in range(NT):
                        last = copy(sig[:, t, c * 512:(c + 1) * 512], pair[t][:, :], ACT.Sigmoid)
                last.then_inc(chunk_out, 1)

            def stage(name, layer, arg):
                p, a, d = base[(name, layer, arg)]
                if STAGE_SHAPES[name][1] == 0:
                    return
                dve = lambda n: act_e.wait_ge(dve_step, d + n)
                psum = lambda: act_e.wait_ge(stage_psum, p + 1)
                done = lambda ins: ins.then_inc(act_step, 1)
                if name == "bounds":
                    dve(2)
                    done(act_e.activation(lower1[:, 0:4], lower1[:, 4:8], ACT.Exp))
                elif name == "norm":
                    dve(3)
                    done(act_e.activation(stat[:, 2:4], stat[:, 2:4], ACT.Sqrt))
                elif name == "pool_out":
                    psum()
                    for c in range(2):
                        last = act_e.activation(oT_hi[0][:, c, :], MB[0][:, c * SEQ:(c + 1) * SEQ], ACT.Copy,
                                                scale=pool_s[:, layer, c:c + 1])
                    done(last)
                elif name in ("ret_last", "hgrn_last"):
                    psum()
                    if name == "hgrn_last":
                        act_e.wait_ge(stage_psum, base[("branch_turn", layer, 1)][0] + 1)
                    for t in range(NT):
                        last = act_e.activation(o_nat[:, t, :], MB[2 + t][:, 0:BW], ACT.Copy)
                    done(last)
                elif name == "ret_norm":
                    dve(6)
                    done(act_e.activation(stat[:, 32:40], stat[:, 32:40], ACT.Sqrt))
                elif name == "hgrn_norm":
                    dve(3)
                    done(act_e.activation(stat[:, 32:40], stat[:, 32:40], ACT.Sqrt))
                elif name == "fox_log":
                    dve(1)
                    done(act_e.activation(stat[:, 48:56], stat[:, 40:48], ACT.Abs))
                    act_e.wait_ge(act_step, a + 1)
                    done(act_e.activation(stat[:, 48:56], stat[:, 48:56], ACT.Exp, scale=-1.0))
                    dve(2)
                    done(act_e.activation(stat[:, 48:56], stat[:, 48:56], ACT.Ln))
                elif name == "fox_pair":
                    for i in range(2):
                        h = 2 * arg + i
                        dve(3 * (i + 1))
                        for t in range(NT):
                            cs = slice(0, P) if t == 0 else slice(P, 3 * P)
                            g = 2 * h + t
                            done(act_e.activation(fox_p[:, h, cs], fox_p[:, h, cs], ACT.Exp,
                                                  bias=stat[:, 64 + g:65 + g], accum_out=stat[:, 72 + g:73 + g]))
                elif name == "fox_probs":
                    psum()
                    for h in (2 * arg, 2 * arg + 1):
                        done(act_e.activation(fox_pT[:, h, :], MB[h % 2][:, 0:384], ACT.Copy))
                elif name == "hgrn_ln":
                    act_e.wait_ge(dve_step, base[("hgrn_log", layer, 0)][2] + 5)
                    done(act_e.activation(hf[:, :, :].rearrange("p c n -> p (c n)"),
                                          hf[:, :, :].rearrange("p c n -> p (c n)"), ACT.Ln))
                elif name == "hgrn_exp":
                    act_e.wait_ge(dve_step, base[("hgrn_exponents", layer, arg)][2] + 14)
                    done(act_e.activation(span[:, :, :].rearrange("p l n -> p (l n)"),
                                          span[:, :, :].rearrange("p l n -> p (l n)"), ACT.Exp))
                elif name == "branch_turn":
                    psum()
                    i = BRANCHES.index(arg)
                    if i >= 2:
                        act_e.wait_ge(unit_used, (0, LAYER1)[layer] + N_MIX + 5 * (i - 2) + 5)
                    done(act_e.activation(oT_hi[i % 2][:, :, :].rearrange("p c n -> p (c n)"), MB[0][:, :], ACT.Copy))
                elif name == "gates":
                    dve(8)
                    done(act_e.activation(stat[:, 8:10], stat[:, 8:10], ACT.Exp))
                    for t in range(NT):
                        last = act_e.activation(h_hi[:, t, :], nat[:, t, :], ACT.Copy)
                    done(last)

            def layer_points(layer, u0):
                q = 0
                for u in range(N_LAYER):
                    if 0 < u <= N_MIX and u % 2 == 0:
                        take_chunk(q, u0 + u - 1, layer)
                        q += 1
                    elif u > N_MIX and (u - N_MIX) % 5 in (2, 4) and u < N_LAYER - 4:
                        take_chunk(q, u0 + u - 1, layer)
                        q += 1
                    for name, arg in PLANS[layer].get(u, []):
                        stage(name, layer, arg)
                    if u == N_LAYER - 4:
                        turn(("turn", layer, 1))
                    convert(u0 + u + AHEAD, 0)

            def take_silu(u, turns, c, tiles):
                act_e.wait_ge(unit_used, turns * RAW + (u + 1))
                if not (isinstance(c, int) and c == 0):
                    act_e.wait_ge(act_made, c)
                for t in range(tiles):
                    last = act_e.activation(silu_g[:, t, :], PB[t][:, :], ACT.Silu)
                last.then_inc(silu_made, 1)

            def take_turned(c, tiles):
                act_e.wait_ge(act_turned, c + 1)
                for t in range(tiles):
                    last = act_e.activation(aT_hi[:, :, t * P:(t + 1) * P],
                                            PB[2 + t][:, :].rearrange("p (b n) -> p b n", b=FB), ACT.Copy)
                last.then_inc(aT_hi_made, 1)

            def ffn_points(u0, turns, c0, tiles, first=None, third=None, late=None):
                ahead = lambda u, o: convert(u + AHEAD, o)
                if first:
                    first()
                ahead(u0, turns)
                ahead(u0 + 1, turns)
                if third:
                    third()
                take_silu(u0 + 1, turns, c0, tiles)
                ahead(u0 + 2, turns)
                ahead(u0 + 3, turns)
                take_turned(c0, tiles)
                with act_e.Fori(1, NF) as j:
                    o = turns + (j - 1)
                    c = c0 + j
                    ahead(u0 + 4, o)
                    ahead(u0 + 5, o)
                    take_silu(u0 + 5, o, c, tiles)
                    for i in range(6, 10):
                        ahead(u0 + i, o)
                    take_turned(c, tiles)
                if late:
                    late()
                ahead(u0 + 40, turns)
                ahead(u0 + 41, turns)

            stage("norm", 0, 0)
            convert(0, 0)
            turn(("turn", 0, 0))
            convert(1, 0)
            layer_points(0, 0)
            stage("norm", 0, 1)
            turn(("turn", 0, 2))
            ffn_points(FFN0, 0, 0, NT)
            stage("norm", 1, 0)
            turn(("turn", 1, 0))
            layer_points(1, LAYER1)
            stage("norm", 1, 1)
            turn(("turn", 1, 2))
            stage("gates", 1, 0)
            act_e.wait_ge(dve_step, base[("places", 1, 0)][2] + STAGE_SHAPES["places"][2])
            n_pass = act_e.value_load(passes[0:1, 0:1], min_val=1, max_val=2)

            def take_gathered(job):
                act_e.wait_ge(gathered, job + 1)
                for b in range(2):
                    last = act_e.activation(e_hi[:, 4 * b:4 * b + 4, :].rearrange("p k n -> p (k n)"),
                                            MB[2 + b][:, :], ACT.Copy)
                last.then_inc(gather_hi, 1)

            def take_y(n):
                act_e.wait_ge(unit_used, n * N_FFN + MOE0)
                for c in range(2):
                    last = act_e.activation(y_hi[:, c * 512:(c + 1) * 512], MB[c][:, :], ACT.Copy)
                last.then_inc(y_hi_made, 1)

            def take_back(n):
                act_e.wait_ge(back_turned, n + 1)
                act_e.activation(pickT[:, :], PB[3][:, 0:SEQ], ACT.Copy).then_inc(pickT_made, 1)

            take_gathered(0)
            with act_e.Fori(0, n_pass) as ps:
                with act_e.Fori(0, NE) as e:
                    job = ps * NE + e
                    ffn_points(MOE0, job * NF, NF + job * NF, 1, lambda: take_y(job), lambda: take_back(job),
                               lambda: take_gathered(job + 1))
            take_y(n_pass * NE)
            take_back(n_pass * NE)
            stage("norm", DEPTH, 0)

        @block.vector
        def _(dve):
            v = nc.vector
            count = [0]

            def inc(instruction):
                count[0] += 1
                return instruction.then_inc(dve_step, 1)

            def link(instruction):
                inc(instruction)
                dve.wait_ge(dve_step, count[0])

            def end(key):
                want = base[key][2] + STAGE_SHAPES[key[0]][2]
                assert count[0] == want, (key, count[0] - base[key][2])

            def convert(u, turns):
                dve.wait_ge(hi_made, turns * RAW + (u + 1))
                if u >= RING:
                    dve.wait_ge(unit_used, turns * RAW + (u - RING + 1))
                n = size_of(u)
                v.tensor_tensor(w_lo[slot_of(u)][:, 0:n], raw[u % RAW][:, 0:n], w_hi[slot_of(u)][:, 0:n].bitcast(F32),
                                ALU.subtract).then_inc(lo_made, 1)

            def rest(lo, src, hi):
                return v.tensor_tensor(lo, src, hi.bitcast(F32), ALU.subtract)

            def turn(key):
                p, a, d = base[key]
                for b in range(4):
                    dve.wait_ge(act_step, a + b + 1)
                    f = lambda t: t[:, 2 * b:2 * b + 2, :].rearrange("p k n -> p (k n)")
                    inc(rest(f(hT_lo), PB[b][:, :], f(hT_hi)))
                end(key)

            def norm(layer, i):
                key = ("norm", layer, i)
                p, a, d = base[key]
                n = 2 * layer + i
                if n == 0:
                    dve.wait_ge(x_in, 16)
                if d:
                    dve.wait_ge(dve_step, d)
                for t in range(NT):
                    inc(v.scalar_tensor_tensor(out=nat[:, t, :], in0=x[:, t, :], scalar=1.0, in1=x[:, t, :],
                                               op0=ALU.mult, op1=ALU.mult, accum_out=stat[:, t:t + 1]))
                dve.wait_ge(dve_step, count[0])
                link(v.tensor_scalar(stat[:, 2:4], stat[:, 0:2], 1.0 / DM, RMS_EPS, ALU.mult, ALU.add))
                dve.wait_ge(act_step, a + 1)
                link(v.reciprocal(stat[:, 4:6], stat[:, 2:4]))
                if n:
                    dve.wait_ge(gains_in, 16 * n)
                else:
                    dve.wait_ge(first_gains_in, 16)
                for t in range(NT):
                    link(v.scalar_tensor_tensor(out=nat[:, t, :], in0=x[:, t, :], scalar=stat[:, 4 + t:5 + t],
                                                in1=gain_row, op0=ALU.mult, op1=ALU.mult))
                end(key)

            def head_norm(key, center):
                p, a, d = base[key]
                before = base[("ret_last" if center else "hgrn_last", key[1], 0)]
                dve.wait_ge(act_step, before[1] + 1)
                o3 = o_nat[:, :, :].rearrange("p t (h d) -> p (t h) d", d=HD)
                sq3 = square.rearrange("p (g d) -> p g d", d=HD)
                eps = RMS_EPS
                if center:
                    eps = LN_EPS
                    link(v.tensor_reduce(stat[:, 32:40], o3, axis=AX.X, op=ALU.add))
                    link(v.tensor_scalar(stat[:, 32:40], stat[:, 32:40], 1.0 / HD, None, ALU.mult))
                    link(v.tensor_tensor(o3, o3, broadcast(stat[:, 32:40], HD), ALU.subtract))
                link(v.tensor_tensor(sq3, o3, o3, ALU.mult))
                link(v.tensor_reduce(stat[:, 32:40], sq3, axis=AX.X, op=ALU.add))
                link(v.tensor_scalar(stat[:, 32:40], stat[:, 32:40], 1.0 / HD, eps, ALU.mult, ALU.add))
                dve.wait_ge(act_step, a + 1)
                link(v.reciprocal(stat[:, 32:40], stat[:, 32:40]))
                link(v.tensor_tensor(o3, o3, broadcast(stat[:, 32:40], HD), ALU.mult))
                row = lambda i: rows[:, i:i + 1, :].broadcast_to([P, NT, BW])
                dve.wait_ge(rows_in, 48 * (key[1] + 1))
                link(v.tensor_tensor(o_nat[:, :, :], o_nat[:, :, :], row(1 if center else 0), ALU.mult))
                if center:
                    link(v.tensor_tensor(o_nat[:, :, :], o_nat[:, :, :], row(2), ALU.add))
                g = rg if center else hg
                dve.wait_ge(chunk_out, 15 * key[1] + (Q_RG if center else Q_HI) + 1)
                link(v.tensor_tensor(o_nat[:, :, :], o_nat[:, :, :], g[:, :, :], ALU.mult))

            def stage(name, layer, arg):
                key = (name, layer, arg)
                p, a, d = base[key]
                assert count[0] == d, key
                if STAGE_SHAPES[name][2] == 0:
                    return
                if d:
                    dve.wait_ge(dve_step, d)
                chunk = lambda q: dve.wait_ge(chunk_out, 15 * layer + q + 1)
                psum = lambda: dve.wait_ge(stage_psum, p + 1)
                if name == "bounds":
                    dve.wait_ge(params_in, 16 * N_PARAMS)
                    l0, l1 = lb_in[:, :, 0], lb_in[:, :, 1]
                    link(v.tensor_tensor(lower1[:, 0:2], l0, l1, ALU.max))
                    top2 = lower1[:, 0:2]
                    both = lower1[:, 4:8].rearrange("p (l c) -> p l c", l=2)
                    v.tensor_tensor(both[:, 0, :], l0, top2, ALU.subtract)
                    inc(v.tensor_tensor(both[:, 1, :], l1, top2, ALU.subtract))
                    dve.wait_ge(act_step, a + 1)
                    link(v.tensor_tensor(lower1[:, 4:6], lower1[:, 0:2], lower1[:, 2:4], ALU.add))
                    link(v.reciprocal(lower1[:, 4:6], lower1[:, 4:6]))
                    link(v.tensor_tensor(lower1[:, 0:2], lower1[:, 0:2], lower1[:, 4:6], ALU.mult))
                    link(v.tensor_tensor(lower1[:, 2:4], lower1[:, 2:4], lower1[:, 4:6], ALU.mult))
                    link(v.tensor_tensor(lower1[:, 4:6], lower1[:, 0:2], lower1[:, 2:4], ALU.add))
                    v.tensor_tensor(lower[:, 0, :], lower1[:, 0:2], lower1[:, 0:2], ALU.subtract)
                    link(v.tensor_tensor(lower[:, 1, :], lower1[:, 4:6], lower1[:, 0:2], ALU.subtract))
                    link(v.tensor_scalar(upper[:, :, :], lower[:, :, :], -1.0, 1.0, ALU.mult, ALU.add))
                elif name == "pool_means":
                    chunk(Q_PU)
                    s2, s4 = pool_sum
                    inc(v.memset(upad[:, :, 0:16], 0.0))
                    dve.wait_ge(dve_step, count[0])
                    link(v.tensor_tensor(s2[:, :, 1:272], upad[:, :, 1:272], upad[:, :, 0:271], ALU.add))
                    link(v.tensor_tensor(s4[:, :, 3:272], s2[:, :, 3:272], s2[:, :, 1:270], ALU.add))
                    link(v.tensor_tensor(s2[:, 1, 7:272], s4[:, 1, 7:272], s4[:, 1, 3:268], ALU.add))
                    link(v.tensor_tensor(s4[64:128, 1, 15:272], s2[64:128, 1, 15:272], s2[64:128, 1, 7:264], ALU.add))
                    heads_tab = T["win_head"].rearrange("p (c n) -> p c n", c=2)
                    for c in range(2):
                        for b, s in ((0, s2), (1, s4)):
                            ps = slice(64 * b, 64 * b + 64)
                            link(v.tensor_tensor(s[ps, c, 16:32], s[ps, c, 16:32], heads_tab[ps, c, :], ALU.mult))
                            inc(v.scalar_tensor_tensor(out=pool_d[ps, c, :], in0=s[ps, c, 16:272],
                                                       scalar=T["inv_win"][ps, c:c + 1], in1=upad[ps, c, 16:272],
                                                       op0=ALU.mult, op1=ALU.subtract))
                elif name == "pool_out":
                    dve.wait_ge(act_step, a + 1)
                    for c in range(2):
                        last = v.scalar_tensor_tensor(out=oT_lo[0][:, c, :], in0=MB[0][:, c * SEQ:(c + 1) * SEQ],
                                                      scalar=pool_s[:, layer, c:c + 1],
                                                      in1=oT_hi[0][:, c, :].bitcast(F32), op0=ALU.mult, op1=ALU.subtract)
                    inc(last)
                elif name == "rope":
                    psum()
                    tmp = o_nat[:, :, :]
                    tab = lambda n: T[n].unsqueeze(1).broadcast_to([P, 2, SEQ])
                    for i, t in enumerate((rq, rk)):
                        link(v.tensor_tensor(tmp, MB[i][:, :].rearrange("p (c n) -> p c n", c=2), tab("sin"), ALU.mult))
                        link(v.tensor_tensor(t[:, :, :], t[:, :, :], tab("cos"), ALU.mult))
                        link(v.tensor_tensor(t[:, :, :], t[:, :, :], tmp, ALU.add))
                elif name == "ret_pair":
                    psum()
                    for h in (2 * arg, 2 * arg + 1):
                        dec = T["decay"][:, h * SEQ:(h + 1) * SEQ]
                        bank = MB[h % 2]
                        inc(v.tensor_tensor(score[:, h % 2, 0:SEQ], bank[:, 0:SEQ], dec, ALU.mult))
                        inc(v.tensor_tensor(score[:, h % 2, SEQ:384], bank[:, SEQ:384], dec[:, 0:P], ALU.mult))
                elif name == "ret_norm":
                    head_norm(key, True)
                elif name == "hgrn_norm":
                    head_norm(key, False)
                elif name == "fox_log":
                    chunk(Q_FV)
                    z3 = stat[:, 40:48].rearrange("p (t h) -> p t h", t=NT)
                    link(v.tensor_tensor(z3, fv[:, :, BW:BW + NH],
                                         fox_b[:, layer:layer + 1, :].broadcast_to([P, NT, NH]), ALU.add))
                    dve.wait_ge(act_step, a + 2)
                    link(v.tensor_scalar(stat[:, 48:56], stat[:, 48:56], 1.0, None, ALU.add))
                    link(v.tensor_scalar(stat[:, 40:48], stat[:, 40:48], 0.0, None, ALU.min))
                    dve.wait_ge(act_step, a + 3)
                    inc(v.tensor_tensor(stat[:, 16:24], stat[:, 48:56], stat[:, 40:48], ALU.subtract))
                elif name == "fox_pair":
                    psum()
                    for h in (2 * arg, 2 * arg + 1):
                        link(v.tensor_tensor(fox_p[:, h, :], MB[h][:, 0:384], T["causal"], ALU.add))
                        g = 64 + 2 * h
                        inc(v.tensor_reduce(stat[:, g:g + 1], fox_p[:, h, 0:P], axis=AX.X, op=ALU.max, negate=True))
                        inc(v.tensor_reduce(stat[:, g + 1:g + 2], fox_p[:, h, P:384], axis=AX.X, op=ALU.max,
                                            negate=True))
                    dve.wait_ge(act_step, a + 4)
                    g = 72 + 4 * arg
                    inc(v.reciprocal(stat[:, g + 8:g + 12], stat[:, g:g + 4]))
                elif name == "fox_last":
                    psum()
                    one_over = stat[:, 80:88].rearrange("p (h t) -> p t h", t=NT)
                    for t in range(NT):
                        inc(v.tensor_tensor(o_nat[:, t, :].rearrange("p (h d) -> p h d", d=HD),
                                            MB[2 + t][:, 0:BW].rearrange("p (h d) -> p h d", d=HD),
                                            broadcast(one_over[:, t, :], HD), ALU.mult))
                elif name == "hgrn_log":
                    chunk(Q_HQ)
                    for c in range(2):
                        inc(v.tensor_scalar(hf[:, c, :], hf[:, c, :], upper[:, layer, c:c + 1],
                                            lower[:, layer, c:c + 1], ALU.mult, ALU.add))
                        inc(v.tensor_scalar(hk[:, c, :], hk[:, c, :], upper[:, layer, c:c + 1], None, ALU.mult))
                    dve.wait_ge(dve_step, count[0])
                    inc(v.tensor_scalar(hf[:, :, :], hf[:, :, :], TINY, None, ALU.max))
                elif name == "hgrn_scan":
                    dve.wait_ge(act_step, base[("hgrn_ln", layer, 0)][1] + 1)
                    for c in range(2):
                        for n in range(NCH):
                            s = slice(n * CH, (n + 1) * CH)
                            inc(v.tensor_tensor_scan(hf[:, c, s], T["ones"][:, 0:CH], hf[:, c, s], 0.0,
                                                     ALU.mult, ALU.add))
                elif name == "hgrn_exponents":
                    c = arg
                    if c == 0:
                        dve.wait_ge(stage_psum, base[("fox_last", layer, 0)][0] + 1)
                    else:
                        dve.wait_ge(stage_psum, base[("hgrn_b", layer, 1)][0] + 1)
                    lg = hf[:, c, :]
                    for i, b in enumerate(LEVELS[1:]):
                        h = b // 2
                        src = lg.rearrange("p (n b) -> p n b", b=b)
                        dst = span[:, 2 + i, :].rearrange("p (n b) -> p n b", b=b)
                        mid = src[:, :, h - 1:h].broadcast_to([P, SEQ // b, h])
                        inc(v.tensor_tensor(dst[:, :, h:b], src[:, :, h:b], mid, ALU.subtract))
                        inc(v.tensor_tensor(dst[:, :, 0:h], mid, src[:, :, 0:h], ALU.subtract))
                    src = lg.rearrange("p (g n b) -> p g n b", n=2, b=CH)
                    dst = span[:, 1, :].rearrange("p (g n b) -> p g n b", n=2, b=CH)
                    v.tensor_copy(dst[:, :, 1, :], src[:, :, 1, :])
                    link(v.tensor_tensor(dst[:, :, 0, :], src[:, :, 0, CH - 1:CH].broadcast_to([P, 2, CH]),
                                         src[:, :, 0, :], ALU.subtract))
                    last_of = lambda n: lg[:, n * CH + CH - 1:n * CH + CH]
                    sl = lambda n: slice(n * CH, (n + 1) * CH)
                    v.tensor_scalar(span[:, 0, sl(0)], span[:, 1, sl(0)], last_of(1), None, ALU.add)
                    v.tensor_tensor(span[:, 0, sl(1)], last_of(1).broadcast_to([P, CH]), lg[:, sl(1)], ALU.subtract)
                    v.tensor_copy(span[:, 0, sl(2)], lg[:, sl(2)])
                    inc(v.tensor_scalar(span[:, 0, sl(3)], lg[:, sl(3)], last_of(2), None, ALU.add))
                elif name == "hgrn_span":
                    c = arg
                    dve.wait_ge(act_step, base[("hgrn_exp", layer, c)][1] + 1)
                    for lev, b in enumerate([256] + LEVELS):
                        h = b // 2
                        e = span[:, lev, :].rearrange("p (n b) -> p n b", b=b)
                        q = hq[:, c, :].rearrange("p (n b) -> p n b", b=b)
                        k = hk[:, c, :].rearrange("p (n b) -> p n b", b=b)
                        inc(v.tensor_tensor(e[:, :, h:b], e[:, :, h:b], q[:, :, h:b], ALU.mult))
                        inc(v.tensor_tensor(e[:, :, 0:h], e[:, :, 0:h], k[:, :, 0:h], ALU.mult))
                elif name in ("hgrn_a", "hgrn_b"):
                    psum()
                    t = 0 if name == "hgrn_a" else 1
                    mk = T["masks"]
                    inc(v.tensor_tensor(masked[:, 0:4, :].rearrange("p l n -> p (l n)"), MB[0][:, :],
                                        table[:, where["masks"][0]:where["masks"][0] + 512], ALU.mult))
                    link(v.tensor_tensor(masked[:, 4:8, :].rearrange("p l n -> p (l n)"), MB[1][:, :],
                                         table[:, where["masks"][0] + 512:where["masks"][0] + 1024], ALU.mult))
                    if t == 1:
                        v.tensor_copy(score[:, arg % 2, P:2 * P], MB[2][:, SEQ:SEQ + P])
                    inc(v.tensor_reduce(score[:, arg % 2, t * SEQ:t * SEQ + P],
                                        masked[:, :, :].rearrange("p l n -> p n l"), axis=AX.X, op=ALU.add))
                    dve.wait_ge(dve_step, count[0])
                elif name == "branch_turn":
                    dve.wait_ge(act_step, a + 1)
                    i = BRANCHES.index(arg)
                    flat = lambda t: t[:, :, :].rearrange("p c n -> p (c n)")
                    inc(rest(flat(oT_lo[i % 2]), MB[0][:, :], flat(oT_hi[i % 2])))
                elif name == "split_router":
                    dve.wait_ge(router_in, 16)
                    link(v.tensor_copy(router_hi[:, :, :], router[:, :, :]))
                    inc(rest(router_lo[:, :, :], router[:, :, :], router_hi[:, :, :]))
                elif name == "router":
                    psum()
                    inc(v.tensor_copy(logit[:, :, :].rearrange("p t e -> p (t e)"), MB[0][:, 0:NT * NE]))
                    dve.wait_ge(dve_step, count[0])
                elif name == "gates":
                    for t in range(NT):
                        inc(v.max(top[:, t, :], logit[:, t, :]))
                    dve.wait_ge(dve_step, count[0])
                    for t in range(NT):
                        inc(v.max_index(top_at[:, t, :], top[:, t, :], logit[:, t, :]))
                    dve.wait_ge(dve_step, count[0])
                    link(v.tensor_copy(top_f[:, :, :], top_at[:, :, :]))
                    iota8 = T["iota"][:, 0:NE]
                    for r in range(2):
                        for t in range(NT):
                            v_ = v.tensor_scalar(hot[:, r, t, :], iota8, top_f[:, t, r:r + 1], None, ALU.is_equal)
                        inc(v_)
                    link(v.tensor_tensor(stat[:, 8:10], top[:, :, 1], top[:, :, 0], ALU.subtract))
                    dve.wait_ge(act_step, a + 1)
                    link(v.tensor_scalar(stat[:, 10:12], stat[:, 8:10], 1.0, None, ALU.add))
                    link(v.reciprocal(weight[:, 0, :], stat[:, 10:12]))
                    link(v.tensor_tensor(weight[:, 1, :], weight[:, 0, :], stat[:, 8:10], ALU.mult))
                    v.memset(job_gate[:, :, 0:1], 0.0)
                    for t in range(NT):
                        link(v.tensor_scalar(gate[:, t, :], hot[:, 1, t, :], weight[:, 1, t:t + 1], None, ALU.mult))
                        link(v.scalar_tensor_tensor(out=gate[:, t, :], in0=hot[:, 0, t, :], scalar=weight[:, 0, t:t + 1],
                                                    in1=gate[:, t, :], op0=ALU.mult, op1=ALU.add))
                    for n in range(2):
                        inc(v.tensor_copy(job_gate[:, :, 1 + n * NE:1 + (n + 1) * NE], gate[:, :, :]))
                    inc(v.tensor_tensor(chosen[:, :, :], hot[:, 0], hot[:, 1], ALU.add))
                    dve.wait_ge(act_step, a + 2)
                    rest(h_lo[:, :, :], nat[:, :, :], h_hi[:, :, :]).then_inc(h_split, 1)
                elif name == "places":
                    psum()
                    cum = MB[0][:, 0:2 * NE].rearrange("p (t e) -> p t e", t=NT)
                    s0, s1 = slot[:, :, 1:1 + NE], slot[:, :, 1 + NE:1 + 2 * NE]
                    link(v.memset(slot[:, :, :], -1.0))
                    link(v.tensor_tensor(s0, cum, chosen[:, :, :], ALU.mult))
                    link(v.tensor_scalar(s0, s0, -1.0, None, ALU.add))
                    link(v.tensor_scalar(s1, s0, -float(P), None, ALU.add))
                    link(v.tensor_reduce(stat[:, 12:13], MB[0][:, 2 * NE:3 * NE], axis=AX.X, op=ALU.max))
                    link(v.tensor_scalar(stat[:, 12:13], stat[:, 12:13], float(P), 1.0, ALU.is_gt, ALU.add))
                    link(v.tensor_copy(passes[:, :], stat[:, 12:13]))
                end(key)

            def layer_points(layer, u0):
                for u in range(N_LAYER):
                    r = (u - N_MIX) % 5
                    if u > N_MIX and r == 0 and u <= N_LAYER - 4:
                        i = (u - N_MIX) // 5 - 1
                        for c in range(2):
                            for t in range(NT):
                                if (c, t) == (1, 1):
                                    dve.wait_ge(unit_used, u0 + u)
                                else:
                                    dve.wait_ge(branch_done, 12 * layer + 3 * i + 2 * c + t + 1)
                                cs = slice(c * 512, (c + 1) * 512)
                                v.tensor_tensor((sig if i else nat)[:, t, cs], gate_bank(c, t)[:, :], sig[:, t, cs],
                                                ALU.mult).then_inc(branch_out, 1)
                    for name, arg in PLANS[layer].get(u, []):
                        stage(name, layer, arg)
                    if u == N_LAYER - 4:
                        turn(("turn", layer, 1))
                    if u == N_LAYER - 2:
                        add_out(layer, 0, u0 + u)
                    convert(u0 + u + AHEAD, 0)
                add_out(layer, 1, u0 + N_LAYER)

            def add_out(layer, c, u):
                dve.wait_ge(unit_used, u)
                for t in range(NT):
                    cs = slice(c * 512, (c + 1) * 512)
                    v.tensor_tensor(x[:, t, cs], x[:, t, cs], PB[2 * c + t][:, :], ALU.add).then_inc(out_added, 1)
                if c:
                    dve.wait_ge(out_added, 4 * (layer + 1))

            def take_act(u, turns, c, tiles):
                dve.wait_ge(unit_used, turns * RAW + (u + 1))
                dve.wait_ge(silu_made, c + 1)
                if not (isinstance(c, int) and c == 0):
                    dve.wait_ge(act_turned, c)
                for t in range(tiles):
                    last = v.tensor_tensor(act[:, t, :], silu_g[:, t, :], PB[2 + t][:, :], ALU.mult)
                last.then_inc(act_made, 1)

            def take_turned(c, tiles):
                dve.wait_ge(aT_hi_made, c + 1)
                for t in range(tiles):
                    ts = slice(t * P, (t + 1) * P)
                    last = rest(aT_lo[:, :, ts], PB[2 + t][:, :].rearrange("p (b n) -> p b n", b=FB), aT_hi[:, :, ts])
                last.then_inc(aT_lo_made, 1)

            def ffn_points(u0, turns, c0, tiles, first=None, third=None, fifth=None, late=None):
                ahead = lambda u, o: convert(u + AHEAD, o)
                for i in range(4):
                    if i == 0 and first:
                        first()
                    if i == 2 and third:
                        third()
                    ahead(u0 + i, turns)
                take_act(u0 + 3, turns, c0, tiles)
                if fifth:
                    fifth()
                take_turned(c0, tiles)
                with dve.Fori(1, NF) as j:
                    o = turns + (j - 1)
                    c = c0 + j
                    for i in range(4, 8):
                        ahead(u0 + i, o)
                    take_act(u0 + 7, o, c, tiles)
                    ahead(u0 + 8, o)
                    ahead(u0 + 9, o)
                    take_turned(c, tiles)
                if late:
                    late()
                ahead(u0 + 40, turns)
                ahead(u0 + 41, turns)

            v.memset(zeros_r[:, :].bitcast(F32), 0.0).then_inc(zeroed, 1)
            norm(0, 0)
            convert(0, 0)
            turn(("turn", 0, 0))
            convert(1, 0)
            dve.wait_ge(table_in, 32)
            layer_points(0, 0)
            norm(0, 1)
            turn(("turn", 0, 2))
            ffn_points(FFN0, 0, 0, NT)
            stage("split_router", 1, 0)
            dve.wait_ge(unit_used, FFN0 + N_FFN)
            for t in range(NT):
                for c in range(2):
                    cs = slice(c * 512, (c + 1) * 512)
                    v.tensor_tensor(x[:, t, cs], x[:, t, cs], MB[2 * t + c][:, :], ALU.add).then_inc(ffn_added, 1)
            dve.wait_ge(ffn_added, 4)
            norm(1, 0)
            turn(("turn", 1, 0))
            layer_points(1, LAYER1)
            norm(1, 1)
            turn(("turn", 1, 2))
            stage("router", 1, 0)
            stage("gates", 1, 0)
            stage("places", 1, 0)
            dve.wait_ge(dve_step, count[0])
            n_pass = dve.value_load(passes[0:1, 0:1], min_val=1, max_val=2)

            def one_hot(to, column):
                for t in range(NT):
                    last = v.tensor_scalar(to[:, t, :], T["iota"], slot[:, t, bass.ds(column, 1)], None, ALU.is_equal)
                return last

            def pick_next(job):
                one_hot(pick, job + 1).then_inc(picked, 1)

            def take_gathered(job):
                dve.wait_ge(gather_hi, job + 1)
                for b in range(2):
                    f = lambda t_: t_[:, 4 * b:4 * b + 4, :].rearrange("p k n -> p (k n)")
                    last = rest(f(e_lo), MB[2 + b][:, :], f(e_hi))
                last.then_inc(gather_lo, 1)

            def take_y(n):
                one_hot(pick_back, n).then_inc(back_picked, 1)
                dve.wait_ge(y_hi_made, n + 1)
                for c in range(2):
                    cs = slice(c * 512, (c + 1) * 512)
                    last = rest(y_lo[:, cs], MB[c][:, :], y_hi[:, cs])
                last.then_inc(y_lo_made, 1)

            def add_y(n):
                dve.wait_ge(scattered, n + 1)
                for t in range(NT):
                    for c in range(2):
                        cs = slice(c * 512, (c + 1) * 512)
                        bank = (MB[2 + c], PB[1 + 2 * c])[t]
                        last = v.scalar_tensor_tensor(out=x[:, t, cs], in0=bank[:, :],
                                                      scalar=job_gate[:, t, bass.ds(n, 1)], in1=x[:, t, cs],
                                                      op0=ALU.mult, op1=ALU.add)
                last.then_inc(moe_added, 1)

            pick_next(0)
            take_gathered(0)
            with dve.Fori(0, n_pass) as ps:
                with dve.Fori(0, NE) as e:
                    job = ps * NE + e

                    def third():
                        dve.wait_ge(gathered, job + 1)
                        pick_next(job + 1)

                    def fifth():
                        add_y(job)
                        dve.wait_ge(moe_added, job + 1)

                    ffn_points(MOE0, job * NF, NF + job * NF, 1, lambda: take_y(job), third, fifth,
                               lambda: take_gathered(job + 1))
            take_y(n_pass * NE)
            dve.wait_ge(moe_added, n_pass * NE)
            add_y(n_pass * NE)
            dve.wait_ge(moe_added, n_pass * NE + 1)
            norm(DEPTH, 0)


_INS = ["x", "w_in", "w_branch", "w_out", "norm_mix_g", "hgrn_lb_logits", "hgrn_norm_g", "fox_f_bias",
        "pool_w", "pool_scale", "ret_gn_g", "ret_gn_b", "norm_ffn_g", "ffn_w_gate", "ffn_w_up",
        "ffn_w_down", "moe_router", "moe_w_gate", "moe_w_up", "moe_w_down", "final_norm_g"]


def kernel(**inputs):
    import concourse.bacc as bacc
    from concourse.bass_utils import run_bass_kernel_spmd

    nc = bacc.Bacc("TRN2", target_bir_lowering=False, num_devices=1)
    consts, where = constants()
    arrays = {"in_consts": consts}
    A = {}
    for name in _INS:
        a = np.ascontiguousarray(inputs[name])
        arrays[f"in_{name}"] = a
        A[name] = nc.dram_tensor(f"in_{name}", a.shape, mybir.dt.from_np(a.dtype), kind="ExternalInput").ap()
    c = nc.dram_tensor("in_consts", consts.shape, F32, kind="ExternalInput").ap()
    o = nc.dram_tensor("out_0", (1, SEQ, DM), F32, kind="ExternalOutput").ap()
    build(nc, where, A, c, o)
    r = run_bass_kernel_spmd(nc, [arrays], core_ids=[0])
    return r.results[0]["out_0"]
```

```python
from contextlib import ExitStack

import numpy as np

import concourse.bass as bass
from concourse import mybir
from concourse.alu_op_type import AluOpType as ALU

F32 = mybir.dt.float32
F32R = mybir.dt.float32r
I32 = mybir.dt.int32
U32 = mybir.dt.uint32
ACT = mybir.ActivationFunctionType
AX = mybir.AxisListType

P = 128
SEQ, DM, DEPTH = 256, 1024, 2
NT = SEQ // P
KC = DM // P
BW, HD, NH, NB = 256, 64, 4, 4
CH = 64
NCH = SEQ // CH
FF, NE = 7 * DM // 2, 8
FCH = 512
NF = FF // FCH
FB = FCH // P
RMS_EPS, LN_EPS = 1e-6, 1e-5
NEG = -1e30
TINY = 2.0 ** -63

RAW, RING, AHEAD = 6, 3, 2
UNIT = 2048
WARM = [40, 26, 20, 5, 8, 4, 13, 12]

C_HQ, C_HI, C_FQ, C_FV, C_PU, C_RK, C_RG, C_GATE = 0, 512, 1024, 1536, 1796, 2308, 2820, 3076
MIX_CHUNKS = [(C_PU, 512, "T"), (C_RK, 512, "M"), (C_FV, 260, "N"), (C_RG, 256, "N"),
              (C_FQ, 512, "T"), (C_HQ, 512, "T"), (C_HI, 512, "N")]
Q_PU, Q_RK, Q_FV, Q_RG, Q_FQ, Q_HQ, Q_HI = range(7)
BRANCHES = [2, 3, 1, 0]
LEVELS = [128, 64, 32, 16, 8, 4, 2]

N_MIX = 2 * len(MIX_CHUNKS)
N_LAYER = N_MIX + NB * 5 + 4
N_FFN = NF * 6
FFN0 = N_LAYER
LAYER1 = N_LAYER + N_FFN
MOE0 = LAYER1 + N_LAYER


def constants():
    i = np.arange(P)
    s, t = i[:, None], i[None, :]
    parts = {}
    masks = []
    for b in LEVELS:
        h = b // 2
        masks.append(((s // b == t // b) & (s % b < h) & (t % b >= h)).astype(np.float32))
    parts["masks"] = np.concatenate(masks, 1)
    parts["ident"] = np.eye(P, dtype=np.float32)
    parts["tri"] = (s <= t).astype(np.float32)
    parts["ones"] = np.ones((P, P), np.float32)
    causal = np.where(t <= s, 0.0, NEG).astype(np.float32)
    parts["causal"] = np.concatenate([causal, np.zeros((P, P), np.float32), causal], 1)
    rot = np.zeros((P, P), np.float32)
    half = HD // 2
    for m in range(P):
        if m % HD < half:
            rot[m + half, m] = -1.0
        else:
            rot[m - half, m] = 1.0
    parts["rot"] = rot
    parts["iota"] = np.broadcast_to(np.arange(P + 1, dtype=np.float32), (P, P + 1))
    tt = np.arange(SEQ)[None, :]
    gamma = np.log1p(-np.exp2(-5.0 - np.arange(NH)))
    parts["decay"] = np.concatenate(
        [np.where(tt >= s, np.exp((tt - s) * gamma[h]), 0.0) for h in range(NH)], 1).astype(np.float32)
    inv_freq = (10000.0 ** (-np.arange(half, dtype=np.float32) / half)).astype(np.float32)
    ang = (np.arange(SEQ, dtype=np.float32)[None, :] * inv_freq[(i % half)][:, None]).astype(np.float32)
    parts["cos"] = np.cos(ang).astype(np.float32)
    parts["sin"] = np.sin(ang).astype(np.float32)
    win = np.array([[2, 8], [4, 16]])[(i >= 64).astype(int)]
    head = np.minimum(np.arange(16)[None, None, :] + 1, win[:, :, None])
    parts["inv_win"] = (1.0 / win).astype(np.float32)
    parts["win_head"] = (win[:, :, None] / head).reshape(P, 32).astype(np.float32)
    where, at = {}, 0
    for name, a in parts.items():
        where[name] = (at, a.shape[1])
        at += a.shape[1]
    return np.ascontiguousarray(np.concatenate(list(parts.values()), 1), dtype=np.float32), where


STAGE_SHAPES = {
    "bounds": (0, 1, 9),
    "norm": (0, 5, 7), "turn": (4, 4, 4),
    "pool_means": (0, 0, 13), "pool_out": (1, 1, 1),
    "rope": (1, 0, 6),
    "ret_pair": (1, 0, 4), "ret_last": (1, 1, 0),
    "ret_square": (0, 0, 6), "ret_sqrt": (0, 1, 0), "ret_norm": (0, 0, 5),
    "fox_log": (0, 0, 3), "fox_ln": (0, 2, 0), "fox_decay": (0, 0, 1),
    "fox_pair": (1, 4, 7), "fox_probs": (1, 2, 0), "fox_last": (1, 0, 2),
    "hgrn_log": (0, 0, 5), "hgrn_ln": (0, 1, 0), "hgrn_scan": (0, 0, 8),
    "hgrn_exponents": (0, 0, 14), "hgrn_exp": (0, 1, 0), "hgrn_span": (0, 0, 16),
    "hgrn_a": (1, 0, 3), "hgrn_b": (1, 0, 3), "hgrn_last": (1, 1, 0),
    "hgrn_square": (0, 0, 3), "hgrn_sqrt": (0, 1, 0), "hgrn_norm": (0, 0, 4),
    "branch_turn": (1, 1, 1),
    "split_router": (0, 0, 2), "split_h": (0, 1, 1), "router": (1, 0, 2), "choose": (0, 0, 8),
    "places": (1, 0, 0), "gates": (0, 1, 11), "slots": (0, 0, 1), "passes": (0, 0, 4),
}


def mixer_plan(layer):
    plan = {}
    put = lambda at, *st: plan.setdefault(at, []).append(st)
    put(2, "pool_means", 0)
    put(4, "pool_out", 0)
    put(5, "rope", 0)
    put(6, "fox_log", 0)
    put(7, "ret_pair", 0)
    put(7, "fox_ln", 0)
    put(8, "ret_pair", 1)
    put(8, "fox_decay", 0)
    put(9, "ret_last", 0)
    put(10, "ret_square", 0)
    put(11, "ret_sqrt", 0)
    put(11, "ret_norm", 0)
    put(12, "fox_pair", 0)
    put(13, "fox_pair", 1)
    put(14, "branch_turn", 3)
    if layer == 0:
        put(14, "bounds", 0)
    put(14, "hgrn_log", 0)
    put(15, "fox_probs", 0)
    put(15, "hgrn_ln", 0)
    put(16, "fox_probs", 1)
    put(16, "hgrn_scan", 0)
    put(17, "fox_last", 0)
    put(18, "hgrn_exponents", 0)
    put(19, "branch_turn", 1)
    put(19, "hgrn_exp", 0)
    put(20, "hgrn_span", 0)
    for h in range(2):
        put(21 + 2 * h, "hgrn_a", h)
        put(22 + 2 * h, "hgrn_b", h)
    put(24, "hgrn_exponents", 1)
    put(25, "hgrn_exp", 1)
    put(26, "hgrn_span", 1)
    for h in range(2):
        put(27 + 2 * h, "hgrn_a", 2 + h)
        put(28 + 2 * h, "hgrn_b", 2 + h)
    put(31, "hgrn_last", 0)
    put(31, "hgrn_square", 0)
    put(32, "hgrn_sqrt", 0)
    put(32, "hgrn_norm", 0)
    put(33, "branch_turn", 0)
    return plan


HGRN_PREPARES = ("bounds", "hgrn_log", "hgrn_ln", "hgrn_scan", "hgrn_exponents", "hgrn_exp")
APART = {"fox_probs": HGRN_PREPARES, "fox_last": HGRN_PREPARES, "branch_turn": HGRN_PREPARES,
         "router": ("split_h",), "ret_pair": ("fox_log", "fox_ln"), "ret_last": ("fox_decay",),
         "fox_pair": ("ret_square", "ret_sqrt", "ret_norm")}

PLANS = [mixer_plan(layer) for layer in range(DEPTH)]


def stage_order():
    order = []
    for layer in range(DEPTH):
        if layer == 1:
            order.append(("split_router", layer, 0))
        order += [("norm", layer, 0), ("turn", layer, 0)]
        for u in range(N_LAYER):
            order += [(name, layer, arg) for name, arg in PLANS[layer].get(u, [])]
            if u == N_LAYER - 4:
                order.append(("turn", layer, 1))
        order += [("norm", layer, 1), ("turn", layer, 2)]
        if layer == 1:
            order += [(name, layer, 0)
                      for name in ("split_h", "router", "choose", "places", "gates", "slots", "passes")]
    order.append(("norm", DEPTH, 0))
    return order


def build(nc, where, A, consts_ap, out_ap):
    ctx = ExitStack()
    with ctx:
        sem = lambda name: ctx.enter_context(nc.semaphore(name))
        keep = ExitStack()

        def sb(name, shape, dt=F32, stack=ctx):
            return stack.enter_context(nc.sbuf_tensor(name, shape, dt))

        raw = [sb(f"raw{i}", [P, UNIT]) for i in range(RAW)]
        w_hi = [sb(f"w_hi{i}", [P, UNIT], F32R) for i in range(RING)]
        w_lo = [sb(f"w_lo{i}", [P, UNIT], F32R) for i in range(RING)]
        table = sb("table", [P, sum(w for _, w in where.values())])
        T = {k: table[:, a:a + w] for k, (a, w) in where.items()}
        ident = T["ident"]
        x = sb("x_sb", [P, NT, DM])
        hT_hi = sb("hT_hi", [P, KC, SEQ], F32R)
        hT_lo = sb("hT_lo", [P, KC, SEQ], F32R)
        nat = sb("nat", [P, NT, DM])
        sig = sb("sig", [P, NT, DM])
        gain_row = sig[:, 0, :]
        zeros_r = sb("zeros_r", [P, P], F32R)
        stat = sb("stat", [P, 88])
        warm = sb("warm", [P, 1])
        lb_in = sb("lb_in", [P, 2, DEPTH])
        lower = sb("lower", [P, DEPTH, 2])
        upper = sb("upper", [P, DEPTH, 2])
        pool_w = sb("pool_w_sb", [P, DEPTH, 2, HD])
        pool_s = sb("pool_s_sb", [P, DEPTH, 2])
        fox_b = sb("fox_b_sb", [P, DEPTH, NH])
        rows = sb("rows", [P, 3, BW])
        lower1 = sb("lower1", [P, 8])
        router = sb("router_sb", [P, KC, NE])
        router_parts = sb("router_parts", [P, KC, 2, NE], F32R)

        mx = ExitStack()
        sbm = lambda name, shape, dt=F32: sb(name, shape, dt, mx)
        hq = sbm("hq", [P, 2, SEQ])
        hf = sbm("hf", [P, 2, SEQ])
        hk = sbm("hk", [P, 2, SEQ])
        fq = sbm("fq", [P, 2, SEQ])
        fk = sbm("fk", [P, 2, SEQ])
        rq = sbm("rq", [P, 2, SEQ])
        rk = sbm("rk", [P, 2, SEQ])
        upad = sbm("upad", [P, 2, 16 + SEQ])
        hv = sbm("hv", [P, NT, BW])
        hg = sbm("hg", [P, NT, BW])
        rv = sbm("rv", [P, NT, BW])
        rg = sbm("rg", [P, NT, BW])
        fv = sbm("fv", [P, NT, BW + NH])
        big = sbm("big", [P, 3072])
        pool_sum = [big[:, 272 * 2 * i:272 * 2 * (i + 1)].rearrange("p (c n) -> p c n", c=2) for i in range(2)]
        pool_d = big[:, 1088 + 512:1088 + 1024].rearrange("p (c n) -> p c n", c=2)
        fox_p = big[:, 0:4 * 384].rearrange("p (h n) -> p h n", h=NH)
        fox_pT = big[:, 4 * 384:8 * 384].rearrange("p (h n) -> p h n", h=NH)
        span = big[:, 0:2048].rearrange("p (l n) -> p l n", l=8)
        masked = big[:, 2048:3072].rearrange("p (l n) -> p l n", l=8)
        score = sbm("score", [P, 2, 384])
        square = score[:, :, :].rearrange("p a b -> p (a b)")[:, 0:512]
        o_nat = sbm("o_nat", [P, NT, BW])
        oT_hi = [sbm(f"oT_hi{i}", [P, 2, SEQ], F32R) for i in range(2)]
        oT_lo = [sbm(f"oT_lo{i}", [P, 2, SEQ], F32R) for i in range(2)]
        mx.close()

        silu_g = sb("silu_g", [P, NT, FCH], stack=keep)
        act = sb("act", [P, NT, FCH], stack=keep)
        aT_hi = sb("aT_hi", [P, FB, SEQ], F32R, keep)
        aT_lo = sb("aT_lo", [P, FB, SEQ], F32R, keep)
        h_hi = sb("h_hi", [P, NT, DM], F32R, keep)
        h_lo = sb("h_lo", [P, NT, DM], F32R, keep)
        pick = sb("pick", [P, NT, P], F32R, keep)
        pickT = sb("pickT", [P, SEQ], F32R, keep)
        e_hi = sb("e_hi", [P, KC, P], F32R, keep)
        e_lo = sb("e_lo", [P, KC, P], F32R, keep)
        y_hi = sb("y_hi", [P, DM], F32R, keep)
        y_lo = sb("y_lo", [P, DM], F32R, keep)
        logit = sb("logit", [P, NT, NE], stack=keep)
        top = sb("top", [P, NT, 8], stack=keep)
        top_at = sb("top_at", [P, NT, 8], U32, keep)
        top_f = sb("top_f", [P, NT, 8], stack=keep)
        hot = sb("hot", [P, 2, NT, NE], stack=keep)
        weight = sb("weight", [P, 2, NT], stack=keep)
        gate = sb("gate", [P, NT, NE], stack=keep)
        chosen = sb("chosen", [P, NT, NE], stack=keep)
        slot = sb("slot", [P, NT, 2 * NE + 2], stack=keep)
        job_gate = sb("job_gate", [P, NT, 2 * NE + 1], stack=keep)
        pick_back = sb("pick_back", [P, NT, P], stack=keep)
        passes = sb("passes", [P, 1], I32, keep)
        keep.close()

        PB = [ctx.enter_context(nc.psum_tensor(f"PB{i}", [P, 512], F32)) for i in range(4)]
        MB = [ctx.enter_context(nc.psum_tensor(f"MB{i}", [P, 512], F32)) for i in range(4)]

        raw_full = [sem(f"raw_full{i}") for i in range(RAW)]
        hi_made, lo_made, unit_used = sem("hi_made"), sem("lo_made"), sem("unit_used")
        chunk_out = sem("chunk_out")
        branch_out = sem("branch_out")
        merged = sem("merged")
        branch_done = sem("branch_done")
        out_added = sem("out_added")
        stage_psum, act_step, dve_step = sem("stage_psum"), sem("act_step"), sem("dve_step")
        x_in = [sem(f"x_in{t}") for t in range(NT)]
        first_gains_in, ident_in, table_in, params_in, rows_in, gains_in, router_in = (
            sem(n) for n in ("first_gains_in", "ident_in", "table_in", "params_in", "rows_in", "gains_in", "router_in"))
        zeroed = sem("zeroed")
        silu_made, act_made, act_turned, aT_hi_made, aT_lo_made = (
            sem(n) for n in ("silu_made", "act_made", "act_turned", "aT_hi_made", "aT_lo_made"))
        ffn_added = sem("ffn_added")
        picked, gathered, gather_hi, gather_lo = (
            sem(n) for n in ("picked", "gathered", "gather_hi", "gather_lo"))
        back_picked, back_turned, pickT_made = (sem(n) for n in ("back_picked", "back_turned", "pickT_made"))
        y_hi_made, y_lo_made, scattered, moe_added, last_added = (
            sem(n) for n in ("y_hi_made", "y_lo_made", "scattered", "moe_added", "last_added"))
        stored = sem("stored")

        ORDER = stage_order()
        base, pe_n, a_n, d_n = {}, 0, 0, 0
        for key in ORDER:
            base[key] = (pe_n, a_n, d_n)
            shape = STAGE_SHAPES[key[0]]
            pe_n, a_n, d_n = pe_n + shape[0], a_n + shape[1], d_n + shape[2]

        def slot_of(u):
            return u % RING

        def size_of(u):
            local = u if u < FFN0 else u - LAYER1
            return 4 * MIX_CHUNKS[local // 2][1] if 0 <= local < N_MIX else UNIT

        def col_view(buf, width):
            return buf[:, 0:4 * width].rearrange("p (k n) -> p k n", k=4)

        def row_view(buf):
            return buf[:, :].rearrange("p (k n) -> p k n", k=2)

        def gate_bank(c, t):
            return PB[2 * ((len(MIX_CHUNKS) + c) % 2) + t]

        def turn_bank(key, b):
            return PB[(b + 2) % 4 if key[2] == 1 else b]

        def out_bank(c, t):
            return PB[2 * (1 - c) + t]

        def broadcast(a, n):
            return a.unsqueeze(2).broadcast_to([P, a.shape[1], n])

        N_PARAMS = 9
        block = ctx.enter_context(nc.Block())

        @block.sync
        def _(sp):
            for t in range(NT):
                sp.dma_start(x[:, t, :], A["x"][0, t * P:(t + 1) * P, :]).then_inc(x_in[t], 16)
            sp.dma_start(gain_row, A["norm_mix_g"][0].partition_broadcast(P)).then_inc(first_gains_in, 16)
            a, w = where["ident"]
            sp.dma_start(ident, consts_ap[:, a:a + w]).then_inc(ident_in, 16)

            def load(u, turns, src, dst):
                if u >= RAW:
                    sp.wait_ge(hi_made, turns * RAW + (u - RAW + 1))
                    sp.wait_ge(lo_made, turns * RAW + (u - RAW + 1))
                sp.dma_start(dst(raw[u % RAW]), src).then_inc(raw_full[u % RAW], 16)

            def load_cols(u, turns, w, half, c0, width):
                src = w[half * 512:(half + 1) * 512, c0:c0 + width].rearrange("(k p) n -> p k n", p=P)
                load(u, turns, src, lambda b: col_view(b, width))

            def load_rows(u, turns, w):
                load(u, turns, w.rearrange("(k p) n -> p k n", p=P), row_view)

            def load_layer(layer, u0):
                u = u0
                for c0, width, _ in MIX_CHUNKS:
                    for half in range(2):
                        load_cols(u, 0, A["w_in"][layer], half, c0, width)
                        u += 1
                for b in BRANCHES:
                    for c in range(2):
                        for half in range(2):
                            load_cols(u, 0, A["w_in"][layer], half, C_GATE + b * DM + c * 512, 512)
                            u += 1
                    load_rows(u, 0, A["w_branch"][layer, b])
                    u += 1
                for c in range(2):
                    for half in range(2):
                        load_cols(u, 0, A["w_out"][layer], half, c * 512, 512)
                        u += 1

            def load_ffn(u0, turns, w_gate, w_up, w_down):
                for half in range(2):
                    load_cols(u0 + half, turns, w_gate, half, 0, FCH)
                for half in range(2):
                    load_cols(u0 + 2 + half, turns, w_up, half, 0, FCH)
                with sp.Fori(1, NF) as j:
                    o = turns + (j - 1)
                    for w, at in ((w_gate, 4), (w_up, 6)):
                        for half in range(2):
                            src = w[half * 512:(half + 1) * 512, bass.ds(j * FCH, FCH)].rearrange(
                                "(k p) n -> p k n", p=P)
                            load(u0 + at + half, o, src, lambda b: col_view(b, FCH))
                    for i in range(2):
                        load_rows(u0 + 8 + i, o, w_down[bass.ds((j - 1) * FCH + i * 256, 256), :])
                for i in range(2):
                    load_rows(u0 + 40 + i, turns, w_down[FF - FCH + i * 256:FF - FCH + (i + 1) * 256, :])

            load_layer(0, 0)
            load_ffn(FFN0, 0, A["ffn_w_gate"][0], A["ffn_w_up"][0], A["ffn_w_down"][0])
            load_layer(1, LAYER1)

            def load_experts(job0):
                with sp.Fori(0, NE) as e:
                    w = [A[n][0, bass.ds(e, 1)].rearrange("a k n -> (a k) n")
                         for n in ("moe_w_gate", "moe_w_up", "moe_w_down")]
                    load_ffn(MOE0, (e + job0) * NF, *w)

            load_experts(0)
            sp.wait_ge(dve_step, base[("passes", 1, 0)][2] + STAGE_SHAPES["passes"][2])
            n_pass = sp.value_load(passes[0:1, 0:1], min_val=1, max_val=2)
            with sp.If(n_pass > 1):
                load_experts(NE)
            for i in range(AHEAD + 1):
                u = MOE0 + i
                sp.wait_ge(hi_made, (n_pass * (NE * N_FFN)) + (u - RAW + 1))
                sp.sem_inc(raw_full[u % RAW], 16)
            key = ("norm", DEPTH, 0)
            for t in range(NT):
                sp.wait_ge(dve_step, base[key][2] + STAGE_SHAPES["norm"][2] - 2 * (NT - 1 - t))
                sp.dma_start(out_ap[0, t * P:(t + 1) * P, :], nat[:, t, :]).then_inc(stored, 16)
            sp.wait_ge(stored, 16 * NT)

        @block.gpsimd
        def _(pool):
            row = lambda a: a.partition_broadcast(P)
            a, w = where["ident"]
            pool.wait_ge(raw_full[0], 16)
            pool.dma_start(table[:, 0:a], consts_ap[:, 0:a]).then_inc(table_in, 16)
            pool.dma_start(table[:, a + w:], consts_ap[:, a + w:]).then_inc(table_in, 16)
            pool.dma_start(rows[:, 0, :], row(A["hgrn_norm_g"][0])).then_inc(rows_in, 16)
            pool.dma_start(rows[:, 1, :], row(A["ret_gn_g"][0])).then_inc(rows_in, 16)
            pool.dma_start(rows[:, 2, :], row(A["ret_gn_b"][0])).then_inc(rows_in, 16)
            for layer in range(DEPTH):
                pool.dma_start(lb_in[:, :, layer], A["hgrn_lb_logits"][layer].rearrange("(c p) -> p c", p=P),
                               allow_slow_non_contiguous=True).then_inc(params_in, 16)
                pool.dma_start(pool_s[:, layer, :], A["pool_scale"][layer].rearrange("(c p) -> p c", p=P),
                               allow_slow_non_contiguous=True).then_inc(params_in, 16)
            for b in range(2):
                for layer in range(DEPTH):
                    pool.dma_start(pool_w[b * HD:(b + 1) * HD, layer],
                                   A["pool_w"][layer].rearrange("(a b) i o -> b i a o", b=2)[b],
                                   ).then_inc(params_in, 16)
            pool.dma_start(fox_b[:, :, :], A["fox_f_bias"].partition_broadcast(P)).then_inc(params_in, 16)

            pool.dma_start(router[:, :, :], A["moe_router"][0].rearrange("(k p) e -> p k e", p=P)).then_inc(router_in, 16)

            def gains(src, n):
                pool.dma_start(gain_row, row(src)).then_inc(gains_in, 16)

            for layer in range(DEPTH):
                for i in range(1, NB):
                    for c in range(2):
                        for t in range(NT):
                            n = 4 * (i - 1) + 2 * c + t
                            pool.wait_ge(branch_out, 16 * layer + 4 + n + 1)
                            if i > 1:
                                pool.wait_ge(merged, 12 * layer + n - 3)
                            cs = slice(c * 512, (c + 1) * 512)
                            pool.tensor_tensor(nat[:, t, cs], nat[:, t, cs], sig[:, t, cs], ALU.add).then_inc(merged, 1)
                pool.wait_ge(merged, 12 * (layer + 1))
                gains(A["norm_ffn_g"][layer], 2 * layer + 1)
                pool.wait_ge(dve_step, base[("norm", layer, 1)][2] + STAGE_SHAPES["norm"][2])
                if layer == 0:
                    gains(A["norm_mix_g"][1], 2)
                    pool.dma_start(rows[:, 0, :], row(A["hgrn_norm_g"][1])).then_inc(rows_in, 16)
                    pool.dma_start(rows[:, 1, :], row(A["ret_gn_g"][1])).then_inc(rows_in, 16)
                    pool.dma_start(rows[:, 2, :], row(A["ret_gn_b"][1])).then_inc(rows_in, 16)
                else:
                    pool.memset(pickT[:, :].bitcast(F32), 0.0).then_inc(pickT_made, 1)
                    pool.memset(y_hi[:, :].bitcast(F32), 0.0)
                    pool.memset(y_lo[:, :].bitcast(F32), 0.0).then_inc(y_lo_made, 1)
                    gains(A["final_norm_g"], 4)

        @block.tensor
        def _(pe):
            def lo_ready(u, turns):
                pe.wait_ge(lo_made, turns * RAW + (u + 1))

            def product(out, lhs, rhs, first, last):
                pe.matmul(out, lhs[0], rhs[0], start=first, stop=False)
                pe.matmul(out, lhs[0], rhs[1], start=False, stop=False)
                return pe.matmul(out, lhs[1], rhs[0], start=False, stop=last)

            def begin(key):
                i = ORDER.index(key)
                while i and ORDER[i - 1][0] in APART.get(key[0], ()):
                    i -= 1
                p, a, d = base[ORDER[i]]
                if key == ("pool_out", 0, 0):
                    pe.wait_ge(table_in, 32)
                    pe.wait_ge(params_in, 16 * N_PARAMS)
                if a:
                    pe.wait_ge(act_step, a)
                if d:
                    pe.wait_ge(dve_step, d)

            def keep_warm(bank, n):
                for _ in range(n):
                    pe.matmul(bank[:, 0:P], zeros_r[:, :].bitcast(F32), zeros_r[:, :].bitcast(F32), start=True, stop=True)

            def turn(key):
                p, a, d = base[key]
                if key == ("turn", 0, 0):
                    keep_warm(MB[3], WARM[0])
                elif key[2] == 0:
                    keep_warm(PB[3], WARM[1])
                elif key[2] == 2:
                    keep_warm(MB[3], WARM[2])
                pe.wait_ge(act_step, a)
                if key == ("turn", 0, 0):
                    pe.wait_ge(ident_in, 16)
                for b in range(4):
                    if b % 2 == 0:
                        if key[2] == 1:
                            pe.wait_ge(merged, 12 * key[1] + (12 if b else 10))
                        else:
                            pe.wait_ge(dve_step, d if b else d - 2)
                    for k in range(2):
                        for t in range(NT):
                            last = pe.transpose(turn_bank(key, b)[:, k * SEQ + t * P:k * SEQ + (t + 1) * P],
                                                nat[:, t, (2 * b + k) * P:(2 * b + k + 1) * P], ident)
                    last.then_inc(stage_psum, 1)

            def half_turned(key, half):
                p, a, d = base[key]
                pe.wait_ge(act_step, a + 2 + 2 * half)
                pe.wait_ge(dve_step, d + 2 + 2 * half)

            def cols(u, half, q, kind, width):
                pair = PB[2 * (q % 2):2 * (q % 2) + 2]
                lo_ready(u, 0)
                hi, lo = (col_view(w[slot_of(u)], width) for w in (w_hi, w_lo))
                for k in range(4):
                    kk = 4 * half + k
                    first, end = kk == 0, kk == KC - 1
                    h = (hT_hi[:, kk, :], hT_lo[:, kk, :])
                    n_t = {"T": 4, "M": 2, "N": 0}[kind]
                    for m in range(n_t):
                        w = tuple(x[:, k, m * P:(m + 1) * P] for x in (hi, lo))
                        last = product(pair[m // 2][:, (m % 2) * SEQ:(m % 2 + 1) * SEQ], w, h,
                                       first and m % 2 == 0, end and m % 2 == 1)
                    if kind == "T":
                        continue
                    for t in range(NT):
                        ht = tuple(x[:, t * P:(t + 1) * P] for x in h)
                        if kind == "N":
                            last = product(pair[t][:, 0:width], ht, (hi[:, k, :], lo[:, k, :]), first, end)
                        else:
                            last = product(pair[1][:, t * BW:(t + 1) * BW], ht,
                                           (hi[:, k, BW:2 * BW], lo[:, k, BW:2 * BW]),
                                           first and t == 0, end and t == 1)
                last.then_inc(unit_used, 1)

            def heads(h):
                return h // 2, (h % 2) * HD

            def values(m, v, h):
                vs = [v[:, t, h * HD:(h + 1) * HD] for t in range(NT)]
                pe.matmul(MB[2][:, h * HD:(h + 1) * HD], m[:, 0:P], vs[0], start=True, stop=True)
                pe.matmul(MB[3][:, h * HD:(h + 1) * HD], m[:, P:2 * P], vs[0], start=True, stop=False)
                return pe.matmul(MB[3][:, h * HD:(h + 1) * HD], m[:, 2 * P:3 * P], vs[1], start=False, stop=True)

            def stage(name, layer, arg):
                key = (name, layer, arg)
                if not STAGE_SHAPES[name][0]:
                    return
                begin(key)
                if name == "pool_out":
                    for c in range(2):
                        for b in range(2):
                            s = slice(b * HD, (b + 1) * HD)
                            last = pe.matmul(MB[0][s, c * SEQ:(c + 1) * SEQ], pool_w[s, layer, c, :],
                                             pool_d[s, c, :], start=True, stop=True)
                elif name == "rope":
                    pe.wait_ge(chunk_out, 15 * layer + Q_RK + 1)
                    for i, t in enumerate((rq, rk)):
                        last = pe.matmul(MB[i][:, :], T["rot"], t[:, :, :].rearrange("p c n -> p (c n)"),
                                         start=True, stop=True)
                elif name == "ret_pair":
                    for h in (2 * arg, 2 * arg + 1):
                        if arg:
                            values(score[:, h % 2, :], rv, h - 2)
                    for h in (2 * arg, 2 * arg + 1):
                        c, b = heads(h)
                        s = slice(b, b + HD)
                        bank = MB[h % 2]
                        pe.matmul(bank[:, 0:SEQ], rk[s, c, 0:P], rq[s, c, :], start=True, stop=True)
                        last = pe.matmul(bank[:, SEQ:SEQ + P], rk[s, c, P:SEQ], rq[s, c, P:SEQ], start=True, stop=True)
                elif name == "ret_last":
                    for h in (NH - 2, NH - 1):
                        last = values(score[:, h % 2, :], rv, h)
                elif name == "hgrn_last":
                    last = values(score[:, (NH - 1) % 2, :], hv, NH - 1)
                elif name == "fox_pair":
                    pe.wait_ge(chunk_out, 15 * layer + Q_FQ + 1)
                    for h in (2 * arg, 2 * arg + 1):
                        c, b = heads(h)
                        s = slice(b, b + HD)
                        for t in range(NT):
                            n = P * (t + 1)
                            o = MB[h][:, t * P:t * P + n]
                            pe.matmul(o, fq[s, c, t * P:(t + 1) * P], fk[s, c, 0:n], start=True, stop=False)
                            for tt in range(t + 1):
                                nl = stat[:, 16 + tt * NH + h:17 + tt * NH + h].broadcast_to([P, P])
                                if tt == 0:
                                    rhs, oo = table[:, where["tri"][0]:where["tri"][0] + n], o
                                else:
                                    rhs, oo = T["tri"], o[:, P:2 * P]
                                last = pe.matmul(oo, nl, rhs, start=False, stop=tt == t)
                elif name == "fox_probs":
                    if arg:
                        for h in range(2):
                            values(fox_pT[:, h, :], fv, h)
                    for h in (2 * arg, 2 * arg + 1):
                        for i in range(3):
                            last = pe.transpose(MB[h % 2][:, i * P:(i + 1) * P], fox_p[:, h, i * P:(i + 1) * P], ident)
                elif name == "fox_last":
                    for h in (2, 3):
                        last = values(fox_pT[:, h, :], fv, h)
                elif name in ("hgrn_a", "hgrn_b"):
                    t = 0 if name == "hgrn_a" else 1
                    c, b = heads(arg)
                    s = slice(b, b + HD)
                    pe.wait_ge(chunk_out, 15 * layer + Q_HI + 1)
                    if t == 0 and arg:
                        values(score[:, (arg - 1) % 2, :], hv, arg - 1)
                    ts = slice(t * P, (t + 1) * P)
                    for i in range(8):
                        o = MB[i // 4][:, (i % 4) * P:(i % 4 + 1) * P]
                        if i < 7:
                            last = pe.matmul(o, span[s, 1 + i, ts], span[s, 1 + i, ts], start=True, stop=True)
                        else:
                            last = pe.matmul(o, hk[s, c, ts], hq[s, c, ts], start=True, stop=True)
                    if t == 1:
                        last = pe.matmul(MB[2][:, SEQ:SEQ + P], span[s, 0, 0:P], span[s, 0, P:SEQ], start=True, stop=True)
                elif name == "branch_turn":
                    for c in range(2):
                        for t in range(NT):
                            last = pe.transpose(MB[0][:, c * SEQ + t * P:c * SEQ + (t + 1) * P],
                                                o_nat[:, t, c * P:(c + 1) * P], ident)
                elif name == "router":
                    for t in range(NT):
                        for k in range(KC):
                            ts = slice(t * P, (t + 1) * P)
                            o = MB[0][:, t * 2 * NE:(t + 1) * 2 * NE]
                            parts = router_parts[:, k, :, :].rearrange("p h e -> p (h e)")
                            pe.matmul(o, hT_hi[:, k, ts], parts, start=k == 0, stop=False)
                            last = pe.matmul(o, hT_lo[:, k, ts], parts, start=False, stop=k == KC - 1)
                elif name == "places":
                    m = [chosen[:, t, :] for t in range(NT)]
                    pe.matmul(MB[0][:, 0:NE], T["tri"], m[0], start=True, stop=True)
                    pe.matmul(MB[0][:, NE:2 * NE], T["ones"], m[0], start=True, stop=False)
                    pe.matmul(MB[0][:, NE:2 * NE], T["tri"], m[1], start=False, stop=True)
                    pe.matmul(MB[0][:, 2 * NE:3 * NE], T["ones"], m[0], start=True, stop=False)
                    last = pe.matmul(MB[0][:, 2 * NE:3 * NE], T["ones"], m[1], start=False, stop=True)
                last.then_inc(stage_psum, 1)

            def layer_body(layer, u0):
                turn(("turn", layer, 0))
                q = 0
                for u in range(N_LAYER):
                    if u < 2:
                        half_turned(("turn", layer, 0), u)
                    for name, arg in PLANS[layer].get(u, []):
                        stage(name, layer, arg)
                    if u < N_MIX:
                        if u % 2 == 0:
                            if u >= 4:
                                pe.wait_ge(chunk_out, 15 * layer + q - 1)
                        cols(u0 + u, u % 2, q, MIX_CHUNKS[q][2], MIX_CHUNKS[q][1])
                        q += u % 2
                    elif u < N_LAYER - 4:
                        i, r = divmod(u - N_MIX, 5)
                        if r < 4:
                            if r % 2 == 0:
                                pe.wait_ge(chunk_out, 15 * layer + q - 1)
                                if i:
                                    pe.wait_ge(branch_out, 16 * layer + 4 * (i - 1) + (2 if r == 0 else 4))
                            cols(u0 + u, r % 2, q, "N", 512)
                            q += r % 2
                        else:
                            turned = ("pool_out", layer, 0) if BRANCHES[i] == 2 else ("branch_turn", layer, BRANCHES[i])
                            pe.wait_ge(act_step, base[turned][1] + 1)
                            pe.wait_ge(dve_step, base[turned][2] + 1)
                            lo_ready(u0 + u, 0)
                            hi, lo = (row_view(w[slot_of(u0 + u)]) for w in (w_hi, w_lo))
                            for c in range(2):
                                pe.wait_ge(chunk_out, 15 * layer + q - 1 + c)
                                for t in range(NT):
                                    for k in range(2):
                                        ts, cs = slice(t * P, (t + 1) * P), slice(c * 512, (c + 1) * 512)
                                        last = product(gate_bank(c, t)[:, :],
                                                       (oT_hi[i % 2][:, k, ts], oT_lo[i % 2][:, k, ts]),
                                                       (hi[:, k, cs], lo[:, k, cs]), k == 0, k == 1)
                                    if (c, t) != (1, 1):
                                        last.then_inc(branch_done, 1)
                            last.then_inc(unit_used, 1)
                    else:
                        c, half = divmod(u - (N_LAYER - 4), 2)
                        if (c, half) == (0, 0):
                            turn(("turn", layer, 1))
                        if c == 0:
                            half_turned(("turn", layer, 1), half)
                        lo_ready(u0 + u, 0)
                        hi, lo = (col_view(w[slot_of(u0 + u)], 512) for w in (w_hi, w_lo))
                        for k in range(4):
                            kk = 4 * half + k
                            for t in range(NT):
                                ts = slice(t * P, (t + 1) * P)
                                last = product(out_bank(c, t)[:, :], (hT_hi[:, kk, ts], hT_lo[:, kk, ts]),
                                               (hi[:, k, :], lo[:, k, :]), kk == 0, kk == KC - 1)
                        last.then_inc(unit_used, 1)
                turn(("turn", layer, 2))

            def wide(u, turns, bank0, src, tiles, key=None):
                for half in range(2):
                    if key:
                        half_turned(key, half)
                    lo_ready(u + half, turns)
                    hi, lo = (col_view(w[slot_of(u + half)], FCH) for w in (w_hi, w_lo))
                    for k in range(4):
                        kk = 4 * half + k
                        for t in range(tiles):
                            ts = slice(t * P, (t + 1) * P)
                            last = product(PB[bank0 + t][:, :], (src[0][:, kk, ts], src[1][:, kk, ts]),
                                           (hi[:, k, :], lo[:, k, :]), kk == 0, kk == KC - 1)
                    last.then_inc(unit_used, 1)

            def down(u, turns, c, tiles, final):
                for i in range(2):
                    pe.wait_ge(aT_lo_made, c * 2 + (i + 1))
                    lo_ready(u + i, turns)
                    hi, lo = (row_view(w[slot_of(u + i)]) for w in (w_hi, w_lo))
                    for k in range(2):
                        for t in range(tiles):
                            ts = slice(t * P, (t + 1) * P)
                            for cc in range(2):
                                cs = slice(cc * 512, (cc + 1) * 512)
                                last = product(MB[2 * t + cc][:, :], (aT_hi[:, 2 * i + k, ts], aT_lo[:, 2 * i + k, ts]),
                                               (hi[:, k, cs], lo[:, k, cs]), False,
                                               final and i == 1 and k == 1)
                    last.then_inc(unit_used, 1)
                    if i == 0 and not final:
                        turn_act(c + 1, tiles)

            def turn_act(c, tiles):
                pe.wait_ge(act_made, c + 1)
                for t in range(tiles):
                    for b in range(FB):
                        last = pe.transpose(PB[2 + t][:, b * P:(b + 1) * P], act[:, t, b * P:(b + 1) * P], ident)
                last.then_inc(act_turned, 1)

            def clear(tiles):
                for t in range(tiles):
                    for cc in range(2):
                        pe.matmul(MB[2 * t + cc][:, :], zeros_r[:, :],
                                  hT_hi[:, 0:2, :].rearrange("p a b -> p (a b)"), start=True, stop=False)

            def ffn_loop(u0, turns, c0, src, tiles):
                with pe.Fori(1, NF) as j:
                    o = turns + (j - 1)
                    c = c0 + j
                    pe.wait_ge(silu_made, c)
                    wide(u0 + 4, o, 0, src, tiles)
                    pe.wait_ge(aT_lo_made, c * 2)
                    wide(u0 + 6, o, 2, src, tiles)
                    down(u0 + 8, o, c - 1, tiles, False)

            def dense():
                half_turned(("turn", 0, 2), 0)
                clear(NT)
                wide(FFN0, 0, 0, (hT_hi, hT_lo), NT, ("turn", 0, 2))
                wide(FFN0 + 2, 0, 2, (hT_hi, hT_lo), NT)
                turn_act(0, NT)
                ffn_loop(FFN0, 0, 0, (hT_hi, hT_lo), NT)
                down(FFN0 + 40, 0, NF - 1, NT, True)

            def gather(job):
                pe.wait_ge(picked, job + 1)
                for k in range(KC):
                    o = MB[2 + k // 4][:, (k % 4) * P:(k % 4 + 1) * P]
                    ks = slice(k * P, (k + 1) * P)
                    for t in range(NT):
                        pe.matmul(o, h_hi[:, t, ks], pick[:, t, :], start=t == 0, stop=False)
                        last = pe.matmul(o, h_lo[:, t, ks], pick[:, t, :], start=False, stop=t == NT - 1)
                last.then_inc(gathered, 1)

            def turn_back(n):
                pe.wait_ge(back_picked, n)
                for t in range(NT):
                    last = pe.transpose(PB[3][:, t * P:(t + 1) * P], pick_back[:, t, :], ident)
                last.then_inc(back_turned, 1)

            def scatter(n):
                pe.wait_ge(pickT_made, n + 1)
                pe.wait_ge(y_lo_made, n + 1)
                for t in range(NT):
                    for c in range(2):
                        bank = (MB[2 + c], PB[1 + 2 * c])[t]
                        cs = slice(c * 512, (c + 1) * 512)
                        pe.matmul(bank[:, :], pickT[:, t * P:(t + 1) * P], y_hi[:, cs], start=True, stop=False)
                        last = pe.matmul(bank[:, :], pickT[:, t * P:(t + 1) * P], y_lo[:, cs], start=False, stop=True)
                last.then_inc(scattered, 1)

            pe.wait_ge(zeroed, 1)
            layer_body(0, 0)
            dense()
            layer_body(1, LAYER1)
            keep_warm(MB[3], WARM[3])
            half_turned(("turn", 1, 2), 1)
            stage("router", 1, 0)
            keep_warm(MB[3], WARM[4])
            stage("places", 1, 0)
            keep_warm(MB[3], WARM[5])
            gather(0)
            keep_warm(PB[2], WARM[6])
            pe.wait_ge(dve_step, base[("passes", 1, 0)][2] + STAGE_SHAPES["passes"][2])
            n_pass = pe.value_load(passes[0:1, 0:1], min_val=1, max_val=2)
            with pe.Fori(0, n_pass) as ps:
                with pe.Fori(0, NE) as e:
                    job = ps * NE + e
                    src = (e_hi, e_lo)
                    pe.wait_ge(gather_hi, job + 1)
                    pe.wait_ge(gather_lo, job + 1)
                    wide(MOE0, job * NF, 0, src, 1)
                    wide(MOE0 + 2, job * NF, 2, src, 1)
                    scatter(job)
                    clear(1)
                    turn_act(NF + job * NF, 1)
                    ffn_loop(MOE0, job * NF, NF + job * NF, src, 1)
                    pe.wait_ge(moe_added, job + 1)
                    gather(job + 1)
                    turn_back(job + 1)
                    down(MOE0 + 40, job * NF, NF + job * NF + (NF - 1), 1, True)
            keep_warm(PB[0], WARM[7])
            scatter(n_pass * NE)

        @block.scalar
        def _(act_e):
            def convert(u, turns):
                act_e.wait_ge(raw_full[u % RAW], turns * 16 + (u // RAW + 1) * 16)
                if u >= RING:
                    act_e.wait_ge(unit_used, turns * RAW + (u - RING + 1))
                n = size_of(u)
                act_e.activation(w_hi[slot_of(u)][:, 0:n], raw[u % RAW][:, 0:n], ACT.Copy).then_inc(hi_made, 1)

            def turn(key):
                p, a, d = base[key]
                for b in range(4):
                    act_e.wait_ge(stage_psum, p + b + 1)
                    act_e.activation(hT_hi[:, 2 * b:2 * b + 2, :].rearrange("p k n -> p (k n)"), turn_bank(key, b)[:, :],
                                     ACT.Copy).then_inc(act_step, 1)

            def take_chunk(q, u, layer):
                pair = PB[2 * (q % 2):2 * (q % 2) + 2]
                flat = lambda t: t[:, :, :].rearrange("p c n -> p (c n)")
                act_e.wait_ge(unit_used, u + 1)
                copy = lambda o, i, f=ACT.Copy, **kw: act_e.activation(o, i, f, **kw)
                if layer and q == 0:
                    act_e.wait_ge(ffn_added, 4)
                if q == Q_PU:
                    copy(upad[:, :, 16:16 + SEQ], pair[0][:, :].rearrange("p (c n) -> p c n", c=2))
                    last = copy(flat(rq), pair[1][:, :])
                elif q == Q_RK:
                    copy(flat(rk), pair[0][:, :], scale=HD ** -0.5)
                    last = copy(flat(rv), pair[1][:, :])
                elif q == Q_RG:
                    for t in range(NT):
                        last = copy(rg[:, t, :], pair[t][:, 0:BW], ACT.Silu)
                elif q == Q_FQ:
                    copy(flat(fq), pair[0][:, :], scale=HD ** -0.5)
                    last = copy(flat(fk), pair[1][:, :])
                elif q == Q_FV:
                    for t in range(NT):
                        last = copy(fv[:, t, :], pair[t][:, 0:BW + NH])
                elif q == Q_HQ:
                    copy(flat(hq), pair[0][:, :])
                    copy(flat(hf), pair[1][:, :], ACT.Sigmoid)
                    last = copy(flat(hk), pair[1][:, :], ACT.Sigmoid, scale=-1.0)
                elif q == Q_HI:
                    for t in range(NT):
                        copy(hv[:, t, :], pair[t][:, 0:BW])
                    for t in range(NT):
                        last = copy(hg[:, t, :], pair[t][:, BW:2 * BW], ACT.Silu)
                else:
                    i, c = divmod(q - 7, 2)
                    if c == 0 and i:
                        if i == 1:
                            act_e.wait_ge(branch_out, 16 * layer + 4)
                        else:
                            act_e.wait_ge(merged, 12 * layer + 4 * (i - 1))
                    for t in range(NT):
                        last = copy(sig[:, t, c * 512:(c + 1) * 512], pair[t][:, :], ACT.Sigmoid)
                last.then_inc(chunk_out, 1)

            def stage(name, layer, arg):
                p, a, d = base[(name, layer, arg)]
                if STAGE_SHAPES[name][1] == 0:
                    return
                dve = lambda n: act_e.wait_ge(dve_step, d + n)
                psum = lambda: act_e.wait_ge(stage_psum, p + 1)
                done = lambda ins: ins.then_inc(act_step, 1)
                if name == "bounds":
                    dve(2)
                    done(act_e.activation(lower1[:, 0:4], lower1[:, 4:8], ACT.Exp))
                elif name == "norm":
                    act_e.activation(warm[:, :], zeros_r[:, 0:1].bitcast(F32), ACT.Sqrt)
                    quarters = [(t, c) for c in range(2) for t in range(NT)]
                    if not arg:
                        quarters = [(t, c) for t in range(NT) for c in range(2)]
                    for n, (t, c) in enumerate(quarters):
                        bank = out_bank(c, t)
                        if arg:
                            act_e.wait_ge(out_added, 4 * layer + n + 1)
                        elif layer == DEPTH:
                            act_e.wait_ge(last_added, n + 1)
                            bank = (MB[2 + c], PB[1 + 2 * c])[t]
                        elif layer == 0:
                            act_e.wait_ge(x_in[t], 16)
                        else:
                            act_e.wait_ge(ffn_added, n + 1)
                            bank = MB[2 * t + c]
                        done(act_e.activation(bank[:, :], x[:, t, c * 512:(c + 1) * 512], ACT.Square,
                                              accum_out=stat[:, 2 * c + t:2 * c + t + 1]))
                    dve(2)
                    done(act_e.activation(stat[:, 6:8], stat[:, 6:8], ACT.Sqrt))
                elif name == "pool_out":
                    psum()
                    for c in range(2):
                        last = act_e.activation(oT_hi[0][:, c, :], MB[0][:, c * SEQ:(c + 1) * SEQ], ACT.Copy,
                                                scale=pool_s[:, layer, c:c + 1])
                    done(last)
                elif name in ("ret_last", "hgrn_last"):
                    psum()
                    if name == "hgrn_last":
                        act_e.wait_ge(stage_psum, base[("branch_turn", layer, 1)][0] + 1)
                    for t in range(NT):
                        last = act_e.activation(o_nat[:, t, :], MB[2 + t][:, 0:BW], ACT.Copy)
                    done(last)
                elif name in ("ret_sqrt", "hgrn_sqrt"):
                    squares = name.replace("sqrt", "square")
                    act_e.wait_ge(dve_step, base[(squares, layer, 0)][2] + STAGE_SHAPES[squares][2])
                    done(act_e.activation(stat[:, 32:40], stat[:, 32:40], ACT.Sqrt))
                elif name == "fox_ln":
                    act_e.wait_ge(dve_step, base[("fox_log", layer, 0)][2] + 3)
                    done(act_e.activation(stat[:, 48:56], stat[:, 48:56], ACT.Exp, scale=-1.0))
                    act_e.wait_ge(act_step, a + 1)
                    done(act_e.activation(stat[:, 48:56], stat[:, 48:56], ACT.Ln, bias=T["ones"][:, 0:1]))
                elif name == "fox_pair":
                    for i in range(2):
                        h = 2 * arg + i
                        dve(3 * (i + 1))
                        for t in range(NT):
                            cs = slice(0, P) if t == 0 else slice(P, 3 * P)
                            g = 2 * h + t
                            done(act_e.activation(fox_p[:, h, cs], fox_p[:, h, cs], ACT.Exp,
                                                  bias=stat[:, 64 + g:65 + g], accum_out=stat[:, 72 + g:73 + g]))
                elif name == "fox_probs":
                    psum()
                    for h in (2 * arg, 2 * arg + 1):
                        done(act_e.activation(fox_pT[:, h, :], MB[h % 2][:, 0:384], ACT.Copy))
                elif name == "hgrn_ln":
                    act_e.wait_ge(dve_step, base[("hgrn_log", layer, 0)][2] + 5)
                    done(act_e.activation(hf[:, :, :].rearrange("p c n -> p (c n)"),
                                          hf[:, :, :].rearrange("p c n -> p (c n)"), ACT.Ln))
                elif name == "hgrn_exp":
                    act_e.wait_ge(dve_step, base[("hgrn_exponents", layer, arg)][2] + 14)
                    done(act_e.activation(span[:, :, :].rearrange("p l n -> p (l n)"),
                                          span[:, :, :].rearrange("p l n -> p (l n)"), ACT.Exp))
                elif name == "branch_turn":
                    psum()
                    i = BRANCHES.index(arg)
                    if i >= 2:
                        act_e.wait_ge(unit_used, (0, LAYER1)[layer] + N_MIX + 5 * (i - 2) + 5)
                    done(act_e.activation(oT_hi[i % 2][:, :, :].rearrange("p c n -> p (c n)"), MB[0][:, :], ACT.Copy))
                elif name == "gates":
                    dve(1)
                    done(act_e.activation(stat[:, 8:10], stat[:, 8:10], ACT.Exp))
                elif name == "split_h":
                    for t in range(NT):
                        last = act_e.activation(h_hi[:, t, :], nat[:, t, :], ACT.Copy)
                    done(last)

            def layer_points(layer, u0):
                q = 0
                for u in range(N_LAYER):
                    if 0 < u <= N_MIX and u % 2 == 0:
                        take_chunk(q, u0 + u - 1, layer)
                        q += 1
                    elif u > N_MIX and (u - N_MIX) % 5 in (2, 4) and u < N_LAYER - 4:
                        take_chunk(q, u0 + u - 1, layer)
                        q += 1
                    for name, arg in PLANS[layer].get(u, []):
                        stage(name, layer, arg)
                    if u == N_LAYER - 4:
                        turn(("turn", layer, 1))
                    convert(u0 + u + AHEAD, 0)

            def take_silu(u, turns, c, tiles):
                act_e.wait_ge(unit_used, turns * RAW + (u + 1))
                if not (isinstance(c, int) and c == 0):
                    act_e.wait_ge(act_made, c)
                for t in range(tiles):
                    last = act_e.activation(silu_g[:, t, :], PB[t][:, :], ACT.Silu)
                last.then_inc(silu_made, 1)

            def take_turned(c, half, tiles):
                act_e.wait_ge(act_turned, c + 1)
                if half:
                    act_e.wait_ge(aT_lo_made, c * 2 + 1)
                bs = slice(0, FB) if half is None else slice(2 * half, 2 * half + 2)
                for t in range(tiles):
                    last = act_e.activation(aT_hi[:, bs, t * P:(t + 1) * P],
                                            PB[2 + t][:, :].rearrange("p (b n) -> p b n", b=FB)[:, bs, :], ACT.Copy)
                last.then_inc(aT_hi_made, 2 if half is None else 1)

            def ffn_points(u0, turns, c0, tiles, late=None, end=None):
                ahead = lambda u, o: convert(u + AHEAD, o)
                if tiles == NT:
                    ahead(u0, turns)
                ahead(u0 + 1, turns)
                take_silu(u0 + 1, turns, c0, tiles)
                ahead(u0 + 2, turns)
                ahead(u0 + 3, turns)
                take_turned(c0, None, tiles)
                with act_e.Fori(1, NF) as j:
                    o = turns + (j - 1)
                    c = c0 + j
                    ahead(u0 + 4, o)
                    ahead(u0 + 5, o)
                    take_silu(u0 + 5, o, c, tiles)
                    for i in range(6, 9):
                        ahead(u0 + i, o)
                    if tiles == NT:
                        take_turned(c, 0, tiles)
                    ahead(u0 + 9, o)
                    act_e.wait_ge(unit_used, o * RAW + (u0 + 10))
                    take_turned(c, 1 if tiles == NT else None, tiles)
                if late:
                    late()
                ahead(u0 + 40, turns)
                ahead(u0 + 41, turns)
                if end:
                    end()
                    ahead(u0 + 42, turns)

            def take_gathered(job):
                act_e.wait_ge(gathered, job + 1)
                for b in range(2):
                    last = act_e.activation(e_hi[:, 4 * b:4 * b + 4, :].rearrange("p k n -> p (k n)"),
                                            MB[2 + b][:, :], ACT.Copy)
                last.then_inc(gather_hi, 1)

            act_e.wait_ge(zeroed, 1)
            stage("norm", 0, 0)
            convert(0, 0)
            turn(("turn", 0, 0))
            convert(1, 0)
            layer_points(0, 0)
            stage("norm", 0, 1)
            turn(("turn", 0, 2))
            ffn_points(FFN0, 0, 0, NT)
            stage("norm", 1, 0)
            turn(("turn", 1, 0))
            layer_points(1, LAYER1)
            stage("norm", 1, 1)
            turn(("turn", 1, 2))
            stage("split_h", 1, 0)
            convert(MOE0 + AHEAD, 0)
            stage("gates", 1, 0)
            take_gathered(0)
            act_e.wait_ge(dve_step, base[("passes", 1, 0)][2] + STAGE_SHAPES["passes"][2])
            n_pass = act_e.value_load(passes[0:1, 0:1], min_val=1, max_val=2)

            def take_y(n):
                act_e.wait_ge(unit_used, n * N_FFN + MOE0)
                for c in range(2):
                    last = act_e.activation(y_hi[:, c * 512:(c + 1) * 512], MB[c][:, :], ACT.Copy)
                last.then_inc(y_hi_made, 1)

            def take_back(n):
                act_e.wait_ge(back_turned, n)
                act_e.activation(pickT[:, :], PB[3][:, 0:SEQ], ACT.Copy).then_inc(pickT_made, 1)

            with act_e.Fori(0, n_pass) as ps:
                with act_e.Fori(0, NE) as e:
                    job = ps * NE + e

                    def late():
                        take_gathered(job + 1)
                        take_back(job + 1)

                    ffn_points(MOE0, job * NF, NF + job * NF, 1, late, lambda: take_y(job + 1))
            stage("norm", DEPTH, 0)

        @block.vector
        def _(dve):
            v = nc.vector
            count = [0]

            def inc(instruction):
                count[0] += 1
                return instruction.then_inc(dve_step, 1)

            def link(instruction):
                inc(instruction)
                dve.wait_ge(dve_step, count[0])

            def end(key):
                want = base[key][2] + STAGE_SHAPES[key[0]][2]
                assert count[0] == want, (key, count[0] - base[key][2])

            def convert(u, turns):
                dve.wait_ge(hi_made, turns * RAW + (u + 1))
                if u >= RING:
                    dve.wait_ge(unit_used, turns * RAW + (u - RING + 1))
                n = size_of(u)
                v.tensor_tensor(w_lo[slot_of(u)][:, 0:n], raw[u % RAW][:, 0:n], w_hi[slot_of(u)][:, 0:n].bitcast(F32),
                                ALU.subtract).then_inc(lo_made, 1)

            def rest(lo, src, hi):
                return v.tensor_tensor(lo, src, hi.bitcast(F32), ALU.subtract)

            def turn(key):
                p, a, d = base[key]
                for b in range(4):
                    dve.wait_ge(act_step, a + b + 1)
                    f = lambda t: t[:, 2 * b:2 * b + 2, :].rearrange("p k n -> p (k n)")
                    inc(rest(f(hT_lo), turn_bank(key, b)[:, :], f(hT_hi)))
                end(key)

            def norm(layer, i):
                key = ("norm", layer, i)
                p, a, d = base[key]
                n = 2 * layer + i
                if n == 0:
                    for t in range(NT):
                        dve.wait_ge(x_in[t], 16)
                if d:
                    dve.wait_ge(dve_step, d)
                dve.wait_ge(act_step, a + 4)
                link(v.tensor_tensor(stat[:, 4:6], stat[:, 0:2], stat[:, 2:4], ALU.add))
                link(v.tensor_scalar(stat[:, 6:8], stat[:, 4:6], 1.0 / DM, RMS_EPS, ALU.mult, ALU.add))
                dve.wait_ge(act_step, a + 5)
                link(v.reciprocal(stat[:, 4:6], stat[:, 6:8]))
                if n:
                    dve.wait_ge(gains_in, 16 * n)
                else:
                    dve.wait_ge(first_gains_in, 16)
                quarters = [(t, c) for c in range(2) for t in range(NT)]
                if layer == DEPTH:
                    quarters = [(t, c) for t in range(NT) for c in range(2)]
                for t, c in quarters:
                    cs = slice(c * 512, (c + 1) * 512)
                    inc(v.scalar_tensor_tensor(out=nat[:, t, cs], in0=x[:, t, cs], scalar=stat[:, 4 + t:5 + t],
                                               in1=gain_row[:, cs], op0=ALU.mult, op1=ALU.mult))
                end(key)

            def head_squares(layer, center):
                last = base[("ret_last" if center else "hgrn_last", layer, 0)]
                dve.wait_ge(act_step, last[1] + 1)
                o3 = o_nat[:, :, :].rearrange("p t (h d) -> p (t h) d", d=HD)
                sq3 = square.rearrange("p (g d) -> p g d", d=HD)
                eps = RMS_EPS
                if center:
                    eps = LN_EPS
                    link(v.tensor_reduce(stat[:, 32:40], o3, axis=AX.X, op=ALU.add))
                    link(v.tensor_scalar(stat[:, 32:40], stat[:, 32:40], 1.0 / HD, None, ALU.mult))
                    link(v.tensor_tensor(o3, o3, broadcast(stat[:, 32:40], HD), ALU.subtract))
                link(v.tensor_tensor(sq3, o3, o3, ALU.mult))
                link(v.tensor_reduce(stat[:, 32:40], sq3, axis=AX.X, op=ALU.add))
                link(v.tensor_scalar(stat[:, 32:40], stat[:, 32:40], 1.0 / HD, eps, ALU.mult, ALU.add))

            def head_norm(layer, center):
                dve.wait_ge(act_step, base[("ret_sqrt" if center else "hgrn_sqrt", layer, 0)][1] + 1)
                o3 = o_nat[:, :, :].rearrange("p t (h d) -> p (t h) d", d=HD)
                link(v.reciprocal(stat[:, 32:40], stat[:, 32:40]))
                link(v.tensor_tensor(o3, o3, broadcast(stat[:, 32:40], HD), ALU.mult))
                row = lambda i: rows[:, i:i + 1, :].broadcast_to([P, NT, BW])
                dve.wait_ge(rows_in, 48 * (layer + 1))
                link(v.tensor_tensor(o_nat[:, :, :], o_nat[:, :, :], row(1 if center else 0), ALU.mult))
                if center:
                    link(v.tensor_tensor(o_nat[:, :, :], o_nat[:, :, :], row(2), ALU.add))
                g = rg if center else hg
                dve.wait_ge(chunk_out, 15 * layer + (Q_RG if center else Q_HI) + 1)
                link(v.tensor_tensor(o_nat[:, :, :], o_nat[:, :, :], g[:, :, :], ALU.mult))

            def stage(name, layer, arg):
                key = (name, layer, arg)
                p, a, d = base[key]
                assert count[0] == d, key
                if STAGE_SHAPES[name][2] == 0:
                    return
                if d:
                    dve.wait_ge(dve_step, d)
                chunk = lambda q: dve.wait_ge(chunk_out, 15 * layer + q + 1)
                psum = lambda: dve.wait_ge(stage_psum, p + 1)
                if name == "bounds":
                    dve.wait_ge(params_in, 16 * N_PARAMS)
                    l0, l1 = lb_in[:, :, 0], lb_in[:, :, 1]
                    link(v.tensor_tensor(lower1[:, 0:2], l0, l1, ALU.max))
                    top2 = lower1[:, 0:2]
                    both = lower1[:, 4:8].rearrange("p (l c) -> p l c", l=2)
                    v.tensor_tensor(both[:, 0, :], l0, top2, ALU.subtract)
                    inc(v.tensor_tensor(both[:, 1, :], l1, top2, ALU.subtract))
                    dve.wait_ge(act_step, a + 1)
                    link(v.tensor_tensor(lower1[:, 4:6], lower1[:, 0:2], lower1[:, 2:4], ALU.add))
                    link(v.reciprocal(lower1[:, 4:6], lower1[:, 4:6]))
                    link(v.tensor_tensor(lower1[:, 0:2], lower1[:, 0:2], lower1[:, 4:6], ALU.mult))
                    link(v.tensor_tensor(lower1[:, 2:4], lower1[:, 2:4], lower1[:, 4:6], ALU.mult))
                    link(v.tensor_tensor(lower1[:, 4:6], lower1[:, 0:2], lower1[:, 2:4], ALU.add))
                    v.tensor_tensor(lower[:, 0, :], lower1[:, 0:2], lower1[:, 0:2], ALU.subtract)
                    link(v.tensor_tensor(lower[:, 1, :], lower1[:, 4:6], lower1[:, 0:2], ALU.subtract))
                    link(v.tensor_scalar(upper[:, :, :], lower[:, :, :], -1.0, 1.0, ALU.mult, ALU.add))
                elif name == "pool_means":
                    chunk(Q_PU)
                    dve.wait_ge(table_in, 32)
                    s2, s4 = pool_sum
                    inc(v.memset(upad[:, :, 0:16], 0.0))
                    dve.wait_ge(dve_step, count[0])
                    link(v.tensor_tensor(s2[:, :, 1:272], upad[:, :, 1:272], upad[:, :, 0:271], ALU.add))
                    link(v.tensor_tensor(s4[:, :, 3:272], s2[:, :, 3:272], s2[:, :, 1:270], ALU.add))
                    link(v.tensor_tensor(s2[:, 1, 7:272], s4[:, 1, 7:272], s4[:, 1, 3:268], ALU.add))
                    link(v.tensor_tensor(s4[64:128, 1, 15:272], s2[64:128, 1, 15:272], s2[64:128, 1, 7:264], ALU.add))
                    heads_tab = T["win_head"].rearrange("p (c n) -> p c n", c=2)
                    for c in range(2):
                        for b, s in ((0, s2), (1, s4)):
                            ps = slice(64 * b, 64 * b + 64)
                            link(v.tensor_tensor(s[ps, c, 16:32], s[ps, c, 16:32], heads_tab[ps, c, :], ALU.mult))
                            inc(v.scalar_tensor_tensor(out=pool_d[ps, c, :], in0=s[ps, c, 16:272],
                                                       scalar=T["inv_win"][ps, c:c + 1], in1=upad[ps, c, 16:272],
                                                       op0=ALU.mult, op1=ALU.subtract))
                elif name == "pool_out":
                    dve.wait_ge(act_step, a + 1)
                    for c in range(2):
                        last = v.scalar_tensor_tensor(out=oT_lo[0][:, c, :], in0=MB[0][:, c * SEQ:(c + 1) * SEQ],
                                                      scalar=pool_s[:, layer, c:c + 1],
                                                      in1=oT_hi[0][:, c, :].bitcast(F32), op0=ALU.mult, op1=ALU.subtract)
                    inc(last)
                elif name == "rope":
                    psum()
                    tmp = o_nat[:, :, :]
                    tab = lambda n: T[n].unsqueeze(1).broadcast_to([P, 2, SEQ])
                    for i, t in enumerate((rq, rk)):
                        link(v.tensor_tensor(tmp, MB[i][:, :].rearrange("p (c n) -> p c n", c=2), tab("sin"), ALU.mult))
                        link(v.tensor_tensor(t[:, :, :], t[:, :, :], tab("cos"), ALU.mult))
                        link(v.tensor_tensor(t[:, :, :], t[:, :, :], tmp, ALU.add))
                elif name == "ret_pair":
                    psum()
                    for h in (2 * arg, 2 * arg + 1):
                        dec = T["decay"][:, h * SEQ:(h + 1) * SEQ]
                        bank = MB[h % 2]
                        inc(v.tensor_tensor(score[:, h % 2, 0:SEQ], bank[:, 0:SEQ], dec, ALU.mult))
                        inc(v.tensor_tensor(score[:, h % 2, SEQ:384], bank[:, SEQ:384], dec[:, 0:P], ALU.mult))
                elif name in ("ret_square", "hgrn_square"):
                    head_squares(layer, name == "ret_square")
                elif name in ("ret_norm", "hgrn_norm"):
                    head_norm(layer, name == "ret_norm")
                elif name == "fox_log":
                    chunk(Q_FV)
                    z3 = stat[:, 40:48].rearrange("p (t h) -> p t h", t=NT)
                    link(v.tensor_tensor(z3, fv[:, :, BW:BW + NH],
                                         fox_b[:, layer:layer + 1, :].broadcast_to([P, NT, NH]), ALU.add))
                    link(v.scalar_tensor_tensor(out=stat[:, 48:56], in0=stat[:, 40:48], scalar=-1.0,
                                                in1=stat[:, 40:48], op0=ALU.mult, op1=ALU.max))
                    inc(v.tensor_scalar(stat[:, 40:48], stat[:, 40:48], 0.0, None, ALU.min))
                elif name == "fox_decay":
                    dve.wait_ge(act_step, base[("fox_ln", layer, 0)][1] + 2)
                    inc(v.tensor_tensor(stat[:, 16:24], stat[:, 48:56], stat[:, 40:48], ALU.subtract))
                elif name == "fox_pair":
                    psum()
                    for h in (2 * arg, 2 * arg + 1):
                        link(v.tensor_tensor(fox_p[:, h, :], MB[h][:, 0:384], T["causal"], ALU.add))
                        g = 64 + 2 * h
                        inc(v.tensor_reduce(stat[:, g:g + 1], fox_p[:, h, 0:P], axis=AX.X, op=ALU.max, negate=True))
                        inc(v.tensor_reduce(stat[:, g + 1:g + 2], fox_p[:, h, P:384], axis=AX.X, op=ALU.max,
                                            negate=True))
                    dve.wait_ge(act_step, a + 4)
                    g = 72 + 4 * arg
                    inc(v.reciprocal(stat[:, g + 8:g + 12], stat[:, g:g + 4]))
                elif name == "fox_last":
                    psum()
                    one_over = stat[:, 80:88].rearrange("p (h t) -> p t h", t=NT)
                    for t in range(NT):
                        inc(v.tensor_tensor(o_nat[:, t, :].rearrange("p (h d) -> p h d", d=HD),
                                            MB[2 + t][:, 0:BW].rearrange("p (h d) -> p h d", d=HD),
                                            broadcast(one_over[:, t, :], HD), ALU.mult))
                elif name == "hgrn_log":
                    chunk(Q_HQ)
                    for c in range(2):
                        inc(v.tensor_scalar(hf[:, c, :], hf[:, c, :], upper[:, layer, c:c + 1],
                                            lower[:, layer, c:c + 1], ALU.mult, ALU.add))
                        inc(v.tensor_scalar(hk[:, c, :], hk[:, c, :], upper[:, layer, c:c + 1], None, ALU.mult))
                    dve.wait_ge(dve_step, count[0])
                    inc(v.tensor_scalar(hf[:, :, :], hf[:, :, :], TINY, None, ALU.max))
                elif name == "hgrn_scan":
                    dve.wait_ge(act_step, base[("hgrn_ln", layer, 0)][1] + 1)
                    for c in range(2):
                        for n in range(NCH):
                            s = slice(n * CH, (n + 1) * CH)
                            inc(v.tensor_tensor_scan(hf[:, c, s], T["ones"][:, 0:CH], hf[:, c, s], 0.0,
                                                     ALU.mult, ALU.add))
                elif name == "hgrn_exponents":
                    c = arg
                    if c == 0:
                        dve.wait_ge(stage_psum, base[("fox_last", layer, 0)][0] + 1)
                    else:
                        dve.wait_ge(stage_psum, base[("hgrn_b", layer, 1)][0] + 1)
                    lg = hf[:, c, :]
                    for i, b in enumerate(LEVELS[1:]):
                        h = b // 2
                        src = lg.rearrange("p (n b) -> p n b", b=b)
                        dst = span[:, 2 + i, :].rearrange("p (n b) -> p n b", b=b)
                        mid = src[:, :, h - 1:h].broadcast_to([P, SEQ // b, h])
                        inc(v.tensor_tensor(dst[:, :, h:b], src[:, :, h:b], mid, ALU.subtract))
                        inc(v.tensor_tensor(dst[:, :, 0:h], mid, src[:, :, 0:h], ALU.subtract))
                    src = lg.rearrange("p (g n b) -> p g n b", n=2, b=CH)
                    dst = span[:, 1, :].rearrange("p (g n b) -> p g n b", n=2, b=CH)
                    v.tensor_copy(dst[:, :, 1, :], src[:, :, 1, :])
                    link(v.tensor_tensor(dst[:, :, 0, :], src[:, :, 0, CH - 1:CH].broadcast_to([P, 2, CH]),
                                         src[:, :, 0, :], ALU.subtract))
                    last_of = lambda n: lg[:, n * CH + CH - 1:n * CH + CH]
                    sl = lambda n: slice(n * CH, (n + 1) * CH)
                    v.tensor_scalar(span[:, 0, sl(0)], span[:, 1, sl(0)], last_of(1), None, ALU.add)
                    v.tensor_tensor(span[:, 0, sl(1)], last_of(1).broadcast_to([P, CH]), lg[:, sl(1)], ALU.subtract)
                    v.tensor_copy(span[:, 0, sl(2)], lg[:, sl(2)])
                    inc(v.tensor_scalar(span[:, 0, sl(3)], lg[:, sl(3)], last_of(2), None, ALU.add))
                elif name == "hgrn_span":
                    c = arg
                    dve.wait_ge(act_step, base[("hgrn_exp", layer, c)][1] + 1)
                    for lev, b in enumerate([256] + LEVELS):
                        h = b // 2
                        e = span[:, lev, :].rearrange("p (n b) -> p n b", b=b)
                        q = hq[:, c, :].rearrange("p (n b) -> p n b", b=b)
                        k = hk[:, c, :].rearrange("p (n b) -> p n b", b=b)
                        inc(v.tensor_tensor(e[:, :, h:b], e[:, :, h:b], q[:, :, h:b], ALU.mult))
                        inc(v.tensor_tensor(e[:, :, 0:h], e[:, :, 0:h], k[:, :, 0:h], ALU.mult))
                elif name in ("hgrn_a", "hgrn_b"):
                    psum()
                    t = 0 if name == "hgrn_a" else 1
                    inc(v.tensor_tensor(masked[:, 0:4, :].rearrange("p l n -> p (l n)"), MB[0][:, :],
                                        table[:, where["masks"][0]:where["masks"][0] + 512], ALU.mult))
                    link(v.tensor_tensor(masked[:, 4:8, :].rearrange("p l n -> p (l n)"), MB[1][:, :],
                                         table[:, where["masks"][0] + 512:where["masks"][0] + 1024], ALU.mult))
                    if t == 1:
                        v.tensor_copy(score[:, arg % 2, P:2 * P], MB[2][:, SEQ:SEQ + P])
                    inc(v.tensor_reduce(score[:, arg % 2, t * SEQ:t * SEQ + P],
                                        masked[:, :, :].rearrange("p l n -> p n l"), axis=AX.X, op=ALU.add))
                    dve.wait_ge(dve_step, count[0])
                elif name == "branch_turn":
                    dve.wait_ge(act_step, a + 1)
                    i = BRANCHES.index(arg)
                    flat = lambda t: t[:, :, :].rearrange("p c n -> p (c n)")
                    inc(rest(flat(oT_lo[i % 2]), MB[0][:, :], flat(oT_hi[i % 2])))
                elif name == "split_router":
                    dve.wait_ge(router_in, 16)
                    link(v.tensor_copy(router_parts[:, :, 0, :], router[:, :, :]))
                    inc(rest(router_parts[:, :, 1, :], router[:, :, :], router_parts[:, :, 0, :]))
                elif name == "split_h":
                    dve.wait_ge(act_step, a + 1)
                    inc(rest(h_lo[:, :, :], nat[:, :, :], h_hi[:, :, :]))
                elif name == "router":
                    psum()
                    o = MB[0][:, 0:NT * 2 * NE].rearrange("p (t h e) -> p t h e", t=NT, h=2)
                    link(v.tensor_copy(logit[:, :, :], o[:, :, 0, :]))
                    link(v.tensor_tensor(logit[:, :, :], logit[:, :, :], o[:, :, 1, :], ALU.add))
                elif name == "choose":
                    for t in range(NT):
                        inc(v.max(top[:, t, :], logit[:, t, :]))
                    dve.wait_ge(dve_step, count[0])
                    for t in range(NT):
                        inc(v.max_index(top_at[:, t, :], top[:, t, :], logit[:, t, :]))
                    dve.wait_ge(dve_step, count[0])
                    link(v.tensor_copy(top_f[:, :, :], top_at[:, :, :]))
                    iota8 = T["iota"][:, 0:NE]
                    for r in range(2):
                        for t in range(NT):
                            v_ = v.tensor_scalar(hot[:, r, t, :], iota8, top_f[:, t, r:r + 1], None, ALU.is_equal)
                        inc(v_)
                    dve.wait_ge(dve_step, count[0])
                    inc(v.tensor_tensor(chosen[:, :, :], hot[:, 0], hot[:, 1], ALU.add))
                elif name == "gates":
                    link(v.tensor_tensor(stat[:, 8:10], top[:, :, 1], top[:, :, 0], ALU.subtract))
                    link(v.memset(slot[:, :, :], 0.0))
                    dve.wait_ge(act_step, a + 1)
                    link(v.tensor_scalar(stat[:, 10:12], stat[:, 8:10], 1.0, None, ALU.add))
                    link(v.reciprocal(weight[:, 0, :], stat[:, 10:12]))
                    link(v.tensor_tensor(weight[:, 1, :], weight[:, 0, :], stat[:, 8:10], ALU.mult))
                    v.memset(job_gate[:, :, 0:1], 0.0)
                    for t in range(NT):
                        link(v.tensor_scalar(gate[:, t, :], hot[:, 1, t, :], weight[:, 1, t:t + 1], None, ALU.mult))
                        link(v.scalar_tensor_tensor(out=gate[:, t, :], in0=hot[:, 0, t, :], scalar=weight[:, 0, t:t + 1],
                                                    in1=gate[:, t, :], op0=ALU.mult, op1=ALU.add))
                    for n in range(2):
                        inc(v.tensor_copy(job_gate[:, :, 1 + n * NE:1 + (n + 1) * NE], gate[:, :, :]))
                elif name == "slots":
                    dve.wait_ge(stage_psum, base[("places", layer, 0)][0] + 1)
                    cum = MB[0][:, 0:2 * NE].rearrange("p (t e) -> p t e", t=NT)
                    link(v.tensor_tensor(slot[:, :, 1:1 + NE], cum, chosen[:, :, :], ALU.mult))
                elif name == "passes":
                    s0, s1 = slot[:, :, 1:1 + NE], slot[:, :, 1 + NE:1 + 2 * NE]
                    link(v.tensor_scalar(s1, s0, -float(P), None, ALU.add))
                    link(v.tensor_reduce(stat[:, 12:13], MB[0][:, 2 * NE:3 * NE], axis=AX.X, op=ALU.max))
                    link(v.tensor_scalar(stat[:, 12:13], stat[:, 12:13], float(P), 1.0, ALU.is_gt, ALU.add))
                    link(v.tensor_copy(passes[:, :], stat[:, 12:13]))
                end(key)

            def layer_points(layer, u0):
                for u in range(N_LAYER):
                    r = (u - N_MIX) % 5
                    if u > N_MIX and r == 0 and u <= N_LAYER - 4:
                        i = (u - N_MIX) // 5 - 1
                        for c in range(2):
                            for t in range(NT):
                                if (c, t) == (1, 1):
                                    dve.wait_ge(unit_used, u0 + u)
                                else:
                                    dve.wait_ge(branch_done, 12 * layer + 3 * i + 2 * c + t + 1)
                                cs = slice(c * 512, (c + 1) * 512)
                                v.tensor_tensor((sig if i else nat)[:, t, cs], gate_bank(c, t)[:, :], sig[:, t, cs],
                                                ALU.mult).then_inc(branch_out, 1)
                    for name, arg in PLANS[layer].get(u, []):
                        stage(name, layer, arg)
                    if u == N_LAYER - 4:
                        turn(("turn", layer, 1))
                    if u == N_LAYER - 2:
                        add_out(layer, 0, u0 + u)
                    convert(u0 + u + AHEAD, 0)
                add_out(layer, 1, u0 + N_LAYER)

            def add_out(layer, c, u):
                dve.wait_ge(unit_used, u)
                for t in range(NT):
                    cs = slice(c * 512, (c + 1) * 512)
                    v.tensor_tensor(x[:, t, cs], x[:, t, cs], out_bank(c, t)[:, :], ALU.add).then_inc(out_added, 1)
                if c:
                    dve.wait_ge(out_added, 4 * (layer + 1))

            def take_act(u, turns, c, tiles):
                dve.wait_ge(unit_used, turns * RAW + (u + 1))
                dve.wait_ge(silu_made, c + 1)
                if not (isinstance(c, int) and c == 0):
                    dve.wait_ge(act_turned, c)
                for t in range(tiles):
                    last = v.tensor_tensor(act[:, t, :], silu_g[:, t, :], PB[2 + t][:, :], ALU.mult)
                last.then_inc(act_made, 1)

            def take_turned(c, half, tiles):
                dve.wait_ge(aT_hi_made, c * 2 + (2 if half is None else half + 1))
                bs = slice(0, FB) if half is None else slice(2 * half, 2 * half + 2)
                for t in range(tiles):
                    ts = slice(t * P, (t + 1) * P)
                    last = rest(aT_lo[:, bs, ts], PB[2 + t][:, :].rearrange("p (b n) -> p b n", b=FB)[:, bs, :],
                                aT_hi[:, bs, ts])
                last.then_inc(aT_lo_made, 2 if half is None else 1)

            def ffn_points(u0, turns, c0, tiles, third=None, fifth=None, late=None, end=None):
                ahead = lambda u, o: convert(u + AHEAD, o)
                for i in range(4):
                    if i == 2 and third:
                        third()
                    if i or tiles == NT:
                        ahead(u0 + i, turns)
                take_act(u0 + 3, turns, c0, tiles)
                if fifth:
                    fifth()
                take_turned(c0, None, tiles)
                with dve.Fori(1, NF) as j:
                    o = turns + (j - 1)
                    c = c0 + j
                    for i in range(4, 8):
                        ahead(u0 + i, o)
                    take_act(u0 + 7, o, c, tiles)
                    ahead(u0 + 8, o)
                    if tiles == NT:
                        take_turned(c, 0, tiles)
                    ahead(u0 + 9, o)
                    dve.wait_ge(unit_used, o * RAW + (u0 + 10))
                    take_turned(c, 1 if tiles == NT else None, tiles)
                if late:
                    late()
                ahead(u0 + 40, turns)
                ahead(u0 + 41, turns)
                if end:
                    end()
                    ahead(u0 + 42, turns)

            v.memset(zeros_r[:, :].bitcast(F32), 0.0).then_inc(zeroed, 1)
            norm(0, 0)
            convert(0, 0)
            turn(("turn", 0, 0))
            convert(1, 0)
            layer_points(0, 0)
            norm(0, 1)
            turn(("turn", 0, 2))
            ffn_points(FFN0, 0, 0, NT)
            stage("split_router", 1, 0)
            dve.wait_ge(unit_used, FFN0 + N_FFN)
            for t in range(NT):
                for c in range(2):
                    cs = slice(c * 512, (c + 1) * 512)
                    v.tensor_tensor(x[:, t, cs], x[:, t, cs], MB[2 * t + c][:, :], ALU.add).then_inc(ffn_added, 1)
            dve.wait_ge(ffn_added, 4)
            norm(1, 0)
            turn(("turn", 1, 0))
            layer_points(1, LAYER1)
            norm(1, 1)
            turn(("turn", 1, 2))
            def one_hot(to, column):
                for t in range(NT):
                    last = v.tensor_scalar(to[:, t, :], T["iota"][:, 1:], slot[:, t, bass.ds(column, 1)], None, ALU.is_equal)
                return last

            def pick_next(job):
                one_hot(pick, job + 1).then_inc(picked, 1)

            def take_gathered(job):
                dve.wait_ge(gather_hi, job + 1)
                for b in range(2):
                    f = lambda t_: t_[:, 4 * b:4 * b + 4, :].rearrange("p k n -> p (k n)")
                    last = rest(f(e_lo), MB[2 + b][:, :], f(e_hi))
                last.then_inc(gather_lo, 1)

            def take_y(n):
                dve.wait_ge(y_hi_made, n)
                for c in range(2):
                    cs = slice(c * 512, (c + 1) * 512)
                    last = rest(y_lo[:, cs], MB[c][:, :], y_hi[:, cs])
                last.then_inc(y_lo_made, 1)

            def add_y(n, final=False):
                dve.wait_ge(scattered, n + 1)
                for t in range(NT):
                    for c in range(2):
                        cs = slice(c * 512, (c + 1) * 512)
                        bank = (MB[2 + c], PB[1 + 2 * c])[t]
                        last = v.scalar_tensor_tensor(out=x[:, t, cs], in0=bank[:, :],
                                                      scalar=job_gate[:, t, bass.ds(n, 1)], in1=x[:, t, cs],
                                                      op0=ALU.mult, op1=ALU.add)
                        if final:
                            last.then_inc(last_added, 1)
                if not final:
                    last.then_inc(moe_added, 1)

            stage("split_h", 1, 0)
            stage("router", 1, 0)
            stage("choose", 1, 0)
            stage("gates", 1, 0)
            stage("slots", 1, 0)
            pick_next(0)
            stage("passes", 1, 0)
            convert(MOE0 + AHEAD, 0)
            take_gathered(0)
            dve.wait_ge(dve_step, count[0])
            n_pass = dve.value_load(passes[0:1, 0:1], min_val=1, max_val=2)
            with dve.Fori(0, n_pass) as ps:
                with dve.Fori(0, NE) as e:
                    job = ps * NE + e

                    def third():
                        dve.wait_ge(gathered, job + 1)
                        pick_next(job + 1)

                    def fifth():
                        add_y(job)
                        dve.wait_ge(moe_added, job + 1)

                    def late():
                        one_hot(pick_back, job + 1).then_inc(back_picked, 1)
                        take_gathered(job + 1)

                    ffn_points(MOE0, job * NF, NF + job * NF, 1, third, fifth, late, lambda: take_y(job + 1))
            dve.wait_ge(moe_added, n_pass * NE)
            add_y(n_pass * NE, True)
            dve.wait_ge(last_added, 4)
            norm(DEPTH, 0)


_INS = ["x", "w_in", "w_branch", "w_out", "norm_mix_g", "hgrn_lb_logits", "hgrn_norm_g", "fox_f_bias",
        "pool_w", "pool_scale", "ret_gn_g", "ret_gn_b", "norm_ffn_g", "ffn_w_gate", "ffn_w_up",
        "ffn_w_down", "moe_router", "moe_w_gate", "moe_w_up", "moe_w_down", "final_norm_g"]


def kernel(**inputs):
    import concourse.bacc as bacc
    from concourse.bass_utils import run_bass_kernel_spmd

    nc = bacc.Bacc("TRN2", target_bir_lowering=False, num_devices=1)
    consts, where = constants()
    arrays = {"in_consts": consts}
    A = {}
    for name in _INS:
        a = np.ascontiguousarray(inputs[name])
        arrays[f"in_{name}"] = a
        A[name] = nc.dram_tensor(f"in_{name}", a.shape, mybir.dt.from_np(a.dtype), kind="ExternalInput").ap()
    c = nc.dram_tensor("in_consts", consts.shape, F32, kind="ExternalInput").ap()
    o = nc.dram_tensor("out_0", (1, SEQ, DM), F32, kind="ExternalOutput").ap()
    build(nc, where, A, c, o)
    r = run_bass_kernel_spmd(nc, [arrays], core_ids=[0])
    return r.results[0]["out_0"]
```
